# Optimizing a Trainium2 kernel written in Bass

```python
import math
import jax
import jax.numpy as jnp
from jax import lax
import numpy as np

D_MODEL = 1024
BATCH = 1
SEQ = 256
DEPTH = 2

S5_W = D_MODEL // 2
S5_GROUP = 16
S5_GROUPS = S5_W // S5_GROUP
S5_STATE = 64
GLA_HEADS = 4
GLA_DV = (D_MODEL // 2) // GLA_HEADS
GLA_DK = GLA_DV // 2
GLA_QK = GLA_HEADS * GLA_DK
GLA_V = GLA_HEADS * GLA_DV
GLA_RANK = 16
GLA_GATE_NORM = 16.0
AB_IN = S5_W + 2 * GLA_QK + 2 * GLA_V + GLA_RANK
AB_OUT = S5_W + GLA_V
ML_HEADS = 8
ML_W = D_MODEL
ML_DH = ML_W // ML_HEADS
ML_IN = 4 * ML_W + 2 * ML_HEADS
CONV_W = 4
CHUNK = 64
N_EXPERTS = 16
N_EXPERT_GROUPS = 4
EXPERTS_PER_GROUP = N_EXPERTS // N_EXPERT_GROUPS
TOP_K = 2
D_EXPERT = 256

kernel_name = "hybrid_s5_gla_mlstm_moe_deepnorm_adaln"

F32 = jnp.float32

def layer_norm(x, g, b, eps=1e-5):
    xf = x.astype(F32)
    mu = jnp.mean(xf, -1, keepdims=True)
    var = jnp.mean(jnp.square(xf - mu), -1, keepdims=True)
    return ((xf - mu) * lax.rsqrt(var + eps) * g.astype(F32) + b.astype(F32)).astype(x.dtype)

def head_rmsnorm(h, g, eps=1e-6):
    h = h * lax.rsqrt(jnp.mean(h * h, -1, keepdims=True) + eps)
    return h.reshape(h.shape[0], h.shape[1], -1) * g.astype(F32)

def to_chunks(t):
    bsz, L, H = t.shape[:3]
    t = t.reshape(bsz, L // CHUNK, CHUNK, H, *t.shape[3:])
    return jnp.moveaxis(t, (1, 2), (0, 3))

def from_chunks(t):
    t = jnp.moveaxis(t, (0, 3), (1, 2))
    return t.reshape(t.shape[0], t.shape[1] * t.shape[2], t.shape[3], *t.shape[4:])

def causal_mask():
    return jnp.tril(jnp.ones((CHUNK, CHUNK), dtype=bool))

def s5_combine(e1, e2):
    a1r, a1i, b1r, b1i = e1
    a2r, a2i, b2r, b2i = e2
    return (a2r * a1r - a2i * a1i,
            a2r * a1i + a2i * a1r,
            a2r * b1r - a2i * b1i + b2r,
            a2r * b1i + a2i * b1r + b2i)

def s5_mixer(u, lam_re, lam_im, log_dt, b_re, b_im, c_re, c_im, d_skip, glu_w, glu_b):
    bsz, L, _ = u.shape
    uf = u.astype(F32)
    lre, lim = lam_re.astype(F32), lam_im.astype(F32)
    dt = jnp.exp(log_dt.astype(F32))[:, None]
    mag = jnp.exp(lre * dt)
    ang = lim * dt
    abar_re, abar_im = mag * jnp.cos(ang), mag * jnp.sin(ang)
    den = lre * lre + lim * lim
    nre, nim = abar_re - 1.0, abar_im
    coef_re = (nre * lre + nim * lim) / den
    coef_im = (nim * lre - nre * lim) / den
    bre, bim = b_re.astype(F32), b_im.astype(F32)
    bb_re = coef_re[..., None] * bre - coef_im[..., None] * bim
    bb_im = coef_re[..., None] * bim + coef_im[..., None] * bre
    ut = jnp.swapaxes(uf.reshape(bsz, L, S5_GROUPS, S5_GROUP), 0, 1)
    bu_re = jnp.einsum('lbgc,gpc->lbgp', ut, bb_re)
    bu_im = jnp.einsum('lbgc,gpc->lbgp', ut, bb_im)
    a_re = jnp.broadcast_to(abar_re[None, None], (L, 1, S5_GROUPS, S5_STATE))
    a_im = jnp.broadcast_to(abar_im[None, None], (L, 1, S5_GROUPS, S5_STATE))
    _, _, s_re, s_im = lax.associative_scan(s5_combine, (a_re, a_im, bu_re, bu_im), axis=0)
    y = (jnp.einsum('lbgp,gcp->lbgc', s_re, c_re.astype(F32))
         - jnp.einsum('lbgp,gcp->lbgc', s_im, c_im.astype(F32)))
    y = jnp.swapaxes(y, 0, 1).reshape(bsz, L, S5_W) + d_skip.astype(F32) * uf
    z = jax.nn.gelu(y)
    z = z * jax.nn.sigmoid(z @ glu_w.astype(F32) + glu_b.astype(F32))
    return z

def gla_chunked(q, k, v, log_a):
    bsz = q.shape[0]
    q = q * (GLA_DK ** -0.5)
    mask = causal_mask()[:, :, None]

    def step(S, inp):
        qc, kc, vc, gc = inp
        bc = jnp.cumsum(gc, axis=-2)
        inter = jnp.einsum('bhtk,bhkv->bhtv', qc * jnp.exp(bc), S)
        diff = bc[:, :, :, None, :] - bc[:, :, None, :, :]
        decay = jnp.exp(jnp.where(mask, diff, -jnp.inf))
        att = jnp.einsum('bhtsk,bhsk->bhts', qc[:, :, :, None, :] * decay, kc)
        intra = jnp.einsum('bhts,bhsv->bhtv', att, vc)
        blast = bc[:, :, -1:, :]
        S_new = (jnp.exp(blast[:, :, 0, :])[..., None] * S
                 + jnp.einsum('bhsk,bhsv->bhkv', kc * jnp.exp(blast - bc), vc))
        return S_new, inter + intra

    S0 = jnp.zeros((bsz, GLA_HEADS, GLA_DK, GLA_DV), F32)
    _, o = lax.scan(step, S0, (to_chunks(q), to_chunks(k), to_chunks(v), to_chunks(log_a)))
    return from_chunks(o)

def ab_mixer(h, w_in, lam_re, lam_im, log_dt, b_re, b_im, c_re, c_im, d_skip,
             glu_w, glu_b, gate_w, gate_b, norm_g, w_out):
    bsz, L, _ = h.shape
    p = h @ w_in
    o1 = S5_W
    o2 = o1 + GLA_QK
    o3 = o2 + GLA_QK
    o4 = o3 + GLA_V
    o5 = o4 + GLA_V
    u, q, k, v, r, a_lr = jnp.split(p, [o1, o2, o3, o4, o5], axis=-1)
    y_a = s5_mixer(u, lam_re, lam_im, log_dt, b_re, b_im, c_re, c_im, d_skip, glu_w, glu_b)
    log_a = jax.nn.log_sigmoid((a_lr @ gate_w + gate_b).astype(F32)) / GLA_GATE_NORM
    hd = lambda t, d: t.astype(F32).reshape(bsz, L, GLA_HEADS, d)
    o = gla_chunked(hd(q, GLA_DK), hd(k, GLA_DK), hd(v, GLA_DV), hd(log_a, GLA_DK))
    y_b = head_rmsnorm(o, norm_g) * jax.nn.silu(r.astype(F32))
    y = jnp.concatenate([y_a, y_b], axis=-1).astype(h.dtype)
    return y @ w_out

def mlstm_chunked(q, k, v, i_pre, f_pre):
    bsz = q.shape[0]
    k = k * (ML_DH ** -0.5)
    log_f = jax.nn.log_sigmoid(f_pre)
    mask = causal_mask()

    def step(carry, inp):
        Cs, ns, m = carry
        qc, kc, vc, ic, fc = inp
        b = jnp.cumsum(fc, axis=-1)
        dmat = jnp.where(mask, b[..., :, None] - b[..., None, :] + ic[..., None, :], -jnp.inf)
        inter_log = b + m[..., None]
        m_t = jnp.maximum(inter_log, jnp.max(dmat, axis=-1))
        w_intra = jnp.exp(dmat - m_t[..., None])
        w_inter = jnp.exp(inter_log - m_t)
        s = jnp.einsum('bhtd,bhsd->bhts', qc, kc) * w_intra
        num = (w_inter[..., None] * jnp.einsum('bhvd,bhtd->bhtv', Cs, qc)
               + jnp.einsum('bhts,bhsv->bhtv', s, vc))
        den = w_inter * jnp.einsum('bhd,bhtd->bht', ns, qc) + jnp.sum(s, axis=-1)
        hc = num / jnp.maximum(jnp.abs(den), jnp.exp(-m_t))[..., None]
        g_s = b[..., -1:] - b + ic
        m_new = jnp.maximum(b[..., -1] + m, jnp.max(g_s, axis=-1))
        w_s = jnp.exp(g_s - m_new[..., None])
        dec = jnp.exp(b[..., -1] + m - m_new)
        C_new = dec[..., None, None] * Cs + jnp.einsum('bhsv,bhsd->bhvd', vc * w_s[..., None], kc)
        n_new = dec[..., None] * ns + jnp.einsum('bhs,bhsd->bhd', w_s, kc)
        return (C_new, n_new, m_new), hc

    init = (jnp.zeros((bsz, ML_HEADS, ML_DH, ML_DH), F32),
            jnp.zeros((bsz, ML_HEADS, ML_DH), F32),
            jnp.zeros((bsz, ML_HEADS), F32))
    _, hs = lax.scan(step, init, (to_chunks(q), to_chunks(k), to_chunks(v),
                                  to_chunks(i_pre), to_chunks(log_f)))
    return from_chunks(hs)

def causal_depthwise_conv(t, w, b):
    ch = t.shape[-1]
    y = lax.conv_general_dilated(t, w[:, None, :], window_strides=(1,), padding=[(CONV_W - 1, 0)],
                                 dimension_numbers=('NWC', 'WIO', 'NWC'), feature_group_count=ch)
    return y + b

def mlstm_mixer(h, w_in, conv_w, conv_b, igate_b, fgate_b, norm_g, w_out):
    bsz, L, _ = h.shape
    p = h @ w_in
    qk, v, o, ig, fg = jnp.split(p, [2 * ML_W, 3 * ML_W, 4 * ML_W, 4 * ML_W + ML_HEADS], axis=-1)
    qk = jax.nn.silu(causal_depthwise_conv(qk, conv_w, conv_b))
    q, k = jnp.split(qk, 2, axis=-1)
    hd = lambda t: t.astype(F32).reshape(bsz, L, ML_HEADS, ML_DH)
    i_pre = (ig + igate_b).astype(F32)
    f_pre = (fg + fgate_b).astype(F32)
    hh = mlstm_chunked(hd(q), hd(k), hd(v), i_pre, f_pre)
    y = jax.nn.sigmoid(o.astype(F32)) * head_rmsnorm(hh, norm_g)
    return y.astype(h.dtype) @ w_out

def grouped_moe(h, router_w, router_bias, w_gate, w_up, w_down):
    bsz, L, d = h.shape
    t = h.reshape(-1, d)
    T = t.shape[0]
    aff = jax.nn.sigmoid(t.astype(F32) @ router_w.astype(F32))
    sel = (aff + router_bias.astype(F32)).reshape(T, N_EXPERT_GROUPS, EXPERTS_PER_GROUP)
    grp_score = jnp.sum(lax.top_k(sel, TOP_K)[0], axis=-1)
    g_idx = jnp.argmax(grp_score, axis=-1)
    in_grp = jnp.take_along_axis(sel, g_idx[:, None, None], axis=1)[:, 0]
    _, loc = lax.top_k(in_grp, TOP_K)
    e_idx = g_idx[:, None] * EXPERTS_PER_GROUP + loc
    a_sel = jnp.take_along_axis(aff, e_idx, axis=-1)
    wts = a_sel / jnp.sum(a_sel, axis=-1, keepdims=True)
    gates = jnp.sum(jax.nn.one_hot(e_idx, N_EXPERTS, dtype=F32) * wts[..., None], axis=1)
    out = jnp.zeros((T, d), F32)
    for e in range(N_EXPERTS):
        he = jax.nn.silu(t @ w_gate[e]) * (t @ w_up[e])
        out = out + gates[:, e:e + 1] * (he @ w_down[e]).astype(F32)
    return out.astype(h.dtype).reshape(bsz, L, d)

def setup_inputs(seed: int = 0) -> dict:
    key = jax.random.key(seed)
    ks = iter(jax.random.split(key, 48))
    nrm = lambda shape, std: std * jax.random.normal(next(ks), shape, F32)
    n_even = (DEPTH + 1) // 2
    n_odd = DEPTH // 2
    beta = (8.0 * DEPTH) ** -0.25
    dinv = D_MODEL ** -0.5
    lam_im = (jnp.pi * jnp.arange(S5_STATE, dtype=F32))[None, None] + nrm((n_even, S5_GROUPS, S5_STATE), 0.01)
    fgate_b = jnp.linspace(3.0, 6.0, ML_HEADS, dtype=F32)[None] + nrm((n_odd, ML_HEADS), 0.1)
    return {
        "x": nrm((BATCH, SEQ, D_MODEL), 1.0),
        "c": nrm((BATCH, D_MODEL), 1.0),
        "router_w": nrm((D_MODEL, N_EXPERTS), dinv),
        "router_bias": nrm((N_EXPERTS,), 0.01),
        "ada_w": nrm((DEPTH, D_MODEL, 6 * D_MODEL), 0.1 * dinv),
        "ada_b": nrm((DEPTH, 6 * D_MODEL), 0.02),
        "ln1_g": 1.0 + nrm((DEPTH, D_MODEL), 0.02),
        "ln1_b": nrm((DEPTH, D_MODEL), 0.02),
        "ln2_g": 1.0 + nrm((DEPTH, D_MODEL), 0.02),
        "ln2_b": nrm((DEPTH, D_MODEL), 0.02),
        "moe_w_gate": nrm((DEPTH, N_EXPERTS, D_MODEL, D_EXPERT), dinv),
        "moe_w_up": nrm((DEPTH, N_EXPERTS, D_MODEL, D_EXPERT), dinv),
        "moe_w_down": nrm((DEPTH, N_EXPERTS, D_EXPERT, D_MODEL), beta * D_EXPERT ** -0.5),
        "ab_w_in": nrm((n_even, D_MODEL, AB_IN), dinv),
        "s5_lam_re": -0.5 * jnp.exp(nrm((n_even, S5_GROUPS, S5_STATE), 0.02)),
        "s5_lam_im": lam_im,
        "s5_log_dt": jax.random.uniform(next(ks), (n_even, S5_GROUPS), F32,
                                        minval=math.log(0.001), maxval=math.log(0.1)),
        "s5_b_re": nrm((n_even, S5_GROUPS, S5_STATE, S5_GROUP), (2.0 * S5_GROUP) ** -0.5),
        "s5_b_im": nrm((n_even, S5_GROUPS, S5_STATE, S5_GROUP), (2.0 * S5_GROUP) ** -0.5),
        "s5_c_re": nrm((n_even, S5_GROUPS, S5_GROUP, S5_STATE), S5_STATE ** -0.5),
        "s5_c_im": nrm((n_even, S5_GROUPS, S5_GROUP, S5_STATE), S5_STATE ** -0.5),
        "s5_d": nrm((n_even, S5_W), 1.0),
        "s5_glu_w": nrm((n_even, S5_W, S5_W), S5_W ** -0.5),
        "s5_glu_b": nrm((n_even, S5_W), 0.02),
        "gla_gate_w": nrm((n_even, GLA_RANK, GLA_QK), GLA_RANK ** -0.5),
        "gla_gate_b": nrm((n_even, GLA_QK), 0.1),
        "gla_norm_g": 1.0 + nrm((n_even, GLA_V), 0.02),
        "ab_w_out": nrm((n_even, AB_OUT, D_MODEL), beta * AB_OUT ** -0.5),
        "ml_w_in": nrm((n_odd, D_MODEL, ML_IN), dinv),
        "ml_conv_w": nrm((n_odd, CONV_W, 2 * ML_W), CONV_W ** -0.5),
        "ml_conv_b": nrm((n_odd, 2 * ML_W), 0.02),
        "ml_igate_b": nrm((n_odd, ML_HEADS), 0.1),
        "ml_fgate_b": fgate_b,
        "ml_norm_g": 1.0 + nrm((n_odd, ML_W), 0.02),
        "ml_w_out": nrm((n_odd, ML_W, D_MODEL), beta * ML_W ** -0.5),
    }

def reference(x, c, router_w, router_bias, ada_w, ada_b, ln1_g, ln1_b, ln2_g, ln2_b,
              moe_w_gate, moe_w_up, moe_w_down, ab_w_in, s5_lam_re, s5_lam_im, s5_log_dt,
              s5_b_re, s5_b_im, s5_c_re, s5_c_im, s5_d, s5_glu_w, s5_glu_b,
              gla_gate_w, gla_gate_b, gla_norm_g, ab_w_out, ml_w_in, ml_conv_w, ml_conv_b,
              ml_igate_b, ml_fgate_b, ml_norm_g, ml_w_out):
    alpha = (2.0 * DEPTH) ** 0.25
    c_act = jax.nn.silu(c)
    for layer in range(DEPTH):
        j = layer // 2
        mod = c_act @ ada_w[layer] + ada_b[layer]
        sh1, sc1, g1, sh2, sc2, g2 = jnp.split(mod[:, None, :], 6, axis=-1)
        h = x * (1.0 + sc1) + sh1
        if layer % 2 == 0:
            y = ab_mixer(h, ab_w_in[j], s5_lam_re[j], s5_lam_im[j], s5_log_dt[j],
                         s5_b_re[j], s5_b_im[j], s5_c_re[j], s5_c_im[j], s5_d[j],
                         s5_glu_w[j], s5_glu_b[j], gla_gate_w[j], gla_gate_b[j],
                         gla_norm_g[j], ab_w_out[j])
        else:
            y = mlstm_mixer(h, ml_w_in[j], ml_conv_w[j], ml_conv_b[j], ml_igate_b[j],
                            ml_fgate_b[j], ml_norm_g[j], ml_w_out[j])
        x = layer_norm(alpha * x + (1.0 + g1) * y, ln1_g[layer], ln1_b[layer])
        h = x * (1.0 + sc2) + sh2
        y = grouped_moe(h, router_w, router_bias, moe_w_gate[layer], moe_w_up[layer], moe_w_down[layer])
        x = layer_norm(alpha * x + (1.0 + g2) * y, ln2_g[layer], ln2_b[layer])
    return x


_drawn_inputs = setup_inputs


def setup_inputs(seed=0):
    import zlib

    import numpy as np

    out = dict(_drawn_inputs(seed))
    spreads = {}
    factors = {'s5_lam_re': 64.0,
     's5_b_re': 3.019,
     's5_c_re': 2.923,
     's5_glu_b': 8.0,
     'gla_gate_b': 3.108,
     'gla_norm_g': 4.978,
     'ml_conv_b': 8.0,
     'ml_igate_b': 64.0,
     'ml_norm_g': 11.431,
     's5_b_im': 2.892}
    for name, (base, spread) in spreads.items():
        noise = np.random.default_rng([zlib.crc32(name.encode()), seed]).standard_normal(out[name].shape)
        drawn = base * np.exp(spread * noise) if base else spread * noise
        out[name] = jnp.asarray(drawn.astype(out[name].dtype))
    for name, factor in factors.items():
        out[name] = (out[name] * factor).astype(out[name].dtype)
    return out
```

```python
from contextlib import ExitStack

import numpy as np

import concourse.bass as bass
from concourse import mybir

F32 = mybir.dt.float32
BF16 = mybir.dt.bfloat16
I32 = mybir.dt.int32
ALU = mybir.AluOpType
ACT = mybir.ActivationFunctionType
AX = mybir.AxisListType

P = 128
TOK = 256
TT = TOK // P
D = 1024
DC = D // P
DEPTH = 2
ALPHA = (2.0 * DEPTH) ** 0.25
S5_W, S5_G, S5_N = 512, 16, 64
UC = S5_W // P
ST = (S5_W // S5_G) * S5_N // P
GH, GDV, GDK = 4, 128, 64
QC = GH * GDK // P
RANK = 16
GATE_NORM = 16.0
AB_LR = S5_W + 2 * GH * GDK + 2 * GH * GDV
MH = 8
CW = 4
NE, NG, EG, DE = 16, 4, 4, 256
SLOT = 2048
SC = SLOT // DC
RING = 6
MRING = 3
LEVELS = 8
BIG = 1.0e30
ROUND = 12582912.0
TWO_PI = (6.28125, 0.0019350051879882812, 3.019916050e-07)
PI_BELOW = 3.1415925

LN_G1, LN_B1, LN_G2, LN_B2, V_D, V_GLUB, V_GATEB, V_GNORM, V_CONVB, V_MNORM, V_END = (
    0, 16, 32, 48, 64, 68, 72, 74, 78, 94, 102)
SH1, SC1, G1, SH2, SC2, G2 = range(6)


def trunk(nc, x, c, router_w, router_bias, ada_w, ada_b, ln1_g, ln1_b, ln2_g, ln2_b,
          moe_w_gate, moe_w_up, moe_w_down, ab_w_in, s5_lam_re, s5_lam_im, s5_log_dt,
          s5_b_re, s5_b_im, s5_c_re, s5_c_im, s5_d, s5_glu_w, s5_glu_b,
          gla_gate_w, gla_gate_b, gla_norm_g, ab_w_out, ml_w_in, ml_conv_w, ml_conv_b,
          ml_igate_b, ml_fgate_b, ml_norm_g, ml_w_out, out):
    with ExitStack() as ctx:
        def sb(name, shape, dt=F32):
            return ctx.enter_context(nc.sbuf_tensor(name, shape, dt))

        def sem(name):
            return ctx.enter_context(nc.semaphore(name))

        bank = ctx.enter_context(nc.psum_tensor("bank", [P, 8, 512], F32))
        ring = sb("ring", [P, RING, SLOT])
        mring = sb("mring", [P, MRING, SLOT])
        hT = sb("hT", [P, DC, TOK])
        axT = sb("axT", [P, DC, TOK])
        rT = sb("rT", [P, DC, TOK])
        sqT = sb("sqT", [P, DC, TOK])
        std = sb("std", [P, 2, TOK])
        ident = sb("ident", [P, P])
        mean_w = sb("mean_w", [P, P])
        head_w = sb("head_w", [P, P])
        ones = sb("ones", [P, P])
        zero16 = sb("zero16", [P, 512], BF16)
        ident16 = sb("ident16", [P, P], BF16)
        future16 = sb("future16", [P, P], BF16)
        level_mask = sb("level_mask", [P, LEVELS, P], I32)
        rows = sb("rows", [P, 3, P])
        cols = sb("cols", [P, 3, P])
        mod = sb("mod", [P, DEPTH, 48])
        coef = sb("coef", [P, 4, 4, DC])
        c_col = sb("c_col", [P, 2, DC])
        router_sb = sb("router_sb", [P, DC, NE])
        rbias = sb("rbias", [P, NE])
        lr_w = sb("lr_w", [P, DC, RANK])
        gate_w = sb("gate_w", [RANK, GH * GDK])
        mg_w = sb("mg_w", [P, DC, 2 * MH])
        mg_b = sb("mg_b", [MH, 2])
        s5p = sb("s5p", [16, 16, P])
        s5dt = sb("s5dt", [16, 2, 2])
        s5c = sb("s5c", [P, 5, ST])
        arena = sb("arena", [P, 20224])

        def view(at, *shape):
            n = int(np.prod(shape))
            v = arena[:, at:at + n]
            if len(shape) == 1:
                return v
            names = "abcd"[:len(shape)]
            return v.rearrange(f"p ({' '.join(names)}) -> p {' '.join(names)}",
                               **dict(zip(names[1:], shape[1:])))

        cosT = view(0, ST, TOK)
        sinT = view(4096, ST, TOK)
        uT = view(8192, UC, TOK)
        rot = view(9216, 2, 2, 2, TOK)
        vin = view(11264, 2, 2, TOK)
        zst = view(12288, 2, TOK)
        sst = view(12800, 2, 2, TOK)
        bbT = view(13824, 2, UC, P)
        ctT = view(14848, 2, ST, 32)
        qT = view(15872, QC, TOK)
        kT = view(16384, QC, TOK)
        vS = view(16896, TT, GH * GDV)
        rS = view(17920, GH, TOK)
        cum = std[:, :, :]
        kd = view(18944, 2, QC, TOK)
        qd = rT[:, 0:4, :].rearrange("p (a c) t -> p a c t", a=2)
        rotp = rT[:, 4:8, :].rearrange("p (a c) t -> p a c t", a=2)
        attD = view(0, 2, 2, 2, P)
        attX = view(1024, 2, 2, P)
        dif = view(1536, 2, QC, TOK)
        dec = view(2560, 2, QC, TOK)
        oT = view(3584, GH, TOK)
        zT = view(8192, UC, TOK)
        yy = view(4608, UC, TOK)
        sgT = view(5632, UC, TOK)
        b_raw = view(15872, 2, ST, S5_G)
        bb = view(16384, 2, ST, 32)
        bt = view(17408, 4, ST, S5_G)
        c_raw = view(18432, 2, UC, P)
        en = view(19520, 3, 2, ST)
        tmpA = view(9216, ST, P)
        qkT = view(0, 2 * MH, TOK)
        vM = view(4096, TT, D)
        oG = view(6144, MH, TOK)
        hh = view(8192, MH, TOK)
        cv = view(10240, 2, 2, TOK)
        dM = view(11264, 2, 384)
        eM = view(12032, 2, 384)
        sM = view(12800, 2, 384)
        fl = view(13568, 2, TOK)
        dn = view(14080, 2, TOK)
        mrow = view(14592, 12, TOK)
        ccol = view(17664, TT, MH)
        gb = view(0, NE, TOK)
        rt = view(4096, 16, 64)
        gT = view(5120, TOK)
        sil = view(5376, 2, TOK)
        pr = view(5888, 2, TOK)
        he = view(6400, 2, 2, TOK)
        pairs = view(7424, 2, 2, NE, EG)
        yT = sqT

        landed = [sem(f"weights_landed{i}") for i in range(RING)]
        used = sem("weights_used")
        mlanded = [sem(f"mod_weights_landed{i}") for i in range(MRING)]
        mused = sem("mod_weights_used")
        names = """x_loaded c_loaded rows_loaded s5_loaded bc_loaded small_loaded stored
        pool_const x_turned xT_ready c_ready cols_turned cols_ready s5_turned s5c_ready
        bb_done bb_turned ct_turned bbT_ready ct_ready tables_ready
        dve_step act_step pool_step
        mod_ready h_ready ax_ready coef_ready
        lr_done lr_copied gate_done gate_x gate_abs gate_ln
        proj_out bu_done rot1_done vin_done scan_done rot2_done sst_done
        ys_done yy_done z_done glu_done glu_sig ya_done
        cum_done dif_done dec_done kq_done att_done att_out av_done av_out hsq_done hms_done
        hstd_done yb_done r_done mean_done cen_done sq_done var_done std_done norm_done
        logit_done aff_done gates_done gt_turned gt_copied gb_done gb_out
        unit_done sil_done prod_done he_done
        mgate_done mgate_x mgate_ln mrow_done mcol_turned mcol_done conv_a conv_done qk_done
        mb_done md_done me_done mqk_done ms_done mnum_done mfl_done mh_done
        final_x final_turned final_out""".split()
        S = {n: sem(n) for n in names}

        def bc(ap, *shape):
            return ap.broadcast_to(list(shape)) if hasattr(ap, "broadcast_to") else ap.to_broadcast(list(shape))

        def mcol(layer, part, ch=0):
            at = 8 * part + ch
            return mod[:, layer, at:at + 1]

        def vcol(row):
            return cols[:, 1, row:row + 1]

        def b2(i, half=None):
            return bank[:, i, :].rearrange("p (a t) -> p a t", a=2)

        block = ctx.enter_context(nc.Block())

        AB_U, AB_Q, AB_K, AB_V, AB_R, AB_GLU, AB_OUT = 0, 2, 3, 4, 6, 8, 9
        MOE0 = AB_OUT + 4
        ML_IN = MOE0 + 3 * NE
        ML_OUT = ML_IN + 16
        MOE1 = ML_OUT + 4
        MOE_AT = (MOE0, MOE1)

        @block.sync
        def _(sp):
            sp.dma_start(sqT[:, :, :].rearrange("p (a b) t -> p a (b t)", a=TT),
                         x[0].rearrange("(a p) d -> p a d", p=P)).then_inc(S["x_loaded"], 16)

            def load(n, src, split=DC):
                if n >= RING:
                    sp.wait_ge(used, n + 1 - RING)
                dst = ring[:, n % RING, :].rearrange("p (c n) -> p c n", c=split)
                sp.dma_start(dst, src).then_inc(landed[n % RING], 16)

            def load_cols(n, w, j):
                load(n, w[:, j * SC:(j + 1) * SC].rearrange("(c p) n -> p c n", p=P))

            def load_mod(n, layer, j):
                if n >= MRING:
                    sp.wait_ge(mused, n + 1 - MRING)
                sp.dma_start(mring[:, n % MRING, :].rearrange("p (c n) -> p c n", c=DC),
                             ada_w[layer, :, j * SC:(j + 1) * SC].rearrange("(p c) n -> p c n", c=DC)
                             ).then_inc(mlanded[n % MRING], 16)

            for j in range(8):
                load_mod(j, 0, j)
            for j in range(8):
                load_cols(AB_U + j, ab_w_in[0], j)
            load(AB_GLU, s5_glu_w[0].rearrange("(c p) n -> p c n", p=P), UC)
            for j in range(8, 24):
                load_mod(j, 0, j)
            for j in range(4):
                load_cols(AB_OUT + j, ab_w_out[0], j)

            def experts(layer):
                first = MOE_AT[layer]
                with sp.Fori(0, NE // 2) as it:
                    for e2 in range(2):
                        for k in range(3):
                            j = 3 * e2 + k
                            n = first + j
                            slot = n % RING
                            w = (moe_w_gate, moe_w_up, moe_w_down)[k][layer]
                            src = w[bass.ds(it * 2 + e2, 1), :, :]
                            if k < 2:
                                src = src.rearrange("e (c p) n -> p (e c) n", p=P)
                                dst = ring[:, slot, :].rearrange("p (c n) -> p c n", c=DC)
                            else:
                                src = src.rearrange("e (c p) n -> p (e c) n", p=P)
                                dst = ring[:, slot, :].rearrange("p (c n) -> p c n", c=2)
                            sp.wait_ge(used, it * RING + (n + 1 - RING))
                            sp.dma_start(dst, src).then_inc(landed[slot], 16)
                            if layer == 0 and j % 2 == 1:
                                m = j // 2
                                sp.wait_ge(mused, it * MRING + (24 + m + 1 - MRING))
                                sp.dma_start(
                                    mring[:, m, :].rearrange("p (c n) -> p c n", c=DC),
                                    ada_w[1, :, bass.ds(it * (MRING * SC) + m * SC, SC)].rearrange(
                                        "(p c) n -> p c n", c=DC)).then_inc(mlanded[m], 16)

            experts(0)
            for j in range(16):
                load_cols(ML_IN + j, ml_w_in[0], j)
            for j in range(4):
                load_cols(ML_OUT + j, ml_w_out[0], j)
            experts(1)
            for b in range(4):
                sp.wait_ge(S["final_out"], b + 1)
                sp.dma_start(out[0].rearrange("(a p) d -> p a d", p=P)[:, b // 2, (b % 2) * 512:(b % 2) * 512 + 512],
                             sqT[:, :, :].rearrange("p (b c) t -> p b (c t)", b=4)[:, b, :]).then_inc(S["stored"], 16)
            sp.wait_ge(S["stored"], 64)

        @block.gpsimd
        def _(pool):
            step = [0]

            def link(ins):
                step[0] += 1
                ins.then_inc(S["pool_step"], 1)
                pool.wait_ge(S["pool_step"], step[0])

            link(pool.memset(ident[:, :], 0.0))
            link(pool.affine_select(out=ident[:, :], in_=ident[:, :], compare_op=ALU.not_equal, fill=1.0,
                                    base=0, pattern=[[-1, P]], channel_multiplier=1))
            pool.memset(mean_w[:, :], 1.0 / D)
            pool.memset(head_w[:, :], 1.0 / P)
            pool.memset(ones[:, :], 1.0)
            pool.memset(zero16[:, :], 0.0)
            pool.memset(future16[:, :], 0.0)
            link(pool.tensor_copy(ident16[:, :], ident[:, :]))
            link(pool.memset(future16[:, :], 0.0))
            pool.affine_select(out=future16[:, :], in_=future16[:, :], compare_op=ALU.is_ge, fill=BIG,
                               base=0, pattern=[[1, P]], channel_multiplier=-1)
            link(pool.memset(level_mask[:, :, :], 0))
            for lv in range(LEVELS - 1):
                h = 1 << lv
                m = level_mask[:, lv, :].rearrange("p (n two h) -> p n two h", two=2, h=h)[:, :, 1, :]
                link(pool.memset(m, 1))
                link(pool.affine_select(out=m, in_=m, compare_op=ALU.is_ge, fill=0.0, base=0,
                                        pattern=[[-2 * h, P // (2 * h)], [0, h]], channel_multiplier=1))
                link(pool.affine_select(out=m, in_=m, compare_op=ALU.is_ge, fill=0.0, base=h - 1,
                                        pattern=[[2 * h, P // (2 * h)], [0, h]], channel_multiplier=-1))
            pool.tensor_copy(level_mask[:, LEVELS - 1, :], ident[:, :]).then_inc(S["pool_const"], 1)

            pool.wait_ge(S["xT_ready"], 4)
            for ch in range(DC):
                pool.tensor_scalar(axT[:, ch, :], rT[:, ch, :], ALPHA, None, ALU.mult).then_inc(S["ax_ready"], 1)

            def rotate_in(j):
                pool.wait_ge(S["rot1_done"], 2 * j + 2)
                if j >= 2:
                    pool.wait_ge(S["scan_done"], 2 * (j - 1))
                q = j % 2
                pool.tensor_tensor(vin[:, q, 0, :], rot[:, q, 0, 0, :], rot[:, q, 1, 1, :], ALU.add)
                pool.tensor_tensor(vin[:, q, 1, :], rot[:, q, 0, 1, :], rot[:, q, 1, 0, :],
                                   ALU.subtract).then_inc(S["vin_done"], 1)

            def rotate_out(j):
                pool.wait_ge(S["rot2_done"], 2 * j + 2)
                if j >= 2:
                    pool.wait_ge(S["ys_done"], j - 1)
                q = j % 2
                pool.tensor_tensor(sst[:, q, 0, :], rotp[:, 0, 0, :], rotp[:, 1, 1, :], ALU.subtract)
                pool.tensor_tensor(sst[:, q, 1, :], rotp[:, 0, 1, :], rotp[:, 1, 0, :],
                                   ALU.add).then_inc(S["sst_done"], 1)

            for j in range(ST + 1):
                if j < ST:
                    rotate_in(j)
                if j >= 1:
                    rotate_out(j - 1)

            pool.memset(kd[:, :, :, :], 0.0)
            link(pool.memset(qd[:, :, :, :], 0.0))
            pool.wait_ge(S["proj_out"], 4)
            for lv in range(LEVELS):
                h = 1 << lv
                q = lv % 2
                pool.wait_ge(S["dec_done"], 2 * lv + 2)
                if lv >= 2:
                    pool.wait_ge(S["att_done"], 2 * (lv - 1))
                k5 = kT.rearrange("p c (n two h) -> p (c n) two h", two=2, h=h)[:, :, 0, :]
                q5 = qT.rearrange("p c (n two h) -> p (c n) two h", two=2, h=h)[:, :, 1, :]
                d5 = dec[:, q, :, :].rearrange("p c (n two h) -> p (c n) two h", two=2, h=h)
                ko = kd[:, q, :, :].rearrange("p c (n two h) -> p (c n) two h", two=2, h=h)[:, :, 0, :]
                qo = qd[:, q, :, :].rearrange("p c (n two h) -> p (c n) two h", two=2, h=h)[:, :, 1, :]
                pool.tensor_tensor(ko, k5, d5[:, :, 0, :], ALU.mult)
                pool.tensor_tensor(qo, q5, d5[:, :, 1, :], ALU.mult).then_inc(S["kq_done"], 1)

            for i in range(3):
                for b in range(4):
                    pool.wait_ge(S["norm_done"], 4 * i + b + 1)
                    if b == 0:
                        pool.wait_ge(S["coef_ready"], i + 1)
                    for ch in (2 * b, 2 * b + 1):
                        pool.tensor_scalar(axT[:, ch, :], rT[:, ch, :], coef[:, i, 2, ch:ch + 1],
                                           coef[:, i, 3, ch:ch + 1], ALU.mult, ALU.add).then_inc(S["ax_ready"], 1)

        @block.scalar
        def _(act):
            step = [0]

            def link(ins):
                step[0] += 1
                ins.then_inc(S["act_step"], 1)
                act.wait_ge(S["act_step"], step[0])

            act.dma_start(c_col[:, 0, :], c.rearrange("b (p c) -> (b p) c", c=DC)).then_inc(S["c_loaded"], 16)
            lam = lambda a: a[0].rearrange("(j g) p -> j g p", g=2)
            for i, a in enumerate((s5_lam_re, s5_lam_im)):
                act.dma_start(s5p[:, i, :].rearrange("j (g p) -> j g p", g=2), lam(a)).then_inc(S["s5_loaded"], 16)
            act.dma_start(s5dt[:, 0, :], s5_log_dt[0].rearrange("(j g) -> j g", g=2)).then_inc(S["s5_loaded"], 16)
            for l in range(DEPTH):
                act.dma_start(rows[48 * l:48 * l + 48, 0, :], ada_b[l].rearrange("(r n) -> r n", n=P)
                              ).then_inc(S["rows_loaded"], 16)
            for a, at in ((ln1_g, LN_G1), (ln1_b, LN_B1), (ln2_g, LN_G2), (ln2_b, LN_B2)):
                act.dma_start(rows[at:at + 16, 1, :], a.rearrange("l (r n) -> (l r) n", n=P)
                              ).then_inc(S["rows_loaded"], 16)
            for a, at, n in ((s5_d, V_D, 4), (s5_glu_b, V_GLUB, 4), (gla_gate_b, V_GATEB, 2),
                             (gla_norm_g, V_GNORM, 4), (ml_conv_b, V_CONVB, 16), (ml_norm_g, V_MNORM, 8)):
                act.dma_start(rows[at:at + n, 1, :], a[0].rearrange("(r n) -> r n", n=P)
                              ).then_inc(S["rows_loaded"], 16)
            act.dma_start(rows[0:64, 2, :], ml_conv_w[0].rearrange("j (r n) -> (j r) n", n=P)
                          ).then_inc(S["rows_loaded"], 16)
            for i, a in enumerate((s5_b_re, s5_b_im)):
                act.dma_start(b_raw[:, i, :, :], a[0].rearrange("(j g) p c -> (g p) j c", g=2)
                              ).then_inc(S["bc_loaded"], 16)
            for i, a in enumerate((s5_c_re, s5_c_im)):
                for h in range(2):
                    act.dma_start(c_raw[:, i, :, h * 64:h * 64 + 64],
                                  a[0].rearrange("(k g) c p -> (g c) k p", g=8)).then_inc(S["bc_loaded"], 16)
            act.dma_start(lr_w[:, :, :], ab_w_in[0, :, AB_LR:AB_LR + RANK].rearrange("(c p) n -> p c n", p=P)
                          ).then_inc(S["small_loaded"], 16)
            act.dma_start(gate_w[:, :], gla_gate_w[0]).then_inc(S["small_loaded"], 16)
            act.dma_start(router_sb[:, :, :], router_w.rearrange("(c p) n -> p c n", p=P)
                          ).then_inc(S["small_loaded"], 16)
            act.dma_start(rbias[:, :], router_bias.rearrange("(a n) -> a n", a=1).to_broadcast([P, NE])
                          ).then_inc(S["small_loaded"], 16)
            act.dma_start(mg_w[:, :, :], ml_w_in[0, :, 4 * D:4 * D + 2 * MH].rearrange("(c p) n -> p c n", p=P)
                          ).then_inc(S["small_loaded"], 16)
            act.dma_start(mg_b[:, 0:1], ml_igate_b[0].rearrange("(h a) -> h a", a=1)).then_inc(S["small_loaded"], 16)
            act.dma_start(mg_b[:, 1:2], ml_fgate_b[0].rearrange("(h a) -> h a", a=1)).then_inc(S["small_loaded"], 16)

            act.wait_ge(S["c_loaded"], 16)
            act.activation(c_col[:, 1, :], c_col[:, 0, :], ACT.Silu).then_inc(S["c_ready"], 1)
            for b in range(4):
                act.wait_ge(S["x_turned"], b + 1)
                act.activation(rT[:, 2 * b:2 * b + 2, :], b2(b), ACT.Copy).then_inc(S["xT_ready"], 1)
            act.wait_ge(S["s5_loaded"], 48)
            act.activation(s5dt[:, 1, :], s5dt[:, 0, :], ACT.Exp).then_inc(S["tables_ready"], 1)
            act.wait_ge(S["tables_ready"], 2)
            act.activation(s5p[:, 4, :], s5p[:, 2, :], ACT.Exp).then_inc(S["tables_ready"], 1)
            act.wait_ge(S["tables_ready"], 4)
            act.activation(s5p[:, 6, :], s5p[:, 3, :], ACT.Sin).then_inc(S["tables_ready"], 1)
            act.activation(s5p[:, 9, :], s5p[:, 3, :], ACT.Sin, scale=0.5).then_inc(S["tables_ready"], 1)

            act.wait_ge(S["mod_ready"], 1)
            for ch in range(DC):
                act.activation(hT[:, ch, :], rT[:, ch, :], ACT.Identity, scale=mcol(0, SC1, ch),
                               bias=mcol(0, SH1, ch)).then_inc(S["h_ready"], 1)

            act.wait_ge(S["lr_done"], 1)
            act.activation(s5p[0:RANK, 0:2, :], bank[0:RANK, 6, 0:TOK].rearrange("p (a t) -> p a t", a=2),
                           ACT.Copy).then_inc(S["lr_copied"], 1)
            act.wait_ge(S["gate_done"], 1)
            for ch in range(QC):
                act.activation(cum[:, ch, :], b2(5)[:, ch, :], ACT.Identity, bias=vcol(V_GATEB + ch)
                               ).then_inc(S["gate_x"], 1)
            act.wait_ge(S["gate_x"], 2)
            link(act.activation(kd[:, 0, :, :], cum[:, :, :], ACT.Abs))
            link(act.activation(kd[:, 1, :, :], kd[:, 0, :, :], ACT.Exp, scale=-1.0))
            act.activation(kd[:, 0, :, :], kd[:, 1, :, :], ACT.Ln, bias=1.0).then_inc(S["gate_ln"], 1)

            def leave(j):
                act.wait_ge(used, j + 1)
                bk = b2(j % 4)
                if j < 2:
                    ins = act.activation(uT[:, 2 * j:2 * j + 2, :], bk, ACT.Copy)
                elif j == 2:
                    ins = act.activation(qT[:, :, :], bk, ACT.Copy, scale=GDK ** -0.5)
                elif j == 3:
                    ins = act.activation(kT[:, :, :], bk, ACT.Copy)
                elif j < 6:
                    ins = act.activation(vS[:, :, (j - 4) * SC:(j - 3) * SC], bk, ACT.Copy)
                else:
                    ins = act.activation(rS[:, 2 * (j - 6):2 * (j - 6) + 2, :], bk, ACT.Silu)
                ins.then_inc(S["proj_out"], 1)

            for j in range(8):
                leave(j)

            for k in range(UC):
                act.wait_ge(S["yy_done"], k + 1)
                act.activation(zT[:, k, :], yy[:, k, :], ACT.Gelu_apprx_tanh).then_inc(S["z_done"], 1)
            for k in range(UC):
                if k == 0:
                    act.wait_ge(S["glu_done"], 1)
                elif k == 2:
                    act.wait_ge(used, AB_GLU + 1)
                act.activation(sgT[:, k, :], b2(4 + k // 2)[:, k % 2, :], ACT.Sigmoid,
                               bias=vcol(V_GLUB + k)).then_inc(S["glu_sig"], 1)

            for lv in range(LEVELS):
                h = 1 << lv
                q = lv % 2
                act.wait_ge(S["dif_done"], lv + 1)
                if lv >= 2:
                    act.wait_ge(S["kq_done"], lv - 1)
                a5 = dif[:, q, :, :].rearrange("p c (n two h) -> p (c n) two h", two=2, h=h)
                d5 = dec[:, q, :, :].rearrange("p c (n two h) -> p (c n) two h", two=2, h=h)
                for half, sign in ((0, -1.0), (1, 1.0)):
                    act.activation(d5[:, :, half, :], a5[:, :, half, :], ACT.Exp,
                                   scale=sign / GATE_NORM).then_inc(S["dec_done"], 1)
            for b in range(2):
                act.wait_ge(S["av_done"], b + 1)
                act.activation(oT[:, 2 * b:2 * b + 2, :], b2(b), ACT.Copy).then_inc(S["av_out"], 1)
            for b in range(2):
                act.wait_ge(S["av_out"], b + 1)
                act.activation(yy[:, 2 * b:2 * b + 2, :], oT[:, 2 * b:2 * b + 2, :], ACT.Square
                               ).then_inc(S["hsq_done"], 1)
            for b in range(2):
                act.wait_ge(S["hms_done"], b + 1)
                act.activation(sgT[:, 2 * b:2 * b + 2, :], b2(4 + b), ACT.Sqrt, bias=EPS_H
                               ).then_inc(S["hstd_done"], 1)

            def norm(i):
                for b in range(4):
                    act.wait_ge(S["cen_done"], 4 * i + b + 1)
                    act.activation(sqT[:, 2 * b:2 * b + 2, :], rT[:, 2 * b:2 * b + 2, :], ACT.Square
                                   ).then_inc(S["sq_done"], 1)
                act.wait_ge(S["var_done"], i + 1)
                act.activation(std[:, 0, :], bank[:, 5, 0:TOK], ACT.Sqrt, bias=EPS_LN).then_inc(S["std_done"], 1)
                for b in range(4):
                    act.wait_ge(S["norm_done"], 4 * i + b + 1)
                    for ch in (2 * b, 2 * b + 1):
                        act.activation(hT[:, ch, :], rT[:, ch, :], ACT.Identity, scale=coef[:, i, 0, ch:ch + 1],
                                       bias=coef[:, i, 1, ch:ch + 1]).then_inc(S["h_ready"], 1)

            def moe(layer):
                act.wait_ge(S["logit_done"], layer + 1)
                act.activation(rt[:, 0, 0:TT * NE], bank[:, 6, 0:TT * NE], ACT.Sigmoid).then_inc(S["aff_done"], 1)
                act.wait_ge(S["gt_turned"], layer + 1)
                act.activation(gT[0:NE, :], bank[0:NE, 6, 0:TOK], ACT.Copy).then_inc(S["gt_copied"], 1)
                for e in range(0, NE, 2):
                    act.wait_ge(S["gb_done"], 8 * layer + e // 2 + 1)
                    act.activation(gb[:, e:e + 2, :], b2(4 + (e // 2) % 2), ACT.Copy).then_inc(S["gb_out"], 1)
                with act.Fori(0, NE // 2) as it:
                    for u in range(4):
                        n = 32 * layer + u
                        act.wait_ge(S["unit_done"], it * 4 + (n + 1))
                        act.wait_ge(S["prod_done"], it * 4 + (n + 1))
                        act.activation(sil[:, u % 2, :], bank[:, 4 + u % 2, 0:TOK], ACT.Silu
                                       ).then_inc(S["sil_done"], 1)

            norm(0)
            moe(0)
            norm(1)

            act.wait_ge(S["mgate_done"], 1)
            for g in range(2):
                act.activation(mrow[0:MH, g, :], bank[0:MH, 6, g * TOK:(g + 1) * TOK], ACT.Identity,
                               bias=mg_b[:, g:g + 1]).then_inc(S["mgate_x"], 1)
            act.wait_ge(S["mgate_x"], 2)
            link(act.activation(mrow[0:MH, 2, :], mrow[0:MH, 1, :], ACT.Abs))
            link(act.activation(mrow[0:MH, 3, :], mrow[0:MH, 2, :], ACT.Exp, scale=-1.0))
            act.activation(mrow[0:MH, 4, :], mrow[0:MH, 3, :], ACT.Ln, bias=1.0).then_inc(S["mgate_ln"], 1)
            for j in range(16):
                act.wait_ge(used, ML_IN + j + 1)
                bk = b2(j % 4)
                if j < 8:
                    if j >= 2:
                        act.wait_ge(S["qk_done"], 2 * (j - 1))
                    for a in range(2):
                        m = 2 * j + a
                        act.activation(cv[:, j % 2, a, :], bk[:, a, :], ACT.Identity,
                                       scale=cols[:, 2, 48 + m:49 + m], bias=vcol(V_CONVB + m)
                                       ).then_inc(S["conv_a"], 1)
                    if j >= 1:
                        for a in range(2):
                            m = 2 * (j - 1) + a
                            act.wait_ge(S["conv_done"], m + 1)
                            act.activation(qkT[:, m, :], cv[:, (j - 1) % 2, a, :], ACT.Silu
                                           ).then_inc(S["qk_done"], 1)
                elif j < 12:
                    if j == 8:
                        for a in range(2):
                            m = 14 + a
                            act.wait_ge(S["conv_done"], m + 1)
                            act.activation(qkT[:, m, :], cv[:, 1, a, :], ACT.Silu).then_inc(S["qk_done"], 1)
                    act.activation(vM[:, :, (j - 8) * SC:(j - 7) * SC], bk, ACT.Copy).then_inc(S["proj_out"], 1)
                else:
                    act.activation(oG[:, 2 * (j - 12):2 * (j - 12) + 2, :], bk, ACT.Sigmoid
                                   ).then_inc(S["proj_out"], 1)
            for hd in range(MH):
                q = hd % 2
                act.wait_ge(S["md_done"], 2 * hd + 2)
                if hd >= 2:
                    act.wait_ge(S["ms_done"], hd - 1)
                act.activation(eM[:, q, :], dM[:, q, :], ACT.Exp, scale=-1.0).then_inc(S["me_done"], 1)
                act.wait_ge(S["mfl_done"], 2 * hd + 1)
                if hd >= 2:
                    act.wait_ge(S["mh_done"], hd - 1)
                act.activation(fl[:, q, :], bank[:, 6, 0:TOK], ACT.Exp, scale=-1.0).then_inc(S["mfl_done"], 1)
            for b in range(4):
                act.wait_ge(S["mh_done"], 2 * b + 2)
                act.activation(qkT[:, 2 * b:2 * b + 2, :], hh[:, 2 * b:2 * b + 2, :], ACT.Square
                               ).then_inc(S["hsq_done"], 1)
            for b in range(4):
                act.wait_ge(S["hms_done"], 2 + b + 1)
                act.activation(qkT[:, 8 + 2 * b:10 + 2 * b, :], b2(b), ACT.Sqrt, bias=EPS_H
                               ).then_inc(S["hstd_done"], 1)
            norm(2)
            moe(1)
            norm(3)
            for b in range(4):
                act.wait_ge(S["final_turned"], b + 1)
                act.activation(sqT[:, 2 * b:2 * b + 2, :], b2(b), ACT.Copy).then_inc(S["final_out"], 1)

        @block.vector
        def _(dve):
            step = [0]

            def link(ins):
                step[0] += 1
                ins.then_inc(S["dve_step"], 1)
                dve.wait_ge(S["dve_step"], step[0])

            tt, ts, stt = dve.tensor_tensor, dve.tensor_scalar, dve.scalar_tensor_tensor
            lre, lim, lrd, ang, mag, are, sn, cs, nre, sh, kk, t0, t1, cre, cim, rdn = (
                s5p[:, i, :] for i in range(16))
            dtb = bc(s5dt[:, 1, :].rearrange("j (g a) -> j g a", a=1), 16, 2, 64)
            g2 = lambda a: a.rearrange("j (g p) -> j g p", g=2)

            dve.nop().then_inc(S["prod_done"], 2)
            dve.nop().then_inc(S["he_done"], 2)
            dve.wait_ge(S["tables_ready"], 1)
            tt(g2(lrd), g2(lre), dtb, ALU.mult).then_inc(S["tables_ready"], 1)
            link(tt(g2(ang), g2(lim), dtb, ALU.mult))
            link(ts(kk, ang, 1.0 / (2.0 * np.pi), ROUND, ALU.mult, ALU.add))
            link(ts(kk, kk, ROUND, None, ALU.subtract))
            for part in TWO_PI:
                link(stt(ang, kk, -part, ang, ALU.mult, ALU.add))
            dve.wait_ge(S["tables_ready"], 3)
            ts(ang, ang, PI_BELOW, -PI_BELOW, ALU.min, ALU.max).then_inc(S["tables_ready"], 1)
            dve.wait_ge(S["tables_ready"], 6)
            link(tt(cs, sh, sh, ALU.mult))
            link(ts(cs, cs, -2.0, 1.0, ALU.mult, ALU.add))
            link(tt(are, mag, cs, ALU.mult))
            link(ts(nre, are, 1.0, None, ALU.subtract))
            link(tt(are, mag, sn, ALU.mult))
            link(tt(t0, lre, lre, ALU.mult))
            link(tt(t1, lim, lim, ALU.mult))
            link(tt(t0, t0, t1, ALU.add))
            link(dve.reciprocal(rdn, t0))
            link(tt(t0, nre, lre, ALU.mult))
            link(tt(t1, are, lim, ALU.mult))
            link(tt(t0, t0, t1, ALU.add))
            link(tt(cre, t0, rdn, ALU.mult))
            link(tt(t0, are, lre, ALU.mult))
            link(tt(t1, nre, lim, ALU.mult))
            link(tt(t0, t0, t1, ALU.subtract))
            tt(cim, t0, rdn, ALU.mult).then_inc(S["bb_done"], 1)

            dve.wait_ge(S["cols_turned"], 1)
            dve.tensor_copy(cols[:, 0, 0:96], bank[:, 6, 0:96])
            dve.tensor_copy(cols[:, 1, 0:V_END], bank[:, 6, P:P + V_END])
            dve.tensor_copy(cols[:, 2, 0:64], bank[:, 6, 2 * P:2 * P + 64]).then_inc(S["cols_ready"], 1)
            dve.wait_ge(S["s5_turned"], 1)
            link(dve.tensor_copy(s5c[:, :, :], bank[:, 5, 0:5 * ST].rearrange("p (a j) -> p a j", a=5)))

            link(dve.memset(bb[:, :, :, :], 0.0))
            dve.wait_ge(S["bc_loaded"], 96)
            coef_b = [bc(s5c[:, 3 + i, :].rearrange("p (j a) -> p j a", a=1), P, ST, S5_G) for i in range(2)]
            for i, (a, b) in enumerate(((0, 0), (1, 1), (0, 1), (1, 0))):
                link(tt(bt[:, i, :, :], b_raw[:, b, :, :], coef_b[a], ALU.mult))
            for i, op in ((0, ALU.subtract), (1, ALU.add)):
                for g in range(2):
                    ps = slice(64 * g, 64 * g + 64)
                    link(tt(bb[ps, i, :, 16 * g:16 * g + 16], bt[ps, 2 * i, :, :], bt[ps, 2 * i + 1, :, :], op))
            dve.nop().then_inc(S["bb_done"], 1)
            link(dve.memset(ctT[:, :, :, :], 0.0))
            for i, sign in ((0, 1.0), (1, -1.0)):
                dve.wait_ge(S["ct_turned"], i + 1)
                for g in range(2):
                    ps = slice(64 * g, 64 * g + 64)
                    src = bank[ps, i, :].rearrange("p (j g c) -> p j g c", g=2, c=16)[:, :, g, :]
                    ins = ts(ctT[ps, i, :, 16 * g:16 * g + 16], src, sign, None, ALU.mult)
                ins.then_inc(S["ct_ready"], 1)
            for i in range(2):
                dve.wait_ge(S["bb_turned"], i + 1)
                dve.tensor_copy(bbT[:, i, :, :], bank[:, 2 + i, :].rearrange("p (k n) -> p k n", k=UC)
                                ).then_inc(S["bbT_ready"], 1)

            dve.memset(cosT[:, :, 0:1], 1.0)
            dve.memset(sinT[:, :, 0:1], 0.0)
            link(dve.tensor_copy(en[:, 0, :, :], s5c[:, 1:3, :]))
            n = 1
            while n < TOK:
                c_n = bc(en[:, 0, 0, :].rearrange("p (j a) -> p j a", a=1), P, ST, n)
                s_n = bc(en[:, 0, 1, :].rearrange("p (j a) -> p j a", a=1), P, ST, n)
                tm = tmpA[:, :, 0:n]
                link(tt(tm, sinT[:, :, 0:n], s_n, ALU.mult))
                link(tt(cosT[:, :, n:2 * n], cosT[:, :, 0:n], c_n, ALU.mult))
                link(tt(cosT[:, :, n:2 * n], cosT[:, :, n:2 * n], tm, ALU.subtract))
                link(tt(tm, cosT[:, :, 0:n], s_n, ALU.mult))
                link(tt(sinT[:, :, n:2 * n], sinT[:, :, 0:n], c_n, ALU.mult))
                link(tt(sinT[:, :, n:2 * n], sinT[:, :, n:2 * n], tm, ALU.add))
                link(tt(en[:, 1, :, :], en[:, 0, :, :], en[:, 0, :, :], ALU.mult))
                link(tt(en[:, 2, 1, :], en[:, 0, 0, :], en[:, 0, 1, :], ALU.mult))
                link(tt(en[:, 0, 0, :], en[:, 1, 0, :], en[:, 1, 1, :], ALU.subtract))
                link(ts(en[:, 0, 1, :], en[:, 2, 1, :], 2.0, None, ALU.mult))
                n *= 2

            def modulation(layer, parts, done):
                dve.wait_ge(mused, done)
                a, b = 8 * parts[0], 8 * parts[-1] + 8
                link(tt(mod[:, layer, a:b], bank[:, 7, 64 * layer + a:64 * layer + b],
                        cols[:, 0, 48 * layer + a:48 * layer + b], ALU.add))
                for q in (SC1, G1, SC2, G2):
                    if q in parts:
                        m = mod[:, layer, 8 * q:8 * q + 8]
                        link(ts(m, m, 1.0, None, ALU.add))

            modulation(0, (SH1, SC1), 8)
            dve.nop().then_inc(S["mod_ready"], 1)

            dve.wait_ge(S["gate_ln"], 1)
            link(stt(cum[:, :, :], cum[:, :, :], 0.0, kd[:, 0, :, :], ALU.min, ALU.subtract))
            dve.wait_ge(S["h_ready"], 8)
            dve.wait_ge(S["ax_ready"], 8)
            for ch in range(QC):
                dve.tensor_tensor_scan(qd[:, 0, ch, :], bc(ones[:, 0:1], P, TOK), cum[:, ch, :], 0.0,
                                       ALU.mult, ALU.add).then_inc(S["cum_done"], 1)
            dve.wait_ge(S["cum_done"], 2)
            link(dve.tensor_copy(cum[:, :, :], qd[:, 0, :, :]))

            def rot1(j):
                dve.wait_ge(S["bu_done"], j + 1)
                if j >= 2:
                    dve.wait_ge(S["vin_done"], j - 1)
                for i, t in enumerate((cosT, sinT)):
                    tb = bc(t[:, j, :].rearrange("p (a t) -> p a t", a=1), P, 2, TOK)
                    tt(rot[:, j % 2, i, :, :], b2(4 + j % 2), tb, ALU.mult).then_inc(S["rot1_done"], 1)

            def scans(j):
                dve.wait_ge(S["vin_done"], j + 1)
                if j:
                    dve.wait_ge(S["rot2_done"], 2 * j)
                for i in range(2):
                    dve.tensor_tensor_scan(zst[:, i, :], bc(s5c[:, 0, j:j + 1], P, TOK), vin[:, j % 2, i, :],
                                           0.0, ALU.mult, ALU.add).then_inc(S["scan_done"], 1)
                dve.wait_ge(S["scan_done"], 2 * j + 2)
                if j >= 1:
                    dve.wait_ge(S["sst_done"], j)
                for i, t in enumerate((cosT, sinT)):
                    tb = bc(t[:, j, :].rearrange("p (a t) -> p a t", a=1), P, 2, TOK)
                    tt(rotp[:, i, :, :], zst[:, :, :], tb, ALU.mult).then_inc(S["rot2_done"], 1)

            def skip(k):
                dve.wait_ge(S["ys_done"], 4 * k + 4)
                stt(yy[:, k, :], uT[:, k, :], vcol(V_D + k), bank[:, 6, 0:TOK], ALU.mult, ALU.add
                    ).then_inc(S["yy_done"], 1)

            for j in range(ST + 1):
                if j < ST:
                    rot1(j)
                if j >= 1:
                    scans(j - 1)
                    if j - 1 >= 4 and (j - 1) % 4 == 1:
                        skip((j - 1) // 4 - 1)
            skip(UC - 1)

            dve.wait_ge(S["rot2_done"], 2 * ST)
            link(dve.memset(attD[:, :, :, :, :], 0.0))

            def level_dif(lv):
                h = 1 << lv
                if lv >= 2:
                    dve.wait_ge(S["dec_done"], 2 * (lv - 1))
                m5 = cum.rearrange("p c (n h) -> p (c n) h", h=2 * h)
                ref = bc(m5[:, :, h - 1:h], P, QC * TOK // (2 * h), 2 * h)
                o5 = dif[:, lv % 2, :, :].rearrange("p c (n h) -> p (c n) h", h=2 * h)
                tt(o5, m5, ref, ALU.subtract).then_inc(S["dif_done"], 1)

            def level_out(n, lv):
                for par in range(2):
                    dve.wait_ge(S["att_done"], 2 * n + par + 1)
                    if n:
                        dve.wait_ge(S["att_out"], 2 * n + par - 1)
                    src = bank[:, 2 * (n % 2) + par, :].rearrange("p (b t) -> p b t", t=P)
                    if lv == LEVELS - 1 and n < LEVELS:
                        dve.tensor_copy(attX[:, par, :, :], src[:, 0:2, :]).then_inc(S["att_out"], 1)
                    else:
                        mask = bc(level_mask[:, lv, :].rearrange("p (a t) -> p a t", a=1), P, 4, P)
                        dve.copy_predicated(attD[:, par, :, :, :].rearrange("p a b t -> p (a b) t"), mask, src
                                            ).then_inc(S["att_out"], 1)

            level_dif(0)
            for lv in range(LEVELS):
                if lv + 1 < LEVELS:
                    level_dif(lv + 1)
                if lv == 1:
                    for k in range(UC):
                        dve.wait_ge(S["glu_sig"], k + 1)
                        tt(yT[:, k, :], zT[:, k, :], sgT[:, k, :], ALU.mult).then_inc(S["ya_done"], 1)
                level_out(lv, lv)
            level_out(LEVELS, LEVELS - 1)

            modulation(0, (G1, SH2, SC2, G2), 24)

            for b in range(2):
                dve.wait_ge(S["hstd_done"], b + 1)
                link(dve.reciprocal(sgT[:, 2 * b:2 * b + 2, :], sgT[:, 2 * b:2 * b + 2, :]))
                link(tt(oT[:, 2 * b:2 * b + 2, :], oT[:, 2 * b:2 * b + 2, :], sgT[:, 2 * b:2 * b + 2, :], ALU.mult))
                for k in (2 * b, 2 * b + 1):
                    stt(yT[:, UC + k, :], oT[:, k, :], vcol(V_GNORM + k), rS[:, k, :], ALU.mult, ALU.mult
                        ).then_inc(S["yb_done"], 1)

            def norm(i):
                layer, second = i // 2, i % 2
                gain, shift = (LN_G2, LN_B2) if second else (LN_G1, LN_B1)
                gv = cols[:, 1, gain + 8 * layer:gain + 8 * layer + 8]
                bv = cols[:, 1, shift + 8 * layer:shift + 8 * layer + 8]
                if i < 3:
                    nl, sc, sh_ = (layer, SC2, SH2) if not second else (layer + 1, SC1, SH1)
                    scv = mod[:, nl, 8 * sc:8 * sc + 8]
                    link(tt(coef[:, i, 0, :], gv, scv, ALU.mult))
                    link(tt(coef[:, i, 1, :], bv, scv, ALU.mult))
                    link(tt(coef[:, i, 1, :], coef[:, i, 1, :], mod[:, nl, 8 * sh_:8 * sh_ + 8], ALU.add))
                    link(ts(coef[:, i, 2, :], gv, ALPHA, None, ALU.mult))
                    ts(coef[:, i, 3, :], bv, ALPHA, None, ALU.mult).then_inc(S["coef_ready"], 1)
                else:
                    link(dve.tensor_copy(coef[:, i, 0, :], gv))
                    dve.tensor_copy(coef[:, i, 1, :], bv).then_inc(S["coef_ready"], 1)
                dve.wait_ge(S["coef_ready"], i + 1)
                dve.wait_ge(S["ax_ready"], 8 * i + 8)
                dve.wait_ge(S["h_ready"], 8 * i + 8)
                for ch in range(DC):
                    if not second:
                        if ch % 2 == 0:
                            dve.wait_ge(used, (ML_OUT if layer else AB_OUT) + ch // 2 + 1)
                    elif ch == 0:
                        dve.wait_ge(used, MOE_AT[layer] + 3 * NE)
                    stt(rT[:, ch, :], b2(ch // 2)[:, ch % 2, :], mcol(layer, G2 if second else G1, ch),
                        axT[:, ch, :], ALU.mult, ALU.add).then_inc(S["r_done"], 1)
                dve.wait_ge(S["mean_done"], i + 1)
                mb = bc(bank[:, 4, 0:TOK].rearrange("p (a t) -> p a t", a=1), P, 2, TOK)
                for b in range(4):
                    v = rT[:, 2 * b:2 * b + 2, :]
                    tt(v, v, mb, ALU.subtract).then_inc(S["cen_done"], 1)
                dve.wait_ge(S["std_done"], i + 1)
                link(dve.reciprocal(std[:, 1, :], std[:, 0, :]))
                sb_ = bc(std[:, 1, :].rearrange("p (a t) -> p a t", a=1), P, 2, TOK)
                for b in range(4):
                    v = rT[:, 2 * b:2 * b + 2, :]
                    tt(v, v, sb_, ALU.mult).then_inc(S["norm_done"], 1)

            def moe(layer):
                aff = rt[:, 0, 0:TT * NE]
                sel, one, two, gates = (rt[:, i, 0:TT * NE] for i in (1, 2, 3, 4))
                psum_ = rt[:, 5, 0:TT * NG * 6].rearrange("p (q s) -> p q s", s=6)
                score, best, key, gsel = (rt[:, i, 0:TT * NG] for i in (6, 7, 8, 9))
                kmax, tot = (rt[:, i, 0:TT] for i in (10, 11))
                order = rt[:, 12, 0:NG]
                v4 = lambda a: a.rearrange("p (q e) -> p q e", e=EG)
                vg = lambda a: a.rearrange("p (a g) -> p a g", g=NG)
                for g in range(NG):
                    link(dve.memset(order[:, g:g + 1], float(NG - g)))
                dve.wait_ge(S["aff_done"], layer + 1)
                link(tt(sel.rearrange("p (a e) -> p a e", e=NE), aff.rearrange("p (a e) -> p a e", e=NE),
                        bc(rbias[:, :].rearrange("p (a e) -> p a e", a=1), P, TT, NE), ALU.add))
                s4 = v4(sel)
                at = 0
                for d in range(1, EG):
                    link(tt(psum_[:, :, at:at + EG - d], s4[:, :, 0:EG - d], s4[:, :, d:EG], ALU.add))
                    at += EG - d
                link(dve.tensor_reduce(score, psum_, AX.X, ALU.max))
                link(dve.tensor_reduce(kmax, vg(score), AX.X, ALU.max))
                link(tt(vg(best), vg(score), bc(kmax.rearrange("p (a g) -> p a g", g=1), P, TT, NG), ALU.is_equal))
                link(tt(vg(key), vg(best), bc(order.rearrange("p (a g) -> p a g", a=1), P, TT, NG), ALU.mult))
                link(dve.tensor_reduce(kmax, vg(key), AX.X, ALU.max))
                link(tt(vg(gsel), vg(key), bc(kmax.rearrange("p (a g) -> p a g", g=1), P, TT, NG), ALU.is_equal))
                cmp_ = pairs[:, 0, :, :, :].rearrange("p a q e -> p (a q e)").rearrange(
                    "p (q i j) -> p q i j", i=EG, j=EG)
                eq_ = pairs[:, 1, :, :, :].rearrange("p a q e -> p (a q e)").rearrange(
                    "p (q i j) -> p q i j", i=EG, j=EG)
                Q = TT * NG
                sj = bc(s4.rearrange("p q (i j) -> p q i j", i=1), P, Q, EG, EG)
                si = bc(s4.rearrange("p q (i j) -> p q i j", j=1), P, Q, EG, EG)
                link(tt(cmp_, sj, si, ALU.is_gt))
                for i in range(1, EG):
                    link(tt(eq_[:, :, i, 0:i], sj[:, :, i, 0:i], si[:, :, i, 0:i], ALU.is_equal))
                    link(tt(cmp_[:, :, i, 0:i], cmp_[:, :, i, 0:i], eq_[:, :, i, 0:i], ALU.add))
                link(dve.tensor_reduce(one, cmp_, AX.X, ALU.add))
                link(ts(one, one, 2.0, None, ALU.is_lt))
                link(tt(v4(one), v4(one), bc(gsel.rearrange("p (q e) -> p q e", e=1), P, Q, EG), ALU.mult))
                link(tt(two, one, aff, ALU.mult))
                link(dve.tensor_reduce(tot, two.rearrange("p (a e) -> p a e", e=NE), AX.X, ALU.add))
                link(dve.reciprocal(tot, tot))
                tt(gates.rearrange("p (a e) -> p a e", e=NE), two.rearrange("p (a e) -> p a e", e=NE),
                   bc(tot.rearrange("p (a e) -> p a e", e=1), P, TT, NE), ALU.mult).then_inc(S["gates_done"], 1)

                dve.wait_ge(S["gb_out"], 8 * layer + 8)
                with dve.Fori(0, NE // 2) as it:
                    for u in range(4):
                        n = 32 * layer + u
                        dve.wait_ge(S["sil_done"], it * 4 + (n + 1))
                        dve.wait_ge(S["he_done"], it * 4 + (n + 1))
                        tt(pr[:, u % 2, :], bank[:, 4 + u % 2, TOK:2 * TOK], sil[:, u % 2, :], ALU.mult
                           ).then_inc(S["prod_done"], 1)
                        dve.wait_ge(S["prod_done"], it * 4 + (n + 3))
                        dve.wait_ge(used, it * RING + (MOE_AT[layer] + 3 * (u // 2) - 3))
                        tt(he[:, u // 2, u % 2, :].rearrange("p (a t) -> p a t", a=1),
                           pr[:, u % 2, :].rearrange("p (a t) -> p a t", a=1),
                           gb[:, bass.ds(it * 2 + u // 2, 1), :], ALU.mult).then_inc(S["he_done"], 1)

            norm(0)
            moe(0)
            modulation(1, (SH1, SC1, G1, SH2, SC2, G2), 48)
            norm(1)

            R = [mrow[0:MH, i, :] for i in range(12)]
            dve.wait_ge(S["mgate_ln"], 1)
            link(stt(R[5], R[1], 0.0, R[4], ALU.min, ALU.subtract))
            link(dve.tensor_tensor_scan(R[6], bc(ones[0:MH, 0:1], MH, TOK), R[5], 0.0, ALU.mult, ALU.add))
            link(tt(R[7], R[0], R[6], ALU.subtract))
            link(dve.tensor_tensor_scan(R[8], R[7], R[7], 0.0, ALU.max, ALU.max))
            tt(R[9], R[8], R[6], ALU.add).then_inc(S["mrow_done"], 1)
            dve.wait_ge(S["mcol_turned"], 1)
            dve.tensor_copy(ccol[:, :, :], bank[:, 6, 0:TT * MH].rearrange("p (a h) -> p a h", a=TT)
                            ).then_inc(S["mcol_done"], 1)
            for j in range(8):
                for a in range(2):
                    m = 2 * j + a
                    dve.wait_ge(S["conv_a"], 2 * j + 2)
                    o = cv[:, j % 2, a, :]
                    src = b2(j % 4)[:, a, :]
                    for tap in range(CW - 2, -1, -1):
                        d = CW - 1 - tap
                        ins = stt(o[:, d:TOK], src[:, 0:TOK - d], cols[:, 2, 16 * tap + m:16 * tap + m + 1],
                                  o[:, d:TOK], ALU.mult, ALU.add)
                        if tap:
                            link(ins)
                    ins.then_inc(S["conv_done"], 1)
            for hd in range(MH):
                q = hd % 2
                dve.wait_ge(S["mb_done"], hd + 1)
                if hd >= 2:
                    dve.wait_ge(S["me_done"], hd - 1)
                src = bank[:, q, 0:384]
                ts(dM[:, q, 0:TOK], src[:, 0:TOK], ccol[:, 0, hd:hd + 1], 0.0, ALU.subtract, ALU.max
                   ).then_inc(S["md_done"], 1)
                ts(dM[:, q, TOK:384], src[:, TOK:384], ccol[:, 1, hd:hd + 1], 0.0, ALU.subtract, ALU.max
                   ).then_inc(S["md_done"], 1)
                dve.wait_ge(S["me_done"], hd + 1)
                dve.wait_ge(S["mqk_done"], hd + 1)
                if hd >= 2:
                    dve.wait_ge(S["mnum_done"], hd - 1)
                stt(sM[:, q, :], bank[:, 2 + q, 0:384], float(P) ** -0.5, eM[:, q, :], ALU.mult, ALU.mult
                    ).then_inc(S["ms_done"], 1)
                dve.wait_ge(S["mnum_done"], hd + 1)
                dve.wait_ge(S["mfl_done"], 2 * hd + 2)
                nd = b2(4 + q)
                if hd:
                    dve.wait_ge(S["mh_done"], hd)
                link(stt(dn[:, 0, :], nd[:, 1, :], -1.0, fl[:, q, :], ALU.mult, ALU.max))
                link(tt(dn[:, 0, :], nd[:, 1, :], dn[:, 0, :], ALU.max))
                link(dve.reciprocal(dn[:, 1, :], dn[:, 0, :]))
                tt(hh[:, hd, :], nd[:, 0, :], dn[:, 1, :], ALU.mult).then_inc(S["mh_done"], 1)
            for b in range(4):
                rs = qkT[:, 8 + 2 * b:10 + 2 * b, :]
                v = hh[:, 2 * b:2 * b + 2, :]
                dve.wait_ge(S["hstd_done"], 2 + b + 1)
                link(dve.reciprocal(rs, rs))
                link(tt(v, v, rs, ALU.mult))
                for k in (2 * b, 2 * b + 1):
                    stt(yT[:, k, :], hh[:, k, :], vcol(V_MNORM + k), oG[:, k, :], ALU.mult, ALU.mult
                        ).then_inc(S["yb_done"], 1)
            norm(2)
            moe(1)
            norm(3)

        @block.tensor
        def _(pe):
            mm = pe.matmul

            pe.wait_ge(S["pool_const"], 1)
            pe.wait_ge(S["x_loaded"], 16)
            xin = sqT[:, :, :].rearrange("p (a b) t -> p a (b t)", a=TT)
            for b in range(4):
                for ch in (2 * b, 2 * b + 1):
                    for t in range(TT):
                        ins = pe.transpose(b2(b)[:, ch % 2, t * P:(t + 1) * P], xin[:, t, ch * P:(ch + 1) * P],
                                           ident[:, :])
                ins.then_inc(S["x_turned"], 1)
            pe.wait_ge(S["rows_loaded"], 16 * 13)
            for i, n in enumerate((96, V_END, 64)):
                ins = pe.transpose(bank[:, 6, i * P:i * P + n], rows[0:n, i, :], ident[0:n, 0:n])
            ins.then_inc(S["cols_turned"], 1)

            def mod_slot(n, col, at=None):
                s = mring[:, n % MRING, :].rearrange("p (c n) -> p c n", c=DC)
                for a in range(2):
                    for k in range(DC):
                        ins = mm(bank[:, 7, col + a:col + a + 1], s[:, k, a * P:(a + 1) * P], c_col[:, 1, k:k + 1],
                                 start=(k == 0), stop=(k == DC - 1))
                ins.then_inc(mused, 1)
                return ins

            pe.wait_ge(S["c_ready"], 1)
            for n in range(3):
                pe.wait_ge(mlanded[n % MRING], 16 * (n // MRING + 1))
                mod_slot(n, 2 * n)
            pe.wait_ge(S["bb_done"], 1)
            for i, row in enumerate((4, 7, 6, 13, 14)):
                ins = pe.transpose(bank[:, 5, i * ST:(i + 1) * ST], s5p[:, row, :], ident[0:ST, 0:ST])
            ins.then_inc(S["s5_turned"], 1)
            pe.wait_ge(S["bc_loaded"], 96)
            pe.wait_ge(S["xT_ready"], 4)
            for i in range(2):
                for k in range(UC):
                    ins = pe.transpose(bank[:, i, k * P:(k + 1) * P], c_raw[:, i, k, :], ident[:, :])
                ins.then_inc(S["ct_turned"], 1)
            pe.wait_ge(S["bb_done"], 2)
            for i in range(2):
                for k in range(UC):
                    ins = pe.transpose(bank[:, 2 + i, k * P:(k + 1) * P],
                                       bb[:, i, 4 * k:4 * k + 4, :].rearrange("p j c -> p (j c)"), ident[:, :])
                ins.then_inc(S["bb_turned"], 1)
            for n in range(3, 8):
                pe.wait_ge(mlanded[n % MRING], 16 * (n // MRING + 1))
                mod_slot(n, 2 * n)

            pe.wait_ge(S["cols_ready"], 1)
            pe.wait_ge(S["small_loaded"], 112)
            pe.wait_ge(S["h_ready"], 8)
            for k in range(DC):
                ins = mm(bank[0:RANK, 6, 0:TOK], lr_w[:, k, :], hT[:, k, :], start=(k == 0), stop=(k == DC - 1))
            ins.then_inc(S["lr_done"], 1)

            def by_feature(n, bk, src):
                s = ring[:, n % RING, :].rearrange("p (c n) -> p c n", c=DC)
                pe.wait_ge(landed[n % RING], 16 * (n // RING + 1))
                for a in range(2):
                    for k in range(DC):
                        ins = mm(b2(bk)[:, a, :], s[:, k, a * P:(a + 1) * P], src[:, k, :],
                                 start=(k == 0), stop=(k == DC - 1))
                ins.then_inc(used, 1)

            def by_token(n, bk):
                s = ring[:, n % RING, :].rearrange("p (c n) -> p c n", c=DC)
                pe.wait_ge(landed[n % RING], 16 * (n // RING + 1))
                for t in range(TT):
                    for k in range(DC):
                        ins = mm(b2(bk)[:, t, :], hT[:, k, t * P:(t + 1) * P], s[:, k, :],
                                 start=(k == 0), stop=(k == DC - 1))
                ins.then_inc(used, 1)

            def bu(j):
                if j >= 2:
                    pe.wait_ge(S["rot1_done"], 2 * (j - 1))
                ps = slice(32 * (j % 4), 32 * (j % 4) + 32)
                for i in range(2):
                    ins = mm(b2(4 + j % 2)[:, i, :], bbT[ps, i, j // 4, :], uT[ps, j // 4, :],
                             start=True, stop=True)
                ins.then_inc(S["bu_done"], 1)

            def ys(j):
                pe.wait_ge(S["sst_done"], j + 1)
                if j % 4 == 0 and j:
                    pe.wait_ge(S["yy_done"], j // 4)
                r = j % 4
                for i in range(2):
                    ins = mm(bank[32 * r:32 * r + 32, 6, 0:TOK], ctT[:, i, j, :], sst[:, j % 2, i, :],
                             start=(i == 0), stop=(i == 1))
                ins.then_inc(S["ys_done"], 1)

            pe.wait_ge(S["ct_ready"], 2)
            by_feature(AB_U, 0, hT)
            by_feature(AB_U + 1, 1, hT)
            pe.wait_ge(S["lr_copied"], 1)
            for m in range(QC):
                ins = mm(b2(5)[:, m, :], gate_w[:, m * P:(m + 1) * P],
                         s5p[0:RANK, 0:2, :].rearrange("p a t -> p (a t)"), start=True, stop=True)
            ins.then_inc(S["gate_done"], 1)
            pe.wait_ge(S["proj_out"], 2)
            pe.wait_ge(S["bbT_ready"], 2)
            pe.wait_ge(S["gate_x"], 2)
            for j in range(2, 8):
                if j >= 4:
                    pe.wait_ge(S["proj_out"], j - 3)
                if 4 <= j < 6:
                    by_token(j, j % 4)
                else:
                    by_feature(j, j % 4, hT)
                bu(2 * (j - 2))
                if j > 2:
                    ys(2 * (j - 2) - 2)
                bu(2 * (j - 2) + 1)
                if j > 2:
                    ys(2 * (j - 2) - 1)
            for j in range(12, 16):
                bu(j)
                ys(j - 2)
            ys(14)
            ys(15)

            pe.wait_ge(S["rot1_done"], 2 * ST)
            pe.wait_ge(landed[AB_GLU % RING], 16 * (AB_GLU // RING + 1))
            s = ring[:, AB_GLU % RING, :].rearrange("p (c n) -> p c n", c=UC)
            pe.wait_ge(S["z_done"], UC)
            for b in range(2):
                for a in range(2):
                    m = 2 * b + a
                    for k in range(UC):
                        ins = mm(b2(4 + b)[:, a, :], s[:, k, m * P:(m + 1) * P], zT[:, k, :],
                                 start=(k == 0), stop=(k == UC - 1))
                ins.then_inc(used if b else S["glu_done"], 1)

            pe.wait_ge(S["proj_out"], 8)
            for n in range(LEVELS + 1):
                diag = n == LEVELS
                if diag:
                    ks, qs = kT, qT
                else:
                    pe.wait_ge(S["kq_done"], n + 1)
                    ks, qs = kd[:, n % 2, :, :], qd[:, n % 2, :, :]
                if n >= 2:
                    pe.wait_ge(S["att_out"], 2 * (n - 1))
                for par in range(2):
                    ps = slice(64 * par, 64 * par + 64)
                    o = bank[:, 2 * (n % 2) + par, :].rearrange("p (b t) -> p b t", t=P)
                    for pair in range(2):
                        if n == LEVELS - 1:
                            ins = mm(o[:, pair, :], ks[ps, pair, 0:P], qs[ps, pair, P:TOK], start=True, stop=True)
                        else:
                            for t in range(TT):
                                ins = mm(o[:, 2 * pair + t, :], ks[ps, pair, t * P:(t + 1) * P],
                                         qs[ps, pair, t * P:(t + 1) * P], start=True, stop=True)
                    ins.then_inc(S["att_done"], 1)
                if n < 8:
                    for m in (8 + 2 * n, 9 + 2 * n):
                        pe.wait_ge(mlanded[m % MRING], 16 * (m // MRING + 1))
                        mod_slot(m, 2 * m)
            pe.wait_ge(S["att_out"], 2 * (LEVELS + 1))
            for b in range(2):
                for a in range(2):
                    hd = 2 * b + a
                    o = b2(b)[:, a, :]
                    vh = lambda t: vS[:, t, hd * GDV:(hd + 1) * GDV]
                    mm(o[:, 0:P], vh(0), attD[:, hd % 2, hd // 2, 0, :], start=True, stop=True)
                    mm(o[:, P:TOK], vh(0), attX[:, hd % 2, hd // 2, :], start=True, stop=False)
                    ins = mm(o[:, P:TOK], vh(1), attD[:, hd % 2, hd // 2, 1, :], start=False, stop=True)
                ins.then_inc(S["av_done"], 1)
            pe.wait_ge(S["glu_sig"], 4)
            for b in range(2):
                pe.wait_ge(S["hsq_done"], b + 1)
                mm(bank[:, 4 + b, :], head_w[:, :], yy[:, 2 * b:2 * b + 2, :].rearrange("p a t -> p (a t)"),
                   start=True, stop=True).then_inc(S["hms_done"], 1)
            pe.wait_ge(S["av_out"], 2)
            pe.wait_ge(S["ya_done"], 4)
            pe.wait_ge(S["yb_done"], 4)
            for j in range(4):
                by_feature(AB_OUT + j, j, yT)

            def norm(i):
                for ch in range(DC):
                    pe.wait_ge(S["r_done"], 8 * i + ch + 1)
                    ins = mm(bank[:, 4, 0:TOK], mean_w[:, :], rT[:, ch, :], start=(ch == 0), stop=(ch == DC - 1))
                ins.then_inc(S["mean_done"], 1)
                for ch in range(DC):
                    if ch % 2 == 0:
                        pe.wait_ge(S["sq_done"], 4 * i + ch // 2 + 1)
                    ins = mm(bank[:, 5, 0:TOK], mean_w[:, :], sqT[:, ch, :], start=(ch == 0), stop=(ch == DC - 1))
                ins.then_inc(S["var_done"], 1)

            def moe(layer):
                pe.wait_ge(S["h_ready"], 8 * (2 * layer + 2))
                for t in range(TT):
                    for k in range(DC):
                        ins = mm(bank[:, 6, t * NE:(t + 1) * NE], hT[:, k, t * P:(t + 1) * P], router_sb[:, k, :],
                                 start=(k == 0), stop=(k == DC - 1))
                ins.then_inc(S["logit_done"], 1)
                pe.wait_ge(S["r_done"], 8 * (2 * layer + 1))
                for b in range(4):
                    mm(bank[:, b, :], zero16[:, 0:P], zero16[:, :], start=True, stop=True, skip_group_check=True)
                pe.wait_ge(S["gates_done"], layer + 1)
                for t in range(TT):
                    ins = pe.transpose(bank[0:NE, 6, t * P:(t + 1) * P],
                                       rt[:, 4, t * NE:(t + 1) * NE], ident[:, :])
                ins.then_inc(S["gt_turned"], 1)
                pe.wait_ge(S["gt_copied"], layer + 1)
                pe.wait_ge(S["norm_done"], 4 * (2 * layer + 1))
                for e in range(NE):
                    if e % 2 == 0 and e >= 4:
                        pe.wait_ge(S["gb_out"], 8 * layer + e // 2 - 1)
                    ins = mm(b2(4 + (e // 2) % 2)[:, e % 2, :], bc(ident[0:NE, e:e + 1], NE, P), gT[0:NE, :],
                             start=True, stop=True)
                    if e % 2:
                        ins.then_inc(S["gb_done"], 1)
                pe.wait_ge(S["gb_out"], 8 * layer + 8)
                first = MOE_AT[layer]

                with pe.Fori(0, NE // 2) as it:
                    def unit(e2, half):
                        if half == 0:
                            for k in range(2):
                                n = first + 3 * e2 + k
                                pe.wait_ge(landed[n % RING], it * 16 + 16 * (n // RING + 1))
                        u = 2 * e2 + half
                        n = 32 * layer + u
                        pe.wait_ge(S["prod_done"], it * 4 + (n + 1))
                        for g in range(2):
                            s = ring[:, (first + 3 * e2 + g) % RING, :].rearrange("p (c n) -> p c n", c=DC)
                            for k in range(DC):
                                ins = mm(b2(4 + half)[:, g, :], s[:, k, half * P:(half + 1) * P], hT[:, k, :],
                                         start=(k == 0), stop=(k == DC - 1))
                        ins.then_inc(S["unit_done"], 1)

                    def down(e2, half):
                        n = first + 3 * e2 + 2
                        if half == 0:
                            pe.wait_ge(landed[n % RING], it * 16 + 16 * (n // RING + 1))
                        s = ring[:, n % RING, :].rearrange("p (c n) -> p c n", c=2)
                        pe.wait_ge(S["he_done"], it * 4 + (32 * layer + 2 * e2 + half + 3))
                        for m in range(DC):
                            ins = mm(b2(m // 2)[:, m % 2, :], s[:, half, m * P:(m + 1) * P], he[:, e2, half, :],
                                     start=False, stop=True, skip_group_check=True)
                        return ins

                    for e2 in range(2):
                        unit(e2, 0)
                        unit(e2, 1)
                        if layer == 0:
                            for m in ((0,), (1, 2))[e2]:
                                pe.wait_ge(mlanded[m], it * 16 + 16 * 9)
                                ms = mring[:, m, :].rearrange("p (c n) -> p c n", c=DC)
                                for a in range(2):
                                    for k in range(DC):
                                        ins = mm(bank[:, 7, bass.ds(it * 6 + (64 + 2 * m + a), 1)],
                                                 ms[:, k, a * P:(a + 1) * P], c_col[:, 1, k:k + 1],
                                                 start=(k == 0), stop=(k == DC - 1))
                                ins.then_inc(mused, 1)
                        down(e2, 0)
                        down(e2, 1).then_inc(used, 3)

            norm(0)
            moe(0)
            norm(1)

            pe.wait_ge(S["h_ready"], 24)
            for g in range(2):
                for k in range(DC):
                    ins = mm(bank[0:MH, 6, g * TOK:(g + 1) * TOK], mg_w[:, k, g * MH:(g + 1) * MH], hT[:, k, :],
                             start=(k == 0), stop=(k == DC - 1))
            ins.then_inc(S["mgate_done"], 1)
            pe.wait_ge(S["r_done"], 16)
            for j in range(16):
                if j == 2:
                    pe.wait_ge(S["mrow_done"], 1)
                    for t in range(TT):
                        ins = pe.transpose(bank[:, 6, t * MH:(t + 1) * MH], mrow[0:MH, 7, t * P:(t + 1) * P],
                                           ident[0:MH, 0:MH])
                    ins.then_inc(S["mcol_turned"], 1)
                if 4 <= j < 12:
                    pe.wait_ge(S["conv_done"], 2 * (j - 4) + 2)
                elif j >= 12:
                    pe.wait_ge(S["proj_out"], 8 + j - 12 + 1)
                if 8 <= j < 12:
                    by_token(ML_IN + j, j % 4)
                else:
                    by_feature(ML_IN + j, j % 4, hT)
            pe.wait_ge(S["proj_out"], 16)
            pe.wait_ge(S["qk_done"], 16)
            pe.wait_ge(S["mcol_done"], 1)
            pe.wait_ge(S["norm_done"], 8)

            def scores(hd):
                q = hd % 2
                if hd >= 2:
                    pe.wait_ge(S["md_done"], 2 * (hd - 1))
                pick = bc(ident[0:MH, hd:hd + 1], MH, P)
                o = bank[:, q, :]
                mm(o[:, 0:TOK], pick, mrow[0:MH, 8, :], start=True, stop=True, skip_group_check=True)
                mm(o[:, 0:P], ident16[:, :], future16[:, :], start=False, stop=True, skip_group_check=True)
                mm(o[:, TOK:384], pick, mrow[0:MH, 8, P:TOK], start=False, stop=True, skip_group_check=True)
                mm(o[:, TOK:384], ident16[:, :], future16[:, :], start=False, stop=True, skip_group_check=True
                   ).then_inc(S["mb_done"], 1)
                if hd >= 2:
                    pe.wait_ge(S["ms_done"], hd - 1)
                o = bank[:, 2 + q, :]
                mm(o[:, 0:TOK], qkT[:, MH + hd, 0:P], qkT[:, hd, :], start=True, stop=True)
                mm(o[:, TOK:384], qkT[:, MH + hd, P:TOK], qkT[:, hd, P:TOK], start=True, stop=True
                   ).then_inc(S["mqk_done"], 1)

            def values(hd):
                q = hd % 2
                if hd >= 2:
                    pe.wait_ge(S["mh_done"], hd - 1)
                pe.wait_ge(S["ms_done"], hd + 1)
                for i in range(2):
                    o = b2(4 + q)[:, i, :]
                    w = [vM[:, t, hd * P:(hd + 1) * P] if i == 0 else ones[:, :] for t in range(TT)]
                    mm(o[:, 0:TOK], w[0], sM[:, q, 0:TOK], start=True, stop=True)
                    ins = mm(o[:, P:TOK], w[1], sM[:, q, TOK:384], start=False, stop=True,
                             skip_group_check=True)
                ins.then_inc(S["mnum_done"], 1)

            for hd in range(MH):
                scores(hd)
                if hd:
                    pe.wait_ge(S["mfl_done"], 2 * hd)
                mm(bank[:, 6, 0:TOK], bc(ident[0:MH, hd:hd + 1], MH, P), mrow[0:MH, 9, :], start=True, stop=True
                   ).then_inc(S["mfl_done"], 1)
                if hd:
                    values(hd - 1)
            values(MH - 1)
            for b in range(4):
                pe.wait_ge(S["hsq_done"], 2 + b + 1)
                mm(bank[:, b, :], head_w[:, :], qkT[:, 2 * b:2 * b + 2, :].rearrange("p a t -> p (a t)"),
                   start=True, stop=True).then_inc(S["hms_done"], 1)
            pe.wait_ge(S["hstd_done"], 6)
            pe.wait_ge(S["yb_done"], 12)
            for j in range(4):
                by_feature(ML_OUT + j, j, yT)
            norm(2)
            moe(1)
            norm(3)
            pe.wait_ge(S["h_ready"], 40)
            for b in range(4):
                t = b // 2
                for k in range(4):
                    ch = 4 * (b % 2) + k
                    ins = pe.transpose(bank[:, b, k * P:(k + 1) * P], hT[:, ch, t * P:(t + 1) * P], ident[:, :])
                ins.then_inc(S["final_turned"], 1)


EPS_H = 1e-6
EPS_LN = 1e-5

_INS = ["x", "c", "router_w", "router_bias", "ada_w", "ada_b", "ln1_g", "ln1_b", "ln2_g", "ln2_b",
        "moe_w_gate", "moe_w_up", "moe_w_down", "ab_w_in", "s5_lam_re", "s5_lam_im", "s5_log_dt",
        "s5_b_re", "s5_b_im", "s5_c_re", "s5_c_im", "s5_d", "s5_glu_w", "s5_glu_b",
        "gla_gate_w", "gla_gate_b", "gla_norm_g", "ab_w_out", "ml_w_in", "ml_conv_w", "ml_conv_b",
        "ml_igate_b", "ml_fgate_b", "ml_norm_g", "ml_w_out"]


def kernel(**inputs):
    import concourse.bacc as _bacc
    from concourse.bass_utils import run_bass_kernel_spmd as _run

    nc = _bacc.Bacc("TRN2", target_bir_lowering=False, num_devices=1)
    arrays, args = {}, []
    for name in _INS:
        a = np.ascontiguousarray(inputs[name])
        arrays[f"in_{name}_dram"] = a
        args.append(nc.dram_tensor(f"in_{name}_dram", a.shape, mybir.dt.from_np(a.dtype),
                                   kind="ExternalInput").ap())
    args.append(nc.dram_tensor("out_dram", (1, TOK, D), F32, kind="ExternalOutput").ap())
    trunk(nc, *args)
    r = _run(nc, [arrays], core_ids=[0])
    return r.results[0]["out_dram"]
```

```python
from contextlib import ExitStack

import numpy as np

import concourse.bass as bass
from concourse import mybir

F32 = mybir.dt.float32
F32R = mybir.dt.float32r
BF16 = mybir.dt.bfloat16
I32 = mybir.dt.int32
ALU = mybir.AluOpType
ACT = mybir.ActivationFunctionType
AX = mybir.AxisListType

P = 128
TOK = 256
TT = TOK // P
D = 1024
DC = D // P
DEPTH = 2
ALPHA = (2.0 * DEPTH) ** 0.25
S5_W, S5_G, S5_N = 512, 16, 64
UC = S5_W // P
ST = (S5_W // S5_G) * S5_N // P
GH, GDV, GDK = 4, 128, 64
QC = GH * GDK // P
RANK = 16
GATE_NORM = 16.0
AB_LR = S5_W + 2 * GH * GDK + 2 * GH * GDV
MH = 8
CW = 4
NE, NG, EG, DE = 16, 4, 4, 256
SLOT = 2048
SC = SLOT // DC
RING = 6
MRING = 3
LEVELS = 8
TABLE_DVE = 11
BIG = 1.0e30
ROUND = 12582912.0
TWO_PI = (6.28125, 0.0019350051879882812, 3.019916050e-07)
PI_BELOW = 3.1415925

LN_G1, LN_B1, LN_G2, LN_B2, V_D, V_GLUB, V_GATEB, V_GNORM, V_CONVB, V_MNORM, V_END = (
    0, 16, 32, 48, 64, 68, 72, 74, 78, 94, 102)
SH1, SC1, G1, SH2, SC2, G2 = range(6)


def trunk(nc, x, c, router_w, router_bias, ada_w, ada_b, ln1_g, ln1_b, ln2_g, ln2_b,
          moe_w_gate, moe_w_up, moe_w_down, ab_w_in, s5_lam_re, s5_lam_im, s5_log_dt,
          s5_b_re, s5_b_im, s5_c_re, s5_c_im, s5_d, s5_glu_w, s5_glu_b,
          gla_gate_w, gla_gate_b, gla_norm_g, ab_w_out, ml_w_in, ml_conv_w, ml_conv_b,
          ml_igate_b, ml_fgate_b, ml_norm_g, ml_w_out, out):
    with ExitStack() as ctx:
        def sb(name, shape, dt=F32):
            return ctx.enter_context(nc.sbuf_tensor(name, shape, dt))

        def sem(name):
            return ctx.enter_context(nc.semaphore(name))

        bank = ctx.enter_context(nc.psum_tensor("bank", [P, 8, 512], F32))
        ring = sb("ring", [P, RING, SLOT])
        mring = sb("mring", [P, MRING, SLOT])
        hT = sb("hT", [P, DC, TOK])
        axT = sb("axT", [P, DC, TOK])
        wide = sb("wide", [P, 2, DC, TOK])
        rT = wide[:, 0, :, :]
        sqT = wide[:, 1, :, :]
        gsel = wide[0:NE, :, :, :].rearrange("p a c t -> p (a c) t")
        std = sb("std", [P, 2, TOK])
        ident = sb("ident", [P, P])
        mean_w = sb("mean_w", [P, P])
        head_w = sb("head_w", [P, P])
        ones = sb("ones", [P, P])
        zero16 = sb("zero16", [P, 512], BF16)
        ident16 = sb("ident16", [P, P], BF16)
        future16 = sb("future16", [P, P], BF16)
        level_mask = sb("level_mask", [P, LEVELS, P], I32)
        rows = sb("rows", [P, 3, P])
        cols = sb("cols", [P, 3, P])
        mod = sb("mod", [P, DEPTH, 48])
        coef = sb("coef", [P, 4, 4, DC])
        c_col = sb("c_col", [P, 2, DC])
        router_sb = sb("router_sb", [P, DC, NE])
        rbias = sb("rbias", [P, NE])
        lr_w = sb("lr_w", [P, DC, RANK])
        gate_w = sb("gate_w", [RANK, GH * GDK])
        mg_w = sb("mg_w", [P, DC, 2 * MH])
        mg_b = sb("mg_b", [MH, 2])
        macc = sb("macc", [P, MRING, SC])
        s5dt = sb("s5dt", [16, 2, 2])
        s5c = sb("s5c", [P, 5, ST])
        with nc.sbuf_tensor("arena", [P, 20224], F32) as arena_:
            arena = arena_
        whi = sb("whi", [P, 3, SLOT], F32R)
        wlo = sb("wlo", [P, 3, SLOT], F32R)
        hhi = sb("hhi", [P, DC, TOK], F32R)
        hlo = sb("hlo", [P, DC, TOK], F32R)
        ehi = sb("ehi", [P, 2, 2, TOK], F32R)
        elo = sb("elo", [P, 2, 2, TOK], F32R)
        sil = sb("sil", [P, 2, TOK])
        pr = sb("pr", [P, 2, TOK])
        ef = sb("ef", [P, 2, TOK])
        rt = sb("rt", [P, 14, 32])
        pair6 = sb("pair6", [P, TT * NG, 6])
        pairs = sb("pairs", [P, 2, 2, NE, EG])
        gT = sb("gT", [NE, TOK])
        affT = sb("affT", [NE, TOK])

        def view(at, *shape):
            n = int(np.prod(shape))
            v = arena[:, at:at + n]
            if len(shape) == 1:
                return v
            names = "abcd"[:len(shape)]
            return v.rearrange(f"p ({' '.join(names)}) -> p {' '.join(names)}",
                               **dict(zip(names[1:], shape[1:])))

        cosT = view(0, ST, TOK)
        sinT = view(4096, ST, TOK)
        uT = view(8192, UC, TOK)
        rot = view(9216, 2, 2, 2, TOK)
        vin = view(11264, 2, 2, TOK)
        zst = view(12288, 2, TOK)
        sst = view(12800, 2, 2, TOK)
        bbT = view(13824, 2, UC, P)
        ctT = view(14848, 2, ST, 32)
        qT = view(15872, QC, TOK)
        kT = view(16384, QC, TOK)
        vS = view(16896, TT, GH * GDV)
        rS = view(17920, GH, TOK)
        cum = std[:, :, :]
        kd = view(18944, 2, QC, TOK)
        qd = rT[:, 0:4, :].rearrange("p (a c) t -> p a c t", a=2)
        rotp = rT[:, 4:8, :].rearrange("p (a c) t -> p a c t", a=2)
        attD = view(0, 2, 2, 2, P)
        attX = view(1024, 2, 2, P)
        dif = view(1536, 2, QC, TOK)
        dec = view(2560, 2, QC, TOK)
        oT = view(3584, GH, TOK)
        zT = view(8192, UC, TOK)
        yy = view(4608, UC, TOK)
        sgT = view(5632, UC, TOK)
        b_raw = view(15872, 2, ST, S5_G)
        bb = view(16384, 2, ST, 32)
        bt = view(17408, 4, ST, S5_G)
        c_raw = view(18432, 2, UC, P)
        en = view(19968, 3, 2, ST)
        en2 = view(20064, 3, 2, ST)
        tmp_dve = view(9216, TABLE_DVE, P)
        tmp_pool = view(12800, ST - TABLE_DVE, P)
        s5p = view(11264, 16, P)[0:16]
        qkT = view(0, 2 * MH, TOK)
        vM = view(4096, TT, D)
        oG = view(6144, MH, TOK)
        hh = view(8192, MH, TOK)
        cv = view(10240, 2, 2, TOK)
        dM = view(11264, 2, 384)
        eM = view(12032, 2, 384)
        sM = view(12800, 2, 384)
        fl = view(13568, 2, TOK)
        dn = view(14080, 2, TOK)
        mrow = view(14592, 12, TOK)
        ccol = view(17664, TT, MH)

        yT = sqT

        landed = [sem(f"weights_landed{i}") for i in range(RING)]
        used = sem("weights_used")
        gu_used = sem("gate_up_split")
        d_used = sem("down_split")
        mlanded = [sem(f"mod_weights_landed{i}") for i in range(MRING)]
        mused = sem("mod_weights_used")
        names = """x_loaded c_loaded rows_loaded s5_loaded bc_loaded small_loaded stored
        pool_const x_turned xT_ready c_ready cols_turned cols_ready s5_turned s5c_ready
        bb_done bb_turned ct_turned bbT_ready ct_ready tables_ready
        dve_step act_step pool_step
        mod_ready macc_step tables_done h_ready ax_ready coef_ready
        lr_done lr_copied gate_done gate_x gate_abs gate_ln
        proj_out bu_done rot1_done vin_done scan_done rot2_done sst_done
        ys_done yy_done z_done glu_done glu_sig ya_done
        cum_done dif_done dec_done kq_done att_done att_out av_done av_out hsq_done hms_done
        hstd_done yb_done r_done mean_done cen_done sq_done var_done std_done norm_done
        logit_done aff_done aff_turned gates_done gt_turned gt_copied gsel_done gb_done
        hhi_done hlo_done whi_done wlo_done wlod_done block_done
        sil_done prod_done ef_done ehi_done he_done mcol_out
        mgate_done mgate_x mgate_ln mrow_done mcol_turned mcol_done conv_a conv_done qk_done
        mb_done md_done me_done mqk_done ms_done mnum_done mfl_done mh_done
        final_x final_turned final_out""".split()
        S = {n: sem(n) for n in names}

        def bc(ap, *shape):
            return ap.broadcast_to(list(shape)) if hasattr(ap, "broadcast_to") else ap.to_broadcast(list(shape))

        def mcol(layer, part, ch=0):
            at = 8 * part + ch
            return mod[:, layer, at:at + 1]

        def vcol(row):
            return cols[:, 1, row:row + 1]

        def b2(i, half=None):
            return bank[:, i, :].rearrange("p (a t) -> p a t", a=2)

        def doubling(eng, link, j0, j1, e, tmp):
            n_t = j1 - j0
            tt = eng.tensor_tensor
            eng.memset(cosT[:, j0:j1, 0:1], 1.0)
            eng.memset(sinT[:, j0:j1, 0:1], 0.0)
            e = e[:, :, :, j0:j1]
            link(eng.tensor_copy(e[:, 0, :, :], s5c[:, 1:3, j0:j1]))
            n = 1
            while n < TOK:
                c_n = bc(e[:, 0, 0, :].rearrange("p (j a) -> p j a", a=1), P, n_t, n)
                s_n = bc(e[:, 0, 1, :].rearrange("p (j a) -> p j a", a=1), P, n_t, n)
                tm = tmp[:, :, 0:n]
                cn, sn = cosT[:, j0:j1, 0:n], sinT[:, j0:j1, 0:n]
                c2, s2 = cosT[:, j0:j1, n:2 * n], sinT[:, j0:j1, n:2 * n]
                tt(c2, cn, c_n, ALU.mult)
                link(tt(tm, sn, s_n, ALU.mult))
                link(tt(c2, c2, tm, ALU.subtract))
                tt(s2, sn, c_n, ALU.mult)
                link(tt(tm, cn, s_n, ALU.mult))
                link(tt(s2, s2, tm, ALU.add))
                tt(e[:, 1, :, :], e[:, 0, :, :], e[:, 0, :, :], ALU.mult)
                link(tt(e[:, 2, 1, :], e[:, 0, 0, :], e[:, 0, 1, :], ALU.mult))
                tt(e[:, 0, 0, :], e[:, 1, 0, :], e[:, 1, 1, :], ALU.subtract)
                link(tt(e[:, 0, 1, :], e[:, 2, 1, :], e[:, 2, 1, :], ALU.add))
                n *= 2

        def block_part(parts, first, i, g):
            if i < 2:
                dst = parts[:, i, g * D:(g + 1) * D].rearrange("p (c n) -> p c n", c=DC)
                src = ring[:, (first + g) % RING, :].rearrange("p (c n) -> p c n", c=DC)[:, :, i * P:(i + 1) * P]
            else:
                dst = parts[:, 2, g * D:(g + 1) * D]
                src = ring[:, (first + 2) % RING, g * D:(g + 1) * D]
            return dst, src

        block = ctx.enter_context(nc.Block())

        AB_U, AB_Q, AB_K, AB_V, AB_R, AB_GLU, AB_OUT = 0, 2, 3, 4, 6, 8, 9
        MOE0 = AB_OUT + 4
        ML_IN = MOE0 + 3 * NE
        ML_OUT = ML_IN + 16
        MOE1 = ML_OUT + 4
        MOE_AT = (MOE0, MOE1)

        def used_at(n):
            return n if n < ML_IN else n - 3 * NE


        @block.sync
        def _(sp):
            sp.dma_start(sqT[:, :, :].rearrange("p (a b) t -> p a (b t)", a=TT),
                         x[0].rearrange("(a p) d -> p a d", p=P)).then_inc(S["x_loaded"], 16)

            def refill(n):
                old = n - RING
                if 0 <= old < MOE0:
                    sp.wait_ge(used, old + 1)
                elif MOE0 <= old < ML_IN:
                    e, k = divmod(old - MOE0, 3)
                    sp.wait_ge(d_used if k == 2 else gu_used, e + 1)
                elif ML_IN <= old < MOE1:
                    sp.wait_ge(used, MOE0 + old - ML_IN + 1)

            def load(n, src, split=DC):
                refill(n)
                dst = ring[:, n % RING, :].rearrange("p (c n) -> p c n", c=split)
                sp.dma_start(dst, src).then_inc(landed[n % RING], 16)

            def load_cols(n, w, j):
                load(n, w[:, j * SC:(j + 1) * SC].rearrange("(c p) n -> p c n", p=P))

            def load_mod(n, layer, j):
                if n >= MRING:
                    sp.wait_ge(mused, n + 1 - MRING)
                sp.dma_start(mring[:, n % MRING, :].rearrange("p (c n) -> p c n", c=DC),
                             ada_w[layer, :, j * SC:(j + 1) * SC].rearrange("(p c) n -> p c n", c=DC)
                             ).then_inc(mlanded[n % MRING], 16)

            for j in range(8):
                load_mod(j, 0, j)
            for j in range(8):
                load_cols(AB_U + j, ab_w_in[0], j)
            load(AB_GLU, s5_glu_w[0].rearrange("(c p) n -> p c n", p=P), UC)
            for j in range(8, 24):
                load_mod(j, 0, j)
            for j in range(4):
                load_cols(AB_OUT + j, ab_w_out[0], j)

            def experts(layer):
                first = MOE_AT[layer]

                def two(it):
                    for e2 in range(2):
                        for k in range(3):
                            j = 3 * e2 + k
                            n = first + j
                            slot = n % RING
                            w = (moe_w_gate, moe_w_up, moe_w_down)[k][layer]
                            src = w[bass.ds(it * 2 + e2, 1), :, :]
                            if isinstance(it, int):
                                refill(n)
                            else:
                                sp.wait_ge(d_used if k == 2 else gu_used, it * 2 + (NE * layer + e2 - 1))
                            if k < 2:
                                src = src.rearrange("e (c p) n -> p (e c) n", p=P)
                                dst = ring[:, slot, :].rearrange("p (c n) -> p c n", c=DC)
                            else:
                                src = src.rearrange("e (c p) n -> p (e c) n", p=P)
                                dst = ring[:, slot, :].rearrange("p (c n) -> p c n", c=2)
                            sp.dma_start(dst, src).then_inc(landed[slot], 16)
                            if layer == 0 and j % 2 == 1:
                                m = j // 2
                                sp.wait_ge(mused, it * MRING + (24 + m + 1 - MRING))
                                sp.dma_start(
                                    mring[:, m, :].rearrange("p (c n) -> p c n", c=DC),
                                    ada_w[1, :, bass.ds(it * (MRING * SC) + m * SC, SC)].rearrange(
                                        "(p c) n -> p c n", c=DC)).then_inc(mlanded[m], 16)

                two(0)
                with sp.Fori(1, NE // 2) as it:
                    two(it)

            experts(0)
            for j in range(16):
                load_cols(ML_IN + j, ml_w_in[0], j)
            for j in range(4):
                load_cols(ML_OUT + j, ml_w_out[0], j)
            experts(1)
            for b in range(4):
                sp.wait_ge(S["final_out"], b + 1)
                sp.dma_start(out[0].rearrange("(a p) d -> p a d", p=P)[:, b // 2, (b % 2) * 512:(b % 2) * 512 + 512],
                             sqT[:, :, :].rearrange("p (b c) t -> p b (c t)", b=4)[:, b, :]).then_inc(S["stored"], 16)
            sp.wait_ge(S["stored"], 64)

        @block.gpsimd
        def _(pool):
            step = [0]

            def link(ins):
                step[0] += 1
                ins.then_inc(S["pool_step"], 1)
                pool.wait_ge(S["pool_step"], step[0])

            link(pool.memset(ident[:, :], 0.0))
            link(pool.affine_select(out=ident[:, :], in_=ident[:, :], compare_op=ALU.not_equal, fill=1.0,
                                    base=0, pattern=[[-1, P]], channel_multiplier=1))
            pool.memset(mean_w[:, :], 1.0 / D)
            pool.memset(head_w[:, :], 1.0 / P)
            pool.memset(ones[:, :], 1.0)
            pool.memset(zero16[:, :], 0.0)
            pool.memset(future16[:, :], 0.0)
            link(pool.tensor_copy(ident16[:, :], ident[:, :]))
            link(pool.memset(future16[:, :], 0.0))
            pool.affine_select(out=future16[:, :], in_=future16[:, :], compare_op=ALU.is_ge, fill=BIG,
                               base=0, pattern=[[1, P]], channel_multiplier=-1)
            link(pool.memset(level_mask[:, :, :], 0))
            for lv in range(LEVELS - 1):
                h = 1 << lv
                m = level_mask[:, lv, :].rearrange("p (n two h) -> p n two h", two=2, h=h)[:, :, 1, :]
                link(pool.memset(m, 1))
                link(pool.affine_select(out=m, in_=m, compare_op=ALU.is_ge, fill=0.0, base=0,
                                        pattern=[[-2 * h, P // (2 * h)], [0, h]], channel_multiplier=1))
                link(pool.affine_select(out=m, in_=m, compare_op=ALU.is_ge, fill=0.0, base=h - 1,
                                        pattern=[[2 * h, P // (2 * h)], [0, h]], channel_multiplier=-1))
            pool.tensor_copy(level_mask[:, LEVELS - 1, :], ident[:, :]).then_inc(S["pool_const"], 1)

            pool.wait_ge(S["xT_ready"], 4)
            for ch in range(DC):
                pool.tensor_scalar(axT[:, ch, :], rT[:, ch, :], ALPHA, None, ALU.mult).then_inc(S["ax_ready"], 1)

            pool.wait_ge(S["s5c_ready"], 1)
            doubling(pool, link, TABLE_DVE, ST, en2, tmp_pool)
            pool.nop().then_inc(S["tables_done"], 1)

            def rotate_in(j):
                pool.wait_ge(S["rot1_done"], 2 * j + 2)
                if j >= 2:
                    pool.wait_ge(S["scan_done"], 2 * (j - 1))
                q = j % 2
                pool.tensor_tensor(vin[:, q, 0, :], rot[:, q, 0, 0, :], rot[:, q, 1, 1, :], ALU.add)
                pool.tensor_tensor(vin[:, q, 1, :], rot[:, q, 0, 1, :], rot[:, q, 1, 0, :],
                                   ALU.subtract).then_inc(S["vin_done"], 1)

            def rotate_out(j):
                pool.wait_ge(S["rot2_done"], 2 * j + 2)
                if j >= 2:
                    pool.wait_ge(S["ys_done"], j - 1)
                q = j % 2
                pool.tensor_tensor(sst[:, q, 0, :], rotp[:, 0, 0, :], rotp[:, 1, 1, :], ALU.subtract)
                pool.tensor_tensor(sst[:, q, 1, :], rotp[:, 0, 1, :], rotp[:, 1, 0, :],
                                   ALU.add).then_inc(S["sst_done"], 1)

            for j in range(ST + 1):
                if j < ST:
                    rotate_in(j)
                if j >= 1:
                    rotate_out(j - 1)

            pool.memset(kd[:, :, :, :], 0.0)
            link(pool.memset(qd[:, :, :, :], 0.0))
            pool.wait_ge(S["proj_out"], 4)
            for lv in range(LEVELS):
                h = 1 << lv
                q = lv % 2
                pool.wait_ge(S["dec_done"], 2 * lv + 2)
                if lv >= 2:
                    pool.wait_ge(S["att_done"], 2 * (lv - 1))
                k5 = kT.rearrange("p c (n two h) -> p (c n) two h", two=2, h=h)[:, :, 0, :]
                q5 = qT.rearrange("p c (n two h) -> p (c n) two h", two=2, h=h)[:, :, 1, :]
                d5 = dec[:, q, :, :].rearrange("p c (n two h) -> p (c n) two h", two=2, h=h)
                ko = kd[:, q, :, :].rearrange("p c (n two h) -> p (c n) two h", two=2, h=h)[:, :, 0, :]
                qo = qd[:, q, :, :].rearrange("p c (n two h) -> p (c n) two h", two=2, h=h)[:, :, 1, :]
                pool.tensor_tensor(ko, k5, d5[:, :, 0, :], ALU.mult)
                pool.tensor_tensor(qo, q5, d5[:, :, 1, :], ALU.mult).then_inc(S["kq_done"], 1)

            def axes(i):
                for b in range(4):
                    pool.wait_ge(S["norm_done"], 4 * i + b + 1)
                    if b == 0:
                        pool.wait_ge(S["coef_ready"], i + 1)
                    for ch in (2 * b, 2 * b + 1):
                        pool.tensor_scalar(axT[:, ch, :], rT[:, ch, :], coef[:, i, 2, ch:ch + 1],
                                           coef[:, i, 3, ch:ch + 1], ALU.mult, ALU.add).then_inc(S["ax_ready"], 1)

            def moe(layer):
                with pool.Fori(0, NE // 2) as it:
                    for e2 in range(2):
                        n = MOE_AT[layer] + 3 * e2 + 2
                        for half in range(2):
                            at = slice(half * D, half * D + D)
                            pool.wait_ge(S["whi_done"], it * 12 + (6 * (NE * layer + e2) + 5 + half))
                            ins = pool.tensor_tensor(wlo[:, 2, at], ring[:, n % RING, at], whi[:, 2, at].bitcast(F32),
                                                     ALU.subtract)
                            ins.then_inc(S["wlod_done"], 1)
                        pool.wait_ge(S["wlod_done"], it * 4 + (2 * (NE * layer + e2) + 2))
                        pool.nop().then_inc(d_used, 1)

            axes(0)
            moe(0)
            axes(1)
            axes(2)
            moe(1)

        @block.scalar
        def _(act):
            step = [0]

            def link(ins):
                step[0] += 1
                ins.then_inc(S["act_step"], 1)
                act.wait_ge(S["act_step"], step[0])

            act.dma_start(c_col[:, 0, :], c.rearrange("b (p c) -> (b p) c", c=DC)).then_inc(S["c_loaded"], 16)
            lam = lambda a: a[0].rearrange("(j g) p -> j g p", g=2)
            for i, a in enumerate((s5_lam_re, s5_lam_im)):
                act.dma_start(s5p[:, i, :].rearrange("j (g p) -> j g p", g=2), lam(a)).then_inc(S["s5_loaded"], 16)
            act.dma_start(s5dt[:, 0, :], s5_log_dt[0].rearrange("(j g) -> j g", g=2)).then_inc(S["s5_loaded"], 16)
            for l in range(DEPTH):
                act.dma_start(rows[48 * l:48 * l + 48, 0, :], ada_b[l].rearrange("(r n) -> r n", n=P)
                              ).then_inc(S["rows_loaded"], 16)
            for a, at in ((ln1_g, LN_G1), (ln1_b, LN_B1), (ln2_g, LN_G2), (ln2_b, LN_B2)):
                act.dma_start(rows[at:at + 16, 1, :], a.rearrange("l (r n) -> (l r) n", n=P)
                              ).then_inc(S["rows_loaded"], 16)
            for a, at, n in ((s5_d, V_D, 4), (s5_glu_b, V_GLUB, 4), (gla_gate_b, V_GATEB, 2),
                             (gla_norm_g, V_GNORM, 4), (ml_conv_b, V_CONVB, 16), (ml_norm_g, V_MNORM, 8)):
                act.dma_start(rows[at:at + n, 1, :], a[0].rearrange("(r n) -> r n", n=P)
                              ).then_inc(S["rows_loaded"], 16)
            act.dma_start(rows[0:64, 2, :], ml_conv_w[0].rearrange("j (r n) -> (j r) n", n=P)
                          ).then_inc(S["rows_loaded"], 16)
            for i, a in enumerate((s5_b_re, s5_b_im)):
                act.dma_start(b_raw[:, i, :, :], a[0].rearrange("(j g) p c -> (g p) j c", g=2)
                              ).then_inc(S["bc_loaded"], 16)
            for i, a in enumerate((s5_c_re, s5_c_im)):
                for h in range(2):
                    act.dma_start(c_raw[:, i, :, h * 64:h * 64 + 64],
                                  a[0].rearrange("(k g) c p -> (g c) k p", g=8)).then_inc(S["bc_loaded"], 16)
            act.dma_start(lr_w[:, :, :], ab_w_in[0, :, AB_LR:AB_LR + RANK].rearrange("(c p) n -> p c n", p=P)
                          ).then_inc(S["small_loaded"], 16)
            act.dma_start(gate_w[:, :], gla_gate_w[0]).then_inc(S["small_loaded"], 16)
            act.dma_start(router_sb[:, :, :], router_w.rearrange("(c p) n -> p c n", p=P)
                          ).then_inc(S["small_loaded"], 16)
            act.dma_start(rbias[:, :], router_bias.rearrange("(a n) -> a n", a=1).to_broadcast([P, NE])
                          ).then_inc(S["small_loaded"], 16)
            act.dma_start(mg_w[:, :, :], ml_w_in[0, :, 4 * D:4 * D + 2 * MH].rearrange("(c p) n -> p c n", p=P)
                          ).then_inc(S["small_loaded"], 16)
            act.dma_start(mg_b[:, 0:1], ml_igate_b[0].rearrange("(h a) -> h a", a=1)).then_inc(S["small_loaded"], 16)
            act.dma_start(mg_b[:, 1:2], ml_fgate_b[0].rearrange("(h a) -> h a", a=1)).then_inc(S["small_loaded"], 16)

            act.wait_ge(S["c_loaded"], 16)
            act.activation(c_col[:, 1, :], c_col[:, 0, :], ACT.Silu).then_inc(S["c_ready"], 1)
            act.wait_ge(S["s5_loaded"], 48)
            act.activation(s5dt[:, 1, :], s5dt[:, 0, :], ACT.Exp).then_inc(S["tables_ready"], 1)
            act.wait_ge(S["tables_ready"], 2)
            act.activation(s5p[:, 4, :], s5p[:, 2, :], ACT.Exp).then_inc(S["tables_ready"], 1)
            act.wait_ge(S["tables_ready"], 4)
            act.activation(s5p[:, 6, :], s5p[:, 3, :], ACT.Sin).then_inc(S["tables_ready"], 1)
            act.activation(s5p[:, 9, :], s5p[:, 3, :], ACT.Sin, scale=0.5).then_inc(S["tables_ready"], 1)
            for b in range(4):
                act.wait_ge(S["x_turned"], b + 1)
                act.activation(rT[:, 2 * b:2 * b + 2, :], b2(b), ACT.Copy).then_inc(S["xT_ready"], 1)

            act.wait_ge(S["mod_ready"], 1)
            act.wait_ge(S["xT_ready"], 4)
            for ch in range(DC):
                act.activation(hT[:, ch, :], rT[:, ch, :], ACT.Identity, scale=mcol(0, SC1, ch),
                               bias=mcol(0, SH1, ch)).then_inc(S["h_ready"], 1)

            act.wait_ge(S["lr_done"], 1)
            act.activation(s5p[0:RANK, 0:2, :], bank[0:RANK, 6, 0:TOK].rearrange("p (a t) -> p a t", a=2),
                           ACT.Copy).then_inc(S["lr_copied"], 1)
            act.wait_ge(S["gate_done"], 1)
            for ch in range(QC):
                act.activation(cum[:, ch, :], b2(5)[:, ch, :], ACT.Identity, bias=vcol(V_GATEB + ch)
                               ).then_inc(S["gate_x"], 1)
            act.wait_ge(S["gate_x"], 2)
            link(act.activation(kd[:, 0, :, :], cum[:, :, :], ACT.Abs))
            link(act.activation(kd[:, 1, :, :], kd[:, 0, :, :], ACT.Exp, scale=-1.0))
            act.activation(kd[:, 0, :, :], kd[:, 1, :, :], ACT.Ln, bias=1.0).then_inc(S["gate_ln"], 1)

            def leave(j):
                act.wait_ge(used, j + 1)
                bk = b2(j % 4)
                if j < 2:
                    ins = act.activation(uT[:, 2 * j:2 * j + 2, :], bk, ACT.Copy)
                elif j == 2:
                    ins = act.activation(qT[:, :, :], bk, ACT.Copy, scale=GDK ** -0.5)
                elif j == 3:
                    ins = act.activation(kT[:, :, :], bk, ACT.Copy)
                elif j < 6:
                    ins = act.activation(vS[:, :, (j - 4) * SC:(j - 3) * SC], bk, ACT.Copy)
                else:
                    ins = act.activation(rS[:, 2 * (j - 6):2 * (j - 6) + 2, :], bk, ACT.Silu)
                ins.then_inc(S["proj_out"], 1)

            for j in range(8):
                leave(j)

            for k in range(UC):
                act.wait_ge(S["yy_done"], k + 1)
                act.activation(zT[:, k, :], yy[:, k, :], ACT.Gelu_apprx_tanh).then_inc(S["z_done"], 1)
            for k in range(UC):
                if k == 0:
                    act.wait_ge(S["glu_done"], 1)
                elif k == 2:
                    act.wait_ge(used, AB_GLU + 1)
                act.activation(sgT[:, k, :], b2(4 + k // 2)[:, k % 2, :], ACT.Sigmoid,
                               bias=vcol(V_GLUB + k)).then_inc(S["glu_sig"], 1)

            for lv in range(LEVELS):
                h = 1 << lv
                q = lv % 2
                act.wait_ge(S["dif_done"], lv + 1)
                if lv >= 2:
                    act.wait_ge(S["kq_done"], lv - 1)
                a5 = dif[:, q, :, :].rearrange("p c (n two h) -> p (c n) two h", two=2, h=h)
                d5 = dec[:, q, :, :].rearrange("p c (n two h) -> p (c n) two h", two=2, h=h)
                for half, sign in ((0, -1.0), (1, 1.0)):
                    act.activation(d5[:, :, half, :], a5[:, :, half, :], ACT.Exp,
                                   scale=sign / GATE_NORM).then_inc(S["dec_done"], 1)
            for b in range(2):
                act.wait_ge(S["av_done"], b + 1)
                act.activation(oT[:, 2 * b:2 * b + 2, :], b2(b), ACT.Copy).then_inc(S["av_out"], 1)
            for b in range(2):
                act.wait_ge(S["av_out"], b + 1)
                act.activation(yy[:, 2 * b:2 * b + 2, :], oT[:, 2 * b:2 * b + 2, :], ACT.Square
                               ).then_inc(S["hsq_done"], 1)
            for b in range(2):
                act.wait_ge(S["hms_done"], b + 1)
                act.activation(sgT[:, 2 * b:2 * b + 2, :], b2(4 + b), ACT.Sqrt, bias=EPS_H
                               ).then_inc(S["hstd_done"], 1)

            def norm(i):
                for b in range(4):
                    act.wait_ge(S["cen_done"], 4 * i + b + 1)
                    act.activation(sqT[:, 2 * b:2 * b + 2, :], rT[:, 2 * b:2 * b + 2, :], ACT.Square
                                   ).then_inc(S["sq_done"], 1)
                act.wait_ge(S["var_done"], i + 1)
                act.activation(std[:, 0, :], bank[:, 5, 0:TOK], ACT.Sqrt, bias=EPS_LN).then_inc(S["std_done"], 1)
                for b in range(4):
                    act.wait_ge(S["norm_done"], 4 * i + b + 1)
                    for ch in (2 * b, 2 * b + 1):
                        act.activation(hT[:, ch, :], rT[:, ch, :], ACT.Identity, scale=coef[:, i, 0, ch:ch + 1],
                                       bias=coef[:, i, 1, ch:ch + 1]).then_inc(S["h_ready"], 1)

            def moe(layer):
                first = MOE_AT[layer]
                for b in range(4):
                    act.wait_ge(S["h_ready"], 8 * (2 * layer + 1) + 2 * b + 2)
                    act.activation(hhi[:, 2 * b:2 * b + 2, :], hT[:, 2 * b:2 * b + 2, :], ACT.Copy
                                   ).then_inc(S["hhi_done"], 1)
                act.wait_ge(S["logit_done"], layer + 1)
                act.activation(affT[:, :], bank[0:NE, 6, 0:TOK], ACT.Sigmoid).then_inc(S["aff_done"], 1)

                def high(it, e2, i):
                    if i == 0:
                        for k in range(2):
                            n = first + 3 * e2 + k
                            act.wait_ge(landed[n % RING], it * 16 + 16 * (n // RING + 1))
                    elif i == 2:
                        n = first + 3 * e2 + 2
                        act.wait_ge(landed[n % RING], it * 16 + 16 * (n // RING + 1))
                    act.wait_ge(S["block_done"], it * 6 + (3 * (NE * layer + e2) + i + 1))
                    for g in range(2):
                        dst, src = block_part(whi, first + 3 * e2, i, g)
                        act.activation(dst, src, ACT.Copy).then_inc(S["whi_done"], 1)

                def halves(it, e2, half):
                    u = 2 * e2 + half
                    n = 32 * layer + u
                    act.wait_ge(S["block_done"], it * 6 + (3 * (NE * layer + e2) + half + 4))
                    act.wait_ge(S["prod_done"], it * 4 + (n + 1))
                    act.activation(sil[:, u % 2, :], bank[:, 4 + u % 2, 0:TOK], ACT.Silu
                                   ).then_inc(S["sil_done"], 1)
                    return n

                def part(it, e2, half):
                    n = 32 * layer + 2 * e2 + half
                    act.wait_ge(S["ef_done"], it * 4 + (n + 3))
                    act.wait_ge(S["block_done"], it * 6 + (3 * (NE * layer + e2) + 2))
                    act.activation(ehi[:, e2, half, :], ef[:, half, :], ACT.Copy).then_inc(S["ehi_done"], 1)

                def two(it, last=False):
                    for e2 in range(2):
                        halves(it, e2, 0)
                        part(it, e2, 0)
                        high(it, e2, 2)
                        if e2 == 0:
                            high(it, 1, 0)
                        elif not last:
                            high(it + 1, 0, 0)
                        halves(it, e2, 1)
                        part(it, e2, 1)
                        if e2 == 0:
                            high(it, 1, 1)
                        elif not last:
                            high(it + 1, 0, 1)

                high(0, 0, 0)
                high(0, 0, 1)
                act.wait_ge(S["gt_turned"], layer + 1)
                act.activation(gT[:, :], bank[0:NE, 6, 0:TOK], ACT.Copy).then_inc(S["gt_copied"], 1)
                with act.Fori(0, NE // 2 - 1) as it:
                    two(it)
                two(NE // 2 - 1, last=True)

            norm(0)
            moe(0)
            norm(1)

            act.wait_ge(S["mgate_done"], 1)
            for g in range(2):
                act.activation(mrow[0:MH, g, :], bank[0:MH, 6, g * TOK:(g + 1) * TOK], ACT.Identity,
                               bias=mg_b[:, g:g + 1]).then_inc(S["mgate_x"], 1)
            act.wait_ge(S["mgate_x"], 2)
            link(act.activation(mrow[0:MH, 2, :], mrow[0:MH, 1, :], ACT.Abs))
            link(act.activation(mrow[0:MH, 3, :], mrow[0:MH, 2, :], ACT.Exp, scale=-1.0))
            act.activation(mrow[0:MH, 4, :], mrow[0:MH, 3, :], ACT.Ln, bias=1.0).then_inc(S["mgate_ln"], 1)
            for j in range(16):
                act.wait_ge(used, used_at(ML_IN) + j + 1)
                bk = b2(j % 4)
                if j < 8:
                    if j >= 2:
                        act.wait_ge(S["qk_done"], 2 * (j - 1))
                    for a in range(2):
                        m = 2 * j + a
                        act.activation(cv[:, j % 2, a, :], bk[:, a, :], ACT.Identity,
                                       scale=cols[:, 2, 48 + m:49 + m], bias=vcol(V_CONVB + m)
                                       ).then_inc(S["conv_a"], 1)
                    if j >= 1:
                        for a in range(2):
                            m = 2 * (j - 1) + a
                            act.wait_ge(S["conv_done"], m + 1)
                            act.activation(qkT[:, m, :], cv[:, (j - 1) % 2, a, :], ACT.Silu
                                           ).then_inc(S["qk_done"], 1)
                elif j < 12:
                    if j == 8:
                        for a in range(2):
                            m = 14 + a
                            act.wait_ge(S["conv_done"], m + 1)
                            act.activation(qkT[:, m, :], cv[:, 1, a, :], ACT.Silu).then_inc(S["qk_done"], 1)
                    act.activation(vM[:, :, (j - 8) * SC:(j - 7) * SC], bk, ACT.Copy).then_inc(S["proj_out"], 1)
                else:
                    act.activation(oG[:, 2 * (j - 12):2 * (j - 12) + 2, :], bk, ACT.Sigmoid
                                   ).then_inc(S["proj_out"], 1)
            for hd in range(MH):
                q = hd % 2
                act.wait_ge(S["md_done"], 2 * hd + 2)
                if hd >= 2:
                    act.wait_ge(S["ms_done"], hd - 1)
                act.activation(eM[:, q, :], dM[:, q, :], ACT.Exp, scale=-1.0).then_inc(S["me_done"], 1)
                act.wait_ge(S["mfl_done"], 2 * hd + 1)
                if hd >= 2:
                    act.wait_ge(S["mh_done"], hd - 1)
                act.activation(fl[:, q, :], bank[:, 6, 0:TOK], ACT.Exp, scale=-1.0).then_inc(S["mfl_done"], 1)
            for b in range(4):
                act.wait_ge(S["mh_done"], 2 * b + 2)
                act.activation(qkT[:, 2 * b:2 * b + 2, :], hh[:, 2 * b:2 * b + 2, :], ACT.Square
                               ).then_inc(S["hsq_done"], 1)
            for b in range(4):
                act.wait_ge(S["hms_done"], 2 + b + 1)
                act.activation(qkT[:, 8 + 2 * b:10 + 2 * b, :], b2(b), ACT.Sqrt, bias=EPS_H
                               ).then_inc(S["hstd_done"], 1)
            norm(2)
            moe(1)
            norm(3)
            for b in range(4):
                act.wait_ge(S["final_turned"], b + 1)
                act.activation(sqT[:, 2 * b:2 * b + 2, :], b2(b), ACT.Copy).then_inc(S["final_out"], 1)

        @block.vector
        def _(dve):
            step = [0]

            def link(ins):
                step[0] += 1
                ins.then_inc(S["dve_step"], 1)
                dve.wait_ge(S["dve_step"], step[0])

            tt, ts, stt = dve.tensor_tensor, dve.tensor_scalar, dve.scalar_tensor_tensor
            lre, lim, lrd, ang, mag, are, sn, cs, nre, sh, kk, t0, t1, cre, cim, rdn = (
                s5p[:, i, :] for i in range(16))
            dtb = bc(s5dt[:, 1, :].rearrange("j (g a) -> j g a", a=1), 16, 2, 64)
            g2 = lambda a: a.rearrange("j (g p) -> j g p", g=2)

            dve.nop().then_inc(S["prod_done"], 2)
            dve.nop().then_inc(S["he_done"], 2)
            dve.nop().then_inc(S["ef_done"], 2)
            dve.wait_ge(S["tables_ready"], 1)
            tt(g2(lrd), g2(lre), dtb, ALU.mult).then_inc(S["tables_ready"], 1)
            link(tt(g2(ang), g2(lim), dtb, ALU.mult))
            link(ts(kk, ang, 1.0 / (2.0 * np.pi), ROUND, ALU.mult, ALU.add))
            link(ts(kk, kk, ROUND, None, ALU.subtract))
            for part in TWO_PI:
                link(stt(ang, kk, -part, ang, ALU.mult, ALU.add))
            dve.wait_ge(S["tables_ready"], 3)
            ts(ang, ang, PI_BELOW, -PI_BELOW, ALU.min, ALU.max).then_inc(S["tables_ready"], 1)
            dve.wait_ge(S["tables_ready"], 6)
            link(tt(cs, sh, sh, ALU.mult))
            link(ts(cs, cs, -2.0, 1.0, ALU.mult, ALU.add))
            link(tt(are, mag, cs, ALU.mult))
            link(ts(nre, are, 1.0, None, ALU.subtract))
            link(tt(are, mag, sn, ALU.mult))
            link(tt(t0, lre, lre, ALU.mult))
            link(tt(t1, lim, lim, ALU.mult))
            link(tt(t0, t0, t1, ALU.add))
            link(dve.reciprocal(rdn, t0))
            link(tt(t0, nre, lre, ALU.mult))
            link(tt(t1, are, lim, ALU.mult))
            link(tt(t0, t0, t1, ALU.add))
            link(tt(cre, t0, rdn, ALU.mult))
            link(tt(t0, are, lre, ALU.mult))
            link(tt(t1, nre, lim, ALU.mult))
            link(tt(t0, t0, t1, ALU.subtract))
            tt(cim, t0, rdn, ALU.mult).then_inc(S["bb_done"], 1)

            def mod_slot(n, it=None):
                slot = mring[:, n % MRING, :].rearrange("p (c n) -> p c n", c=DC)
                acc = macc[:, n % MRING, :]
                if it is None:
                    dve.wait_ge(mlanded[n % MRING], 16 * (n // MRING + 1))
                    if n >= MRING:
                        dve.wait_ge(S["mcol_out"], n + 1 - MRING)
                else:
                    dve.wait_ge(mlanded[n % MRING], it * 16 + 16 * (n // MRING + 1))
                    dve.wait_ge(S["mcol_out"], it * MRING + (n + 1 - MRING))
                for k in range(DC):
                    if k == 0:
                        ins = ts(acc, slot[:, 0, :], c_col[:, 1, 0:1], None, ALU.mult)
                    else:
                        ins = stt(acc, slot[:, k, :], c_col[:, 1, k:k + 1], acc, ALU.mult, ALU.add)
                    if k == DC - 1:
                        ins.then_inc(mused, 1)
                    else:
                        ins.then_inc(S["macc_step"], 1)
                        count = 7 * n + k + 1
                        dve.wait_ge(S["macc_step"], count if it is None else it * 21 + count)

            def modulation(layer, parts, done):
                dve.wait_ge(S["mcol_out"], done)
                a, b = 8 * parts[0], 8 * parts[-1] + 8
                link(tt(mod[:, layer, a:b], bank[:, 7, 64 * layer + a:64 * layer + b],
                        cols[:, 0, 48 * layer + a:48 * layer + b], ALU.add))
                for q in (SC1, G1, SC2, G2):
                    if q in parts:
                        m = mod[:, layer, 8 * q:8 * q + 8]
                        link(ts(m, m, 1.0, None, ALU.add))

            dve.wait_ge(S["c_ready"], 1)
            for n in range(8):
                mod_slot(n)
            dve.wait_ge(S["cols_turned"], 1)
            dve.tensor_copy(cols[:, 0, 0:96], bank[:, 6, 0:96])
            dve.tensor_copy(cols[:, 1, 0:V_END], bank[:, 6, P:P + V_END])
            dve.tensor_copy(cols[:, 2, 0:64], bank[:, 6, 2 * P:2 * P + 64]).then_inc(S["cols_ready"], 1)
            dve.wait_ge(S["cols_ready"], 1)
            modulation(0, (SH1, SC1), 8)
            dve.nop().then_inc(S["mod_ready"], 1)
            dve.wait_ge(S["s5_turned"], 1)
            dve.tensor_copy(s5c[:, :, :], bank[:, 5, 0:5 * ST].rearrange("p (a j) -> p a j", a=5)
                            ).then_inc(S["s5c_ready"], 1)
            dve.wait_ge(S["s5c_ready"], 1)

            link(dve.memset(bb[:, :, :, :], 0.0))
            dve.wait_ge(S["bc_loaded"], 96)
            coef_b = [bc(s5c[:, 3 + i, :].rearrange("p (j a) -> p j a", a=1), P, ST, S5_G) for i in range(2)]
            for i, (a, b) in enumerate(((0, 0), (1, 1), (0, 1), (1, 0))):
                link(tt(bt[:, i, :, :], b_raw[:, b, :, :], coef_b[a], ALU.mult))
            for i, op in ((0, ALU.subtract), (1, ALU.add)):
                for g in range(2):
                    ps = slice(64 * g, 64 * g + 64)
                    link(tt(bb[ps, i, :, 16 * g:16 * g + 16], bt[ps, 2 * i, :, :], bt[ps, 2 * i + 1, :, :], op))
            dve.nop().then_inc(S["bb_done"], 1)
            link(dve.memset(ctT[:, :, :, :], 0.0))
            for i, sign in ((0, 1.0), (1, -1.0)):
                dve.wait_ge(S["ct_turned"], i + 1)
                for g in range(2):
                    ps = slice(64 * g, 64 * g + 64)
                    src = bank[ps, i, :].rearrange("p (j g c) -> p j g c", g=2, c=16)[:, :, g, :]
                    ins = ts(ctT[ps, i, :, 16 * g:16 * g + 16], src, sign, None, ALU.mult)
                ins.then_inc(S["ct_ready"], 1)
            for i in range(2):
                dve.wait_ge(S["bb_turned"], i + 1)
                dve.tensor_copy(bbT[:, i, :, :], bank[:, 2 + i, :].rearrange("p (k n) -> p k n", k=UC)
                                ).then_inc(S["bbT_ready"], 1)

            doubling(dve, link, 0, TABLE_DVE, en, tmp_dve)

            dve.wait_ge(S["gate_ln"], 1)
            link(stt(cum[:, :, :], cum[:, :, :], 0.0, kd[:, 0, :, :], ALU.min, ALU.subtract))
            dve.wait_ge(S["h_ready"], 8)
            dve.wait_ge(S["ax_ready"], 8)
            for ch in range(QC):
                dve.tensor_tensor_scan(qd[:, 0, ch, :], bc(ones[:, 0:1], P, TOK), cum[:, ch, :], 0.0,
                                       ALU.mult, ALU.add).then_inc(S["cum_done"], 1)
            dve.wait_ge(S["cum_done"], 2)
            link(dve.tensor_copy(cum[:, :, :], qd[:, 0, :, :]))

            def rot1(j):
                dve.wait_ge(S["bu_done"], j + 1)
                if j == TABLE_DVE:
                    dve.wait_ge(S["tables_done"], 1)
                if j >= 2:
                    dve.wait_ge(S["vin_done"], j - 1)
                for i, t in enumerate((cosT, sinT)):
                    tb = bc(t[:, j, :].rearrange("p (a t) -> p a t", a=1), P, 2, TOK)
                    tt(rot[:, j % 2, i, :, :], b2(4 + j % 2), tb, ALU.mult).then_inc(S["rot1_done"], 1)

            def scans(j):
                dve.wait_ge(S["vin_done"], j + 1)
                if j:
                    dve.wait_ge(S["rot2_done"], 2 * j)
                for i in range(2):
                    dve.tensor_tensor_scan(zst[:, i, :], bc(s5c[:, 0, j:j + 1], P, TOK), vin[:, j % 2, i, :],
                                           0.0, ALU.mult, ALU.add).then_inc(S["scan_done"], 1)
                dve.wait_ge(S["scan_done"], 2 * j + 2)
                if j >= 1:
                    dve.wait_ge(S["sst_done"], j)
                for i, t in enumerate((cosT, sinT)):
                    tb = bc(t[:, j, :].rearrange("p (a t) -> p a t", a=1), P, 2, TOK)
                    tt(rotp[:, i, :, :], zst[:, :, :], tb, ALU.mult).then_inc(S["rot2_done"], 1)

            def skip(k):
                dve.wait_ge(S["ys_done"], 4 * k + 4)
                stt(yy[:, k, :], uT[:, k, :], vcol(V_D + k), bank[:, 6, 0:TOK], ALU.mult, ALU.add
                    ).then_inc(S["yy_done"], 1)

            for j in range(ST + 1):
                if j < ST:
                    rot1(j)
                if j >= 1:
                    scans(j - 1)
                    if j - 1 >= 4 and (j - 1) % 4 == 1:
                        skip((j - 1) // 4 - 1)
            skip(UC - 1)

            dve.wait_ge(S["rot2_done"], 2 * ST)
            link(dve.memset(attD[:, :, :, :, :], 0.0))

            def level_dif(lv):
                h = 1 << lv
                if lv >= 2:
                    dve.wait_ge(S["dec_done"], 2 * (lv - 1))
                m5 = cum.rearrange("p c (n h) -> p (c n) h", h=2 * h)
                ref = bc(m5[:, :, h - 1:h], P, QC * TOK // (2 * h), 2 * h)
                o5 = dif[:, lv % 2, :, :].rearrange("p c (n h) -> p (c n) h", h=2 * h)
                tt(o5, m5, ref, ALU.subtract).then_inc(S["dif_done"], 1)

            def level_out(n, lv):
                for par in range(2):
                    dve.wait_ge(S["att_done"], 2 * n + par + 1)
                    if n:
                        dve.wait_ge(S["att_out"], 2 * n + par - 1)
                    src = bank[:, 2 * (n % 2) + par, :].rearrange("p (b t) -> p b t", t=P)
                    if lv == LEVELS - 1 and n < LEVELS:
                        dve.tensor_copy(attX[:, par, :, :], src[:, 0:2, :]).then_inc(S["att_out"], 1)
                    else:
                        mask = bc(level_mask[:, lv, :].rearrange("p (a t) -> p a t", a=1), P, 4, P)
                        dve.copy_predicated(attD[:, par, :, :, :].rearrange("p a b t -> p (a b) t"), mask, src
                                            ).then_inc(S["att_out"], 1)

            level_dif(0)
            for lv in range(LEVELS):
                mod_slot(8 + 2 * lv)
                mod_slot(9 + 2 * lv)
                if lv + 1 < LEVELS:
                    level_dif(lv + 1)
                if lv == 1:
                    for k in range(UC):
                        dve.wait_ge(S["glu_sig"], k + 1)
                        tt(yT[:, k, :], zT[:, k, :], sgT[:, k, :], ALU.mult).then_inc(S["ya_done"], 1)
                level_out(lv, lv)
            level_out(LEVELS, LEVELS - 1)

            modulation(0, (G1, SH2, SC2, G2), 24)

            for b in range(2):
                dve.wait_ge(S["hstd_done"], b + 1)
                link(dve.reciprocal(sgT[:, 2 * b:2 * b + 2, :], sgT[:, 2 * b:2 * b + 2, :]))
                link(tt(oT[:, 2 * b:2 * b + 2, :], oT[:, 2 * b:2 * b + 2, :], sgT[:, 2 * b:2 * b + 2, :], ALU.mult))
                for k in (2 * b, 2 * b + 1):
                    stt(yT[:, UC + k, :], oT[:, k, :], vcol(V_GNORM + k), rS[:, k, :], ALU.mult, ALU.mult
                        ).then_inc(S["yb_done"], 1)

            def norm(i):
                layer, second = i // 2, i % 2
                gain, shift = (LN_G2, LN_B2) if second else (LN_G1, LN_B1)
                gv = cols[:, 1, gain + 8 * layer:gain + 8 * layer + 8]
                bv = cols[:, 1, shift + 8 * layer:shift + 8 * layer + 8]
                if i < 3:
                    nl, sc, sh_ = (layer, SC2, SH2) if not second else (layer + 1, SC1, SH1)
                    scv = mod[:, nl, 8 * sc:8 * sc + 8]
                    link(tt(coef[:, i, 0, :], gv, scv, ALU.mult))
                    link(tt(coef[:, i, 1, :], bv, scv, ALU.mult))
                    link(tt(coef[:, i, 1, :], coef[:, i, 1, :], mod[:, nl, 8 * sh_:8 * sh_ + 8], ALU.add))
                    link(ts(coef[:, i, 2, :], gv, ALPHA, None, ALU.mult))
                    ts(coef[:, i, 3, :], bv, ALPHA, None, ALU.mult).then_inc(S["coef_ready"], 1)
                else:
                    link(dve.tensor_copy(coef[:, i, 0, :], gv))
                    dve.tensor_copy(coef[:, i, 1, :], bv).then_inc(S["coef_ready"], 1)
                dve.wait_ge(S["coef_ready"], i + 1)
                dve.wait_ge(S["ax_ready"], 8 * i + 8)
                dve.wait_ge(S["h_ready"], 8 * i + 8)
                for ch in range(DC):
                    if not second:
                        if ch % 2 == 0:
                            dve.wait_ge(used, used_at(ML_OUT if layer else AB_OUT) + ch // 2 + 1)
                    elif ch == 0:
                        dve.wait_ge(S["block_done"], 3 + 3 * NE * (layer + 1))
                    stt(rT[:, ch, :], b2(ch // 2)[:, ch % 2, :], mcol(layer, G2 if second else G1, ch),
                        axT[:, ch, :], ALU.mult, ALU.add).then_inc(S["r_done"], 1)
                dve.wait_ge(S["mean_done"], i + 1)
                mb = bc(bank[:, 4, 0:TOK].rearrange("p (a t) -> p a t", a=1), P, 2, TOK)
                for b in range(4):
                    v = rT[:, 2 * b:2 * b + 2, :]
                    tt(v, v, mb, ALU.subtract).then_inc(S["cen_done"], 1)
                dve.wait_ge(S["std_done"], i + 1)
                link(dve.reciprocal(std[:, 1, :], std[:, 0, :]))
                sb_ = bc(std[:, 1, :].rearrange("p (a t) -> p a t", a=1), P, 2, TOK)
                for b in range(4):
                    v = rT[:, 2 * b:2 * b + 2, :]
                    tt(v, v, sb_, ALU.mult).then_inc(S["norm_done"], 1)

            def moe(layer):
                first = MOE_AT[layer]

                def low(it, e2, i):
                    for g in range(2):
                        dve.wait_ge(S["whi_done"], it * 12 + (6 * (NE * layer + e2) + 2 * i + g + 1))
                        dst, src = block_part(wlo, first + 3 * e2, i, g)
                        hi, _ = block_part(whi, first + 3 * e2, i, g)
                        tt(dst, src, hi.bitcast(F32), ALU.subtract).then_inc(S["wlo_done"], 1)
                    if i == 1:
                        dve.wait_ge(S["wlo_done"], it * 8 + (4 * (NE * layer + e2) + 4))
                        dve.nop().then_inc(gu_used, 1)

                low(0, 0, 0)
                low(0, 0, 1)
                for b in range(4):
                    dve.wait_ge(S["hhi_done"], 4 * layer + b + 1)
                    v = slice(2 * b, 2 * b + 2)
                    tt(hlo[:, v, :], hT[:, v, :], hhi[:, v, :].bitcast(F32), ALU.subtract).then_inc(S["hlo_done"], 1)
                dve.wait_ge(S["aff_turned"], layer + 1)
                aff = rt[:, 0, 0:TT * NE]
                link(dve.tensor_copy(aff, bank[:, 6, 0:TT * NE]))
                sel, one, two, gates = (rt[:, i, 0:TT * NE] for i in (1, 2, 3, 4))
                psum_ = pair6[:, :, :]
                score, best, key, chosen = (rt[:, i, 0:TT * NG] for i in (6, 7, 8, 9))
                kmax, tot = (rt[:, i, 0:TT] for i in (10, 11))
                order = rt[:, 12, 0:NG]
                v4 = lambda a: a.rearrange("p (q e) -> p q e", e=EG)
                vg = lambda a: a.rearrange("p (a g) -> p a g", g=NG)
                for g in range(NG):
                    link(dve.memset(order[:, g:g + 1], float(NG - g)))
                link(tt(sel.rearrange("p (a e) -> p a e", e=NE), aff.rearrange("p (a e) -> p a e", e=NE),
                        bc(rbias[:, :].rearrange("p (a e) -> p a e", a=1), P, TT, NE), ALU.add))
                s4 = v4(sel)
                at = 0
                for d in range(1, EG):
                    link(tt(psum_[:, :, at:at + EG - d], s4[:, :, 0:EG - d], s4[:, :, d:EG], ALU.add))
                    at += EG - d
                link(dve.tensor_reduce(score, psum_, AX.X, ALU.max))
                link(dve.tensor_reduce(kmax, vg(score), AX.X, ALU.max))
                link(tt(vg(best), vg(score), bc(kmax.rearrange("p (a g) -> p a g", g=1), P, TT, NG), ALU.is_equal))
                link(tt(vg(key), vg(best), bc(order.rearrange("p (a g) -> p a g", a=1), P, TT, NG), ALU.mult))
                link(dve.tensor_reduce(kmax, vg(key), AX.X, ALU.max))
                link(tt(vg(chosen), vg(key), bc(kmax.rearrange("p (a g) -> p a g", g=1), P, TT, NG), ALU.is_equal))
                cmp_ = pairs[:, 0, :, :, :].rearrange("p a q e -> p (a q e)").rearrange(
                    "p (q i j) -> p q i j", i=EG, j=EG)
                eq_ = pairs[:, 1, :, :, :].rearrange("p a q e -> p (a q e)").rearrange(
                    "p (q i j) -> p q i j", i=EG, j=EG)
                Q = TT * NG
                sj = bc(s4.rearrange("p q (i j) -> p q i j", i=1), P, Q, EG, EG)
                si = bc(s4.rearrange("p q (i j) -> p q i j", j=1), P, Q, EG, EG)
                link(tt(cmp_, sj, si, ALU.is_gt))
                for i in range(1, EG):
                    link(tt(eq_[:, :, i, 0:i], sj[:, :, i, 0:i], si[:, :, i, 0:i], ALU.is_equal))
                    link(tt(cmp_[:, :, i, 0:i], cmp_[:, :, i, 0:i], eq_[:, :, i, 0:i], ALU.add))
                link(dve.tensor_reduce(one, cmp_, AX.X, ALU.add))
                link(ts(one, one, 2.0, None, ALU.is_lt))
                link(tt(v4(one), v4(one), bc(chosen.rearrange("p (q e) -> p q e", e=1), P, Q, EG), ALU.mult))
                link(tt(two, one, aff, ALU.mult))
                link(dve.tensor_reduce(tot, two.rearrange("p (a e) -> p a e", e=NE), AX.X, ALU.add))
                link(dve.reciprocal(tot, tot))
                tt(gates.rearrange("p (a e) -> p a e", e=NE), two.rearrange("p (a e) -> p a e", e=NE),
                   bc(tot.rearrange("p (a e) -> p a e", e=1), P, TT, NE), ALU.mult).then_inc(S["gates_done"], 1)

                dve.wait_ge(S["gt_copied"], layer + 1)
                dve.wait_ge(S["ax_ready"], 8 * (2 * layer + 2))
                dve.wait_ge(S["h_ready"], 8 * (2 * layer + 2))
                tt(gsel, bc(gT[:, :].rearrange("p (a t) -> p a t", a=1), NE, NE, TOK),
                   bc(ident[0:NE, 0:NE].rearrange("p (e a) -> p e a", a=1), NE, NE, TOK), ALU.mult
                   ).then_inc(S["gsel_done"], 1)

                def gated(it, e2, half):
                    n = 32 * layer + 2 * e2 + half
                    dve.wait_ge(S["sil_done"], it * 4 + (n + 1))
                    dve.wait_ge(S["ef_done"], it * 4 + (n + 1))
                    tt(pr[:, half, :], bank[:, 4 + half, TOK:2 * TOK], sil[:, half, :], ALU.mult
                       ).then_inc(S["prod_done"], 1)
                    dve.wait_ge(S["prod_done"], it * 4 + (n + 3))
                    dve.wait_ge(S["gb_done"], it + (8 * layer + 1))
                    dve.wait_ge(S["he_done"], it * 4 + (n + 1))
                    tt(ef[:, half, :], pr[:, half, :], b2(6)[:, e2, :], ALU.mult).then_inc(S["ef_done"], 1)

                def gated_low(it, e2, half):
                    n = 32 * layer + 2 * e2 + half
                    dve.wait_ge(S["ehi_done"], it * 4 + (n + 1))
                    tt(elo[:, e2, half, :], ef[:, half, :], ehi[:, e2, half, :].bitcast(F32), ALU.subtract
                       ).then_inc(S["he_done"], 1)

                def two(it, last=False):
                    for e2 in range(2):
                        gated(it, e2, 0)
                        if layer == 0:
                            mod_slot(24 + 2 * e2, it)
                        gated_low(it, e2, 0)
                        if e2 == 0:
                            low(it, 1, 0)
                        elif not last:
                            low(it + 1, 0, 0)
                        gated(it, e2, 1)
                        if layer == 0 and e2 == 0:
                            mod_slot(25, it)
                        gated_low(it, e2, 1)
                        if e2 == 0:
                            low(it, 1, 1)
                        elif not last:
                            low(it + 1, 0, 1)

                with dve.Fori(0, NE // 2 - 1) as it:
                    two(it)
                two(NE // 2 - 1, last=True)

            norm(0)
            moe(0)
            modulation(1, (SH1, SC1, G1, SH2, SC2, G2), 48)
            norm(1)

            R = [mrow[0:MH, i, :] for i in range(12)]
            dve.wait_ge(S["mgate_ln"], 1)
            link(stt(R[5], R[1], 0.0, R[4], ALU.min, ALU.subtract))
            link(dve.tensor_tensor_scan(R[6], bc(ones[0:MH, 0:1], MH, TOK), R[5], 0.0, ALU.mult, ALU.add))
            link(tt(R[7], R[0], R[6], ALU.subtract))
            link(dve.tensor_tensor_scan(R[8], R[7], R[7], 0.0, ALU.max, ALU.max))
            tt(R[9], R[8], R[6], ALU.add).then_inc(S["mrow_done"], 1)
            dve.wait_ge(S["mcol_turned"], 1)
            dve.tensor_copy(ccol[:, :, :], bank[:, 6, 0:TT * MH].rearrange("p (a h) -> p a h", a=TT)
                            ).then_inc(S["mcol_done"], 1)
            for j in range(8):
                for a in range(2):
                    m = 2 * j + a
                    dve.wait_ge(S["conv_a"], 2 * j + 2)
                    o = cv[:, j % 2, a, :]
                    src = b2(j % 4)[:, a, :]
                    for tap in range(CW - 2, -1, -1):
                        d = CW - 1 - tap
                        ins = stt(o[:, d:TOK], src[:, 0:TOK - d], cols[:, 2, 16 * tap + m:16 * tap + m + 1],
                                  o[:, d:TOK], ALU.mult, ALU.add)
                        if tap:
                            link(ins)
                    ins.then_inc(S["conv_done"], 1)
            for hd in range(MH):
                q = hd % 2
                dve.wait_ge(S["mb_done"], hd + 1)
                if hd >= 2:
                    dve.wait_ge(S["me_done"], hd - 1)
                src = bank[:, q, 0:384]
                ts(dM[:, q, 0:TOK], src[:, 0:TOK], ccol[:, 0, hd:hd + 1], 0.0, ALU.subtract, ALU.max
                   ).then_inc(S["md_done"], 1)
                ts(dM[:, q, TOK:384], src[:, TOK:384], ccol[:, 1, hd:hd + 1], 0.0, ALU.subtract, ALU.max
                   ).then_inc(S["md_done"], 1)
                dve.wait_ge(S["me_done"], hd + 1)
                dve.wait_ge(S["mqk_done"], hd + 1)
                if hd >= 2:
                    dve.wait_ge(S["mnum_done"], hd - 1)
                stt(sM[:, q, :], bank[:, 2 + q, 0:384], float(P) ** -0.5, eM[:, q, :], ALU.mult, ALU.mult
                    ).then_inc(S["ms_done"], 1)
                dve.wait_ge(S["mnum_done"], hd + 1)
                dve.wait_ge(S["mfl_done"], 2 * hd + 2)
                nd = b2(4 + q)
                if hd:
                    dve.wait_ge(S["mh_done"], hd)
                link(stt(dn[:, 0, :], nd[:, 1, :], -1.0, fl[:, q, :], ALU.mult, ALU.max))
                link(tt(dn[:, 0, :], nd[:, 1, :], dn[:, 0, :], ALU.max))
                link(dve.reciprocal(dn[:, 1, :], dn[:, 0, :]))
                tt(hh[:, hd, :], nd[:, 0, :], dn[:, 1, :], ALU.mult).then_inc(S["mh_done"], 1)
            for b in range(4):
                rs = qkT[:, 8 + 2 * b:10 + 2 * b, :]
                v = hh[:, 2 * b:2 * b + 2, :]
                dve.wait_ge(S["hstd_done"], 2 + b + 1)
                link(dve.reciprocal(rs, rs))
                link(tt(v, v, rs, ALU.mult))
                for k in (2 * b, 2 * b + 1):
                    stt(yT[:, k, :], hh[:, k, :], vcol(V_MNORM + k), oG[:, k, :], ALU.mult, ALU.mult
                        ).then_inc(S["yb_done"], 1)
            norm(2)
            moe(1)
            norm(3)

        @block.tensor
        def _(pe):
            mm = pe.matmul

            pe.wait_ge(S["pool_const"], 1)
            pe.wait_ge(S["x_loaded"], 16)
            xin = sqT[:, :, :].rearrange("p (a b) t -> p a (b t)", a=TT)
            for b in range(4):
                for ch in (2 * b, 2 * b + 1):
                    for t in range(TT):
                        ins = pe.transpose(b2(b)[:, ch % 2, t * P:(t + 1) * P], xin[:, t, ch * P:(ch + 1) * P],
                                           ident[:, :])
                ins.then_inc(S["x_turned"], 1)
            pe.wait_ge(S["rows_loaded"], 16 * 13)
            for i, n in enumerate((96, V_END, 64)):
                ins = pe.transpose(bank[:, 6, i * P:i * P + n], rows[0:n, i, :], ident[0:n, 0:n])
            ins.then_inc(S["cols_turned"], 1)

            def mod_slot(n, it=None):
                if it is None:
                    pe.wait_ge(mused, n + 1)
                    cols_at = [slice(2 * n + a, 2 * n + a + 1) for a in range(2)]
                else:
                    pe.wait_ge(mused, it * 3 + (n + 1))
                    cols_at = [bass.ds(it * 6 + (64 + 2 * (n - 24) + a), 1) for a in range(2)]
                for a in range(2):
                    ins = mm(bank[:, 7, cols_at[a]], macc[:, n % MRING, a * P:(a + 1) * P], ones[:, 0:1],
                             start=True, stop=True)
                ins.then_inc(S["mcol_out"], 1)

            pe.nop().then_inc(S["block_done"], 3)
            for n in range(8):
                mod_slot(n)
            pe.wait_ge(S["bb_done"], 1)
            for i, row in enumerate((4, 7, 6, 13, 14)):
                ins = pe.transpose(bank[:, 5, i * ST:(i + 1) * ST], s5p[:, row, :], ident[0:ST, 0:ST])
            ins.then_inc(S["s5_turned"], 1)
            pe.wait_ge(S["bc_loaded"], 96)
            pe.wait_ge(S["xT_ready"], 4)
            for i in range(2):
                for k in range(UC):
                    ins = pe.transpose(bank[:, i, k * P:(k + 1) * P], c_raw[:, i, k, :], ident[:, :])
                ins.then_inc(S["ct_turned"], 1)
            pe.wait_ge(S["bb_done"], 2)
            for i in range(2):
                for k in range(UC):
                    ins = pe.transpose(bank[:, 2 + i, k * P:(k + 1) * P],
                                       bb[:, i, 4 * k:4 * k + 4, :].rearrange("p j c -> p (j c)"), ident[:, :])
                ins.then_inc(S["bb_turned"], 1)

            pe.wait_ge(S["cols_ready"], 1)
            pe.wait_ge(S["small_loaded"], 112)
            pe.wait_ge(S["h_ready"], 8)
            for k in range(DC):
                ins = mm(bank[0:RANK, 6, 0:TOK], lr_w[:, k, :], hT[:, k, :], start=(k == 0), stop=(k == DC - 1))
            ins.then_inc(S["lr_done"], 1)

            def by_feature(n, bk, src):
                s = ring[:, n % RING, :].rearrange("p (c n) -> p c n", c=DC)
                pe.wait_ge(landed[n % RING], 16 * (n // RING + 1))
                for a in range(2):
                    for k in range(DC):
                        ins = mm(b2(bk)[:, a, :], s[:, k, a * P:(a + 1) * P], src[:, k, :],
                                 start=(k == 0), stop=(k == DC - 1))
                ins.then_inc(used, 1)

            def by_token(n, bk):
                s = ring[:, n % RING, :].rearrange("p (c n) -> p c n", c=DC)
                pe.wait_ge(landed[n % RING], 16 * (n // RING + 1))
                for t in range(TT):
                    for k in range(DC):
                        ins = mm(b2(bk)[:, t, :], hT[:, k, t * P:(t + 1) * P], s[:, k, :],
                                 start=(k == 0), stop=(k == DC - 1))
                ins.then_inc(used, 1)

            def bu(j):
                if j >= 2:
                    pe.wait_ge(S["rot1_done"], 2 * (j - 1))
                ps = slice(32 * (j % 4), 32 * (j % 4) + 32)
                for i in range(2):
                    ins = mm(b2(4 + j % 2)[:, i, :], bbT[ps, i, j // 4, :], uT[ps, j // 4, :],
                             start=True, stop=True)
                ins.then_inc(S["bu_done"], 1)

            def ys(j):
                pe.wait_ge(S["sst_done"], j + 1)
                if j % 4 == 0 and j:
                    pe.wait_ge(S["yy_done"], j // 4)
                r = j % 4
                for i in range(2):
                    ins = mm(bank[32 * r:32 * r + 32, 6, 0:TOK], ctT[:, i, j, :], sst[:, j % 2, i, :],
                             start=(i == 0), stop=(i == 1))
                ins.then_inc(S["ys_done"], 1)

            pe.wait_ge(S["ct_ready"], 2)
            by_feature(AB_U, 0, hT)
            by_feature(AB_U + 1, 1, hT)
            pe.wait_ge(S["lr_copied"], 1)
            for m in range(QC):
                ins = mm(b2(5)[:, m, :], gate_w[:, m * P:(m + 1) * P],
                         s5p[0:RANK, 0:2, :].rearrange("p a t -> p (a t)"), start=True, stop=True)
            ins.then_inc(S["gate_done"], 1)
            pe.wait_ge(S["proj_out"], 2)
            pe.wait_ge(S["bbT_ready"], 2)
            pe.wait_ge(S["gate_x"], 2)
            for j in range(2, 8):
                if j >= 4:
                    pe.wait_ge(S["proj_out"], j - 3)
                if 4 <= j < 6:
                    by_token(j, j % 4)
                else:
                    by_feature(j, j % 4, hT)
                bu(2 * (j - 2))
                if j > 2:
                    ys(2 * (j - 2) - 2)
                bu(2 * (j - 2) + 1)
                if j > 2:
                    ys(2 * (j - 2) - 1)
            for j in range(12, 16):
                bu(j)
                ys(j - 2)
            ys(14)
            ys(15)

            pe.wait_ge(S["rot1_done"], 2 * ST)
            pe.wait_ge(landed[AB_GLU % RING], 16 * (AB_GLU // RING + 1))
            s = ring[:, AB_GLU % RING, :].rearrange("p (c n) -> p c n", c=UC)
            pe.wait_ge(S["z_done"], UC)
            for b in range(2):
                for a in range(2):
                    m = 2 * b + a
                    for k in range(UC):
                        ins = mm(b2(4 + b)[:, a, :], s[:, k, m * P:(m + 1) * P], zT[:, k, :],
                                 start=(k == 0), stop=(k == UC - 1))
                ins.then_inc(used if b else S["glu_done"], 1)

            pe.wait_ge(S["proj_out"], 8)
            for n in range(LEVELS + 1):
                diag = n == LEVELS
                if diag:
                    ks, qs = kT, qT
                else:
                    pe.wait_ge(S["kq_done"], n + 1)
                    ks, qs = kd[:, n % 2, :, :], qd[:, n % 2, :, :]
                if n >= 2:
                    pe.wait_ge(S["att_out"], 2 * (n - 1))
                for par in range(2):
                    ps = slice(64 * par, 64 * par + 64)
                    o = bank[:, 2 * (n % 2) + par, :].rearrange("p (b t) -> p b t", t=P)
                    for pair in range(2):
                        if n == LEVELS - 1:
                            ins = mm(o[:, pair, :], ks[ps, pair, 0:P], qs[ps, pair, P:TOK], start=True, stop=True)
                        else:
                            for t in range(TT):
                                ins = mm(o[:, 2 * pair + t, :], ks[ps, pair, t * P:(t + 1) * P],
                                         qs[ps, pair, t * P:(t + 1) * P], start=True, stop=True)
                    ins.then_inc(S["att_done"], 1)
                if n < 8:
                    mod_slot(8 + 2 * n)
                    mod_slot(9 + 2 * n)
            pe.wait_ge(S["att_out"], 2 * (LEVELS + 1))
            for b in range(2):
                for a in range(2):
                    hd = 2 * b + a
                    o = b2(b)[:, a, :]
                    vh = lambda t: vS[:, t, hd * GDV:(hd + 1) * GDV]
                    mm(o[:, 0:P], vh(0), attD[:, hd % 2, hd // 2, 0, :], start=True, stop=True)
                    mm(o[:, P:TOK], vh(0), attX[:, hd % 2, hd // 2, :], start=True, stop=False)
                    ins = mm(o[:, P:TOK], vh(1), attD[:, hd % 2, hd // 2, 1, :], start=False, stop=True)
                ins.then_inc(S["av_done"], 1)
            pe.wait_ge(S["glu_sig"], 4)
            for b in range(2):
                pe.wait_ge(S["hsq_done"], b + 1)
                mm(bank[:, 4 + b, :], head_w[:, :], yy[:, 2 * b:2 * b + 2, :].rearrange("p a t -> p (a t)"),
                   start=True, stop=True).then_inc(S["hms_done"], 1)
            pe.wait_ge(S["av_out"], 2)
            pe.wait_ge(S["ya_done"], 4)
            pe.wait_ge(S["yb_done"], 4)
            for j in range(4):
                by_feature(AB_OUT + j, j, yT)

            def norm(i):
                for ch in range(DC):
                    pe.wait_ge(S["r_done"], 8 * i + ch + 1)
                    ins = mm(bank[:, 4, 0:TOK], mean_w[:, :], rT[:, ch, :], start=(ch == 0), stop=(ch == DC - 1))
                ins.then_inc(S["mean_done"], 1)
                for ch in range(DC):
                    if ch % 2 == 0:
                        pe.wait_ge(S["sq_done"], 4 * i + ch // 2 + 1)
                    ins = mm(bank[:, 5, 0:TOK], mean_w[:, :], sqT[:, ch, :], start=(ch == 0), stop=(ch == DC - 1))
                ins.then_inc(S["var_done"], 1)

            def moe(layer):
                for k in range(DC):
                    pe.wait_ge(S["h_ready"], 8 * (2 * layer + 1) + k + 1)
                    ins = mm(bank[0:NE, 6, 0:TOK], router_sb[:, k, :], hT[:, k, :], start=(k == 0), stop=(k == DC - 1))
                ins.then_inc(S["logit_done"], 1)
                pe.wait_ge(S["aff_done"], layer + 1)
                for t in range(TT):
                    ins = pe.transpose(bank[:, 6, t * NE:(t + 1) * NE], affT[:, t * P:(t + 1) * P],
                                       ident[0:NE, 0:NE])
                ins.then_inc(S["aff_turned"], 1)
                pe.wait_ge(S["r_done"], 8 * (2 * layer + 1))
                for b in range(4):
                    mm(bank[:, b, :], zero16[:, 0:P], zero16[:, :], start=True, stop=True, skip_group_check=True)
                first = MOE_AT[layer]
                pe.wait_ge(S["hlo_done"], 4 * layer + 4)

                def gates_turned():
                    pe.wait_ge(S["gates_done"], layer + 1)
                    for t in range(TT):
                        ins = pe.transpose(bank[0:NE, 6, t * P:(t + 1) * P],
                                           rt[:, 4, t * NE:(t + 1) * NE], ident[:, :])
                    ins.then_inc(S["gt_turned"], 1)

                def unit(it, e2, half):
                    u = 2 * e2 + half
                    n = 32 * layer + u
                    pe.wait_ge(S["prod_done"], it * 4 + (n + 1))
                    for g in range(2):
                        pe.wait_ge(S["wlo_done"], it * 8 + (4 * (NE * layer + e2) + 2 * half + g + 1))
                        hi, lo = (block_part(w, first, half, g)[0] for w in (whi, wlo))
                        o = b2(4 + half)[:, g, :]
                        for k in range(DC):
                            mm(o, hi[:, k, :], hhi[:, k, :], start=(k == 0), stop=False)
                            mm(o, hi[:, k, :], hlo[:, k, :], start=False, stop=False)
                            ins = mm(o, lo[:, k, :], hhi[:, k, :], start=False, stop=(k == DC - 1))
                    ins.then_inc(S["block_done"], 1)

                def down(it, e2):
                    for half in range(2):
                        pe.wait_ge(S["wlod_done"], it * 4 + (2 * (NE * layer + e2) + half + 1))
                        pe.wait_ge(S["he_done"], it * 4 + (32 * layer + 2 * e2 + half + 3))
                        hi, lo = (w[:, 2, half * D:(half + 1) * D] for w in (whi, wlo))
                        for m in range(DC):
                            o = b2(m // 2)[:, m % 2, :]
                            cols_m = slice(m * P, (m + 1) * P)
                            for w, e in ((hi, ehi), (hi, elo), (lo, ehi)):
                                ins = mm(o, w[:, cols_m], e[:, e2, half, :], start=False, stop=True,
                                         skip_group_check=True)
                    ins.then_inc(S["block_done"], 1)

                def two(it):
                    for e2 in range(2):
                        unit(it, e2, 0)
                        if e2 == 0:
                            if isinstance(it, int) and it == 0:
                                gates_turned()
                                pe.wait_ge(S["gsel_done"], layer + 1)
                            pe.wait_ge(S["ef_done"], it * 4 + (32 * layer + 2))
                            mm(b2(6), ones[0:NE, :], gsel[:, bass.ds(it * 2, 2), :], start=True, stop=True
                               ).then_inc(S["gb_done"], 1)
                        unit(it, e2, 1)
                        if layer == 0:
                            mod_slot(24 + 2 * e2, it)
                        down(it, e2)
                        if layer == 0 and e2 == 0:
                            mod_slot(25, it)

                two(0)
                with pe.Fori(1, NE // 2) as it:
                    two(it)

            norm(0)
            moe(0)
            norm(1)

            pe.wait_ge(S["h_ready"], 24)
            for g in range(2):
                for k in range(DC):
                    ins = mm(bank[0:MH, 6, g * TOK:(g + 1) * TOK], mg_w[:, k, g * MH:(g + 1) * MH], hT[:, k, :],
                             start=(k == 0), stop=(k == DC - 1))
            ins.then_inc(S["mgate_done"], 1)
            pe.wait_ge(S["r_done"], 16)
            for j in range(16):
                if j == 2:
                    pe.wait_ge(S["mrow_done"], 1)
                    for t in range(TT):
                        ins = pe.transpose(bank[:, 6, t * MH:(t + 1) * MH], mrow[0:MH, 7, t * P:(t + 1) * P],
                                           ident[0:MH, 0:MH])
                    ins.then_inc(S["mcol_turned"], 1)
                if 4 <= j < 12:
                    pe.wait_ge(S["conv_done"], 2 * (j - 4) + 2)
                elif j >= 12:
                    pe.wait_ge(S["proj_out"], 8 + j - 12 + 1)
                if 8 <= j < 12:
                    by_token(ML_IN + j, j % 4)
                else:
                    by_feature(ML_IN + j, j % 4, hT)
            pe.wait_ge(S["proj_out"], 16)
            pe.wait_ge(S["qk_done"], 16)
            pe.wait_ge(S["mcol_done"], 1)
            pe.wait_ge(S["norm_done"], 8)

            def scores(hd):
                q = hd % 2
                if hd >= 2:
                    pe.wait_ge(S["md_done"], 2 * (hd - 1))
                pick = bc(ident[0:MH, hd:hd + 1], MH, P)
                o = bank[:, q, :]
                mm(o[:, 0:TOK], pick, mrow[0:MH, 8, :], start=True, stop=True, skip_group_check=True)
                mm(o[:, 0:P], ident16[:, :], future16[:, :], start=False, stop=True, skip_group_check=True)
                mm(o[:, TOK:384], pick, mrow[0:MH, 8, P:TOK], start=False, stop=True, skip_group_check=True)
                mm(o[:, TOK:384], ident16[:, :], future16[:, :], start=False, stop=True, skip_group_check=True
                   ).then_inc(S["mb_done"], 1)
                if hd >= 2:
                    pe.wait_ge(S["ms_done"], hd - 1)
                o = bank[:, 2 + q, :]
                mm(o[:, 0:TOK], qkT[:, MH + hd, 0:P], qkT[:, hd, :], start=True, stop=True)
                mm(o[:, TOK:384], qkT[:, MH + hd, P:TOK], qkT[:, hd, P:TOK], start=True, stop=True
                   ).then_inc(S["mqk_done"], 1)

            def values(hd):
                q = hd % 2
                if hd >= 2:
                    pe.wait_ge(S["mh_done"], hd - 1)
                pe.wait_ge(S["ms_done"], hd + 1)
                for i in range(2):
                    o = b2(4 + q)[:, i, :]
                    w = [vM[:, t, hd * P:(hd + 1) * P] if i == 0 else ones[:, :] for t in range(TT)]
                    mm(o[:, 0:TOK], w[0], sM[:, q, 0:TOK], start=True, stop=True)
                    ins = mm(o[:, P:TOK], w[1], sM[:, q, TOK:384], start=False, stop=True,
                             skip_group_check=True)
                ins.then_inc(S["mnum_done"], 1)

            for hd in range(MH):
                scores(hd)
                if hd:
                    pe.wait_ge(S["mfl_done"], 2 * hd)
                mm(bank[:, 6, 0:TOK], bc(ident[0:MH, hd:hd + 1], MH, P), mrow[0:MH, 9, :], start=True, stop=True
                   ).then_inc(S["mfl_done"], 1)
                if hd:
                    values(hd - 1)
            values(MH - 1)
            for b in range(4):
                pe.wait_ge(S["hsq_done"], 2 + b + 1)
                mm(bank[:, b, :], head_w[:, :], qkT[:, 2 * b:2 * b + 2, :].rearrange("p a t -> p (a t)"),
                   start=True, stop=True).then_inc(S["hms_done"], 1)
            pe.wait_ge(S["hstd_done"], 6)
            pe.wait_ge(S["yb_done"], 12)
            for j in range(4):
                by_feature(ML_OUT + j, j, yT)
            norm(2)
            moe(1)
            norm(3)
            pe.wait_ge(S["h_ready"], 40)
            for b in range(4):
                t = b // 2
                for k in range(4):
                    ch = 4 * (b % 2) + k
                    ins = pe.transpose(bank[:, b, k * P:(k + 1) * P], hT[:, ch, t * P:(t + 1) * P], ident[:, :])
                ins.then_inc(S["final_turned"], 1)


EPS_H = 1e-6
EPS_LN = 1e-5

_INS = ["x", "c", "router_w", "router_bias", "ada_w", "ada_b", "ln1_g", "ln1_b", "ln2_g", "ln2_b",
        "moe_w_gate", "moe_w_up", "moe_w_down", "ab_w_in", "s5_lam_re", "s5_lam_im", "s5_log_dt",
        "s5_b_re", "s5_b_im", "s5_c_re", "s5_c_im", "s5_d", "s5_glu_w", "s5_glu_b",
        "gla_gate_w", "gla_gate_b", "gla_norm_g", "ab_w_out", "ml_w_in", "ml_conv_w", "ml_conv_b",
        "ml_igate_b", "ml_fgate_b", "ml_norm_g", "ml_w_out"]


def kernel(**inputs):
    import concourse.bacc as _bacc
    from concourse.bass_utils import run_bass_kernel_spmd as _run

    nc = _bacc.Bacc("TRN2", target_bir_lowering=False, num_devices=1)
    arrays, args = {}, []
    for name in _INS:
        a = np.ascontiguousarray(inputs[name])
        arrays[f"in_{name}_dram"] = a
        args.append(nc.dram_tensor(f"in_{name}_dram", a.shape, mybir.dt.from_np(a.dtype),
                                   kind="ExternalInput").ap())
    args.append(nc.dram_tensor("out_dram", (1, TOK, D), F32, kind="ExternalOutput").ap())
    trunk(nc, *args)
    r = _run(nc, [arrays], core_ids=[0])
    return r.results[0]["out_dram"]
```

```python
from contextlib import ExitStack

import numpy as np

import concourse.bass as bass
from concourse import mybir

F32 = mybir.dt.float32
F32R = mybir.dt.float32r
BF16 = mybir.dt.bfloat16
I32 = mybir.dt.int32
ALU = mybir.AluOpType
ACT = mybir.ActivationFunctionType
AX = mybir.AxisListType

P = 128
TOK = 256
TT = TOK // P
D = 1024
DC = D // P
DEPTH = 2
ALPHA = (2.0 * DEPTH) ** 0.25
S5_W, S5_G, S5_N = 512, 16, 64
UC = S5_W // P
ST = (S5_W // S5_G) * S5_N // P
GH, GDV, GDK = 4, 128, 64
QC = GH * GDK // P
RANK = 16
GATE_NORM = 16.0
AB_LR = S5_W + 2 * GH * GDK + 2 * GH * GDV
MH = 8
CW = 4
NE, NG, EG, DE = 16, 4, 4, 256
SLOT = 2048
SC = SLOT // DC
RING = 6
MRING = 3
MOD_A, MOD_S5, MOD_0 = 8, 4, 24
MOD_GLA = (MOD_0 - MOD_A - MOD_S5) // MRING
ROUND_AT = {0: 0, 3: 1}
LEVELS = 8
TABLE_DVE = 11
BIG = 1.0e30
TINY = 1.0e-36
ROUND = 12582912.0
TWO_PI = (6.28125, 0.0019350051879882812, 3.019916050e-07)
PI_BELOW = 3.1415925

LN_G1, LN_B1, LN_G2, LN_B2, V_D, V_GLUB, V_GATEB, V_GNORM, V_CONVB, V_MNORM, V_END = (
    0, 16, 32, 48, 64, 68, 72, 74, 78, 94, 102)
SH1, SC1, G1, SH2, SC2, G2 = range(6)


def trunk(nc, x, c, router_w, router_bias, ada_w, ada_b, ln1_g, ln1_b, ln2_g, ln2_b,
          moe_w_gate, moe_w_up, moe_w_down, ab_w_in, s5_lam_re, s5_lam_im, s5_log_dt,
          s5_b_re, s5_b_im, s5_c_re, s5_c_im, s5_d, s5_glu_w, s5_glu_b,
          gla_gate_w, gla_gate_b, gla_norm_g, ab_w_out, ml_w_in, ml_conv_w, ml_conv_b,
          ml_igate_b, ml_fgate_b, ml_norm_g, ml_w_out, out):
    with ExitStack() as ctx:
        def sb(name, shape, dt=F32):
            return ctx.enter_context(nc.sbuf_tensor(name, shape, dt))

        def sem(name):
            return ctx.enter_context(nc.semaphore(name))

        bank = ctx.enter_context(nc.psum_tensor("bank", [P, 8, 512], F32))
        ring = sb("ring", [P, RING, SLOT])
        mring = sb("mring", [P, MRING, SLOT])
        hT = sb("hT", [P, DC, TOK])
        axT = sb("axT", [P, DC, TOK])
        wide = sb("wide", [P, 2, DC, TOK])
        rT = wide[:, 0, :, :]
        sqT = wide[:, 1, :, :]
        gsel = wide[0:NE, :, :, :].rearrange("p a c t -> p (a c) t")
        std = sb("std", [P, 2, TOK])
        ident = sb("ident", [P, P])
        mean_w = sb("mean_w", [P, P])
        head_w = sb("head_w", [P, P])
        ones = sb("ones", [P, P])
        to_row = sb("to_row", [P, MH, MH])
        zero16 = sb("zero16", [P, 512], BF16)
        ident16 = sb("ident16", [P, P], BF16)
        future16 = sb("future16", [P, P], BF16)
        level_mask = sb("level_mask", [P, LEVELS, P], I32)
        rows = sb("rows", [P, 3, P])
        cols = sb("cols", [P, 3, P])
        mod = sb("mod", [P, DEPTH, 48])
        coef = sb("coef", [P, 4, 4, DC])
        c_col = sb("c_col", [P, 2, DC])
        router_sb = sb("router_sb", [P, DC, NE])
        rbias = sb("rbias", [P, NE])
        lr_w = sb("lr_w", [P, DC, RANK])
        gate_w = sb("gate_w", [RANK, GH * GDK])
        mg_w = sb("mg_w", [P, DC, 2 * MH])
        mg_b = sb("mg_b", [MH, 2])
        macc = sb("macc", [P, MRING, SC])
        mrows = sb("mrows", [64, SC])
        s5dt = sb("s5dt", [16, 2, 2])
        s5c = sb("s5c", [P, 5, ST])
        with nc.sbuf_tensor("arena", [P, 20224], F32) as arena_:
            arena = arena_
        whi = sb("whi", [P, 3, SLOT], F32R)
        wlo = sb("wlo", [P, 3, SLOT], F32R)
        hhi = sb("hhi", [P, DC, TOK], F32R)
        hlo = sb("hlo", [P, DC, TOK], F32R)
        ehi = sb("ehi", [P, 2, 2, TOK], F32R)
        elo = sb("elo", [P, 2, 2, TOK], F32R)
        sil = sb("sil", [P, 2, TOK])
        pr = sb("pr", [P, 2, TOK])
        ef = sb("ef", [P, 2, TOK])
        rt = sb("rt", [P, 14, 32])
        pair6 = sb("pair6", [P, TT * NG, 6])
        pairs = sb("pairs", [P, 2, 2, NE, EG])
        gT = sb("gT", [NE, TOK])
        affT = sb("affT", [NE, TOK])

        def view(at, *shape):
            n = int(np.prod(shape))
            v = arena[:, at:at + n]
            if len(shape) == 1:
                return v
            names = "abcd"[:len(shape)]
            return v.rearrange(f"p ({' '.join(names)}) -> p {' '.join(names)}",
                               **dict(zip(names[1:], shape[1:])))

        cosT = view(0, ST, TOK)
        sinT = view(4096, ST, TOK)
        uT = view(8192, UC, TOK)
        rot = view(9216, 2, 2, 2, TOK)
        vin = view(11264, 2, 2, TOK)
        zst = view(12288, 2, TOK)
        sst = view(12800, 2, 2, TOK)
        bbT = view(13824, 2, UC, P)
        ctT = view(14848, 2, ST, 32)
        qT = view(15872, QC, TOK)
        kT = view(16384, QC, TOK)
        vS = view(16896, TT, GH * GDV)
        rS = view(17920, GH, TOK)
        cum = std[:, :, :]
        kd = view(18944, 2, QC, TOK)
        qd = rT[:, 0:4, :].rearrange("p (a c) t -> p a c t", a=2)
        rotp = rT[:, 4:8, :].rearrange("p (a c) t -> p a c t", a=2)
        attD = view(0, 2, 2, 2, P)
        attX = view(1024, 2, 2, P)
        dif = view(1536, 2, QC, TOK)
        dec = view(2560, 2, QC, TOK)
        oT = view(3584, GH, TOK)
        zT = view(8192, UC, TOK)
        yy = view(4608, UC, TOK)
        sgT = view(5632, UC, TOK)
        b_raw = view(15872, 2, ST, S5_G)
        bb = view(16384, 2, ST, 32)
        bt = view(17408, 4, ST, S5_G)
        c_raw = view(18432, 2, UC, P)
        en = view(19968, 3, 2, ST)
        en2 = view(20064, 3, 2, ST)
        tmp_dve = view(9216, TABLE_DVE, P)
        tmp_pool = view(12800, ST - TABLE_DVE, P)
        s5p = view(11264, 16, P)[0:16]
        qT1 = view(4096, MH, TOK)
        kT1 = view(10240, MH, TOK)
        vM = mring[:, 0, :].rearrange("p (a n) -> p a n", a=TT)
        oG = mring[:, 1, :].rearrange("p (h t) -> p h t", h=MH)
        cv = mring[:, 2, 0:1024].rearrange("p (a b t) -> p a b t", a=2, b=2)
        mrow = view(16384, 12, TOK)
        ccol = view(19456, TT, MH)
        hh = view(12288, MH, TOK)
        dM = view(14336, 2, 384)
        eM = view(15104, 2, 384)
        sM = mring[:, 2, 1024:1792].rearrange("p (a t) -> p a t", a=2)
        numsq = view(15872, 2, TOK)
        yhi = whi[:, 2, :].rearrange("p (c t) -> p c t", c=DC)
        ylo = wlo[:, 2, :].rearrange("p (c t) -> p c t", c=DC)

        def qk_at(m):
            return (qT1 if m < MH else kT1)[:, m % MH, :]

        yT = sqT

        landed = [sem(f"weights_landed{i}") for i in range(RING)]
        used = sem("weights_used")
        gu_used = sem("gate_up_split")
        d_used = sem("down_split")
        mlanded = [sem(f"mod_weights_landed{i}") for i in range(MRING)]
        mod_pe_used = sem("mod_weights_used_by_pe")
        mod_dve_used = sem("mod_weights_used_by_dve")
        mod_pool_used = sem("mod_weights_used_by_pool")
        names = """ident_ready x_loaded c_loaded rows_loaded s5_loaded bc_loaded small_loaded stored
        pool_const x_turned xT_ready c_ready cols_turned cols_ready s5_turned s5c_ready
        bb_done bb_turned ct_turned bbT_ready ct_ready tables_ready
        dve_step act_step pool_step
        mod_ready mod_row_used mod_row_out macc_step mpool_step tables_done h_ready ax_ready coef_ready
        lr_done lr_copied gate_done gate_x gate_ln
        proj_out bu_done rot1_done vin_done scan_done rot2_done sst_done
        ys_done yy_done z_done glu_done glu_sig ya_done
        cum_done dif_done dec_done kq_done att_done att_out av_done av_out hsq_done hms_done
        hstd_done yb_done r_done mean_done cen_done sq_done var_done std_done norm_done
        logit_done aff_done aff_turned gates_done gt_turned gt_copied gsel_done gsel_rest gb_done
        hhi_done hlo_done yhi_done ylo_done mix_hi mix_lo_dve mix_lo_pool whi_done wlo_done wlod_done block_done
        sil_done prod_done ef_done ehi_done he_done mcol_out
        mgate_done mgate_x mgate_ln mrow_done mcol_turned mcol_done conv_a conv_done qk_done
        mb_done md_done me_done mqk_done ms_done mnum_done mfloor_done mnumsq_done mh_done
        mmean_done mvar_done msqrt_done mscale_done mscaleb_done
        final_turned final_out""".split()
        S = {n: sem(n) for n in names}

        def bc(ap, *shape):
            return ap.broadcast_to(list(shape)) if hasattr(ap, "broadcast_to") else ap.to_broadcast(list(shape))

        def mcol(layer, part, ch=0):
            at = 8 * part + ch
            return mod[:, layer, at:at + 1]

        def vcol(row):
            return cols[:, 1, row:row + 1]

        def b2(i, half=None):
            return bank[:, i, :].rearrange("p (a t) -> p a t", a=2)

        def doubling(eng, link, j0, j1, e, tmp, between=None):
            n_t = j1 - j0
            tt = eng.tensor_tensor
            eng.memset(cosT[:, j0:j1, 0:1], 1.0)
            eng.memset(sinT[:, j0:j1, 0:1], 0.0)
            e = e[:, :, :, j0:j1]
            link(eng.tensor_copy(e[:, 0, :, :], s5c[:, 1:3, j0:j1]))
            n = 1
            while n < TOK:
                if n == TOK // 2 and between:
                    between()
                c_n = bc(e[:, 0, 0, :].rearrange("p (j a) -> p j a", a=1), P, n_t, n)
                s_n = bc(e[:, 0, 1, :].rearrange("p (j a) -> p j a", a=1), P, n_t, n)
                tm = tmp[:, :, 0:n]
                cn, sn = cosT[:, j0:j1, 0:n], sinT[:, j0:j1, 0:n]
                c2, s2 = cosT[:, j0:j1, n:2 * n], sinT[:, j0:j1, n:2 * n]
                tt(c2, cn, c_n, ALU.mult)
                link(tt(tm, sn, s_n, ALU.mult))
                link(tt(c2, c2, tm, ALU.subtract))
                tt(s2, sn, c_n, ALU.mult)
                link(tt(tm, cn, s_n, ALU.mult))
                link(tt(s2, s2, tm, ALU.add))
                tt(e[:, 1, :, :], e[:, 0, :, :], e[:, 0, :, :], ALU.mult)
                link(tt(e[:, 2, 1, :], e[:, 0, 0, :], e[:, 0, 1, :], ALU.mult))
                tt(e[:, 0, 0, :], e[:, 1, 0, :], e[:, 1, 1, :], ALU.subtract)
                link(tt(e[:, 0, 1, :], e[:, 2, 1, :], e[:, 2, 1, :], ALU.add))
                n *= 2

        def own_gates(eng, e0, e1):
            n = e1 - e0
            return eng.tensor_tensor(gsel[:, e0:e1, :], bc(gT[:, :].rearrange("p (a t) -> p a t", a=1), NE, n, TOK),
                                     bc(ident[0:NE, e0:e1].rearrange("p (e a) -> p e a", a=1), NE, n, TOK),
                                     ALU.mult)

        def block_part(parts, first, i, g):
            if i < 2:
                dst = parts[:, i, g * D:(g + 1) * D].rearrange("p (c n) -> p c n", c=DC)
                src = ring[:, (first + g) % RING, :].rearrange("p (c n) -> p c n", c=DC)[:, :, i * P:(i + 1) * P]
            else:
                dst = parts[:, 2, g * D:(g + 1) * D]
                src = ring[:, (first + 2) % RING, g * D:(g + 1) * D]
            return dst, src

        def mix_part(parts, i, half):
            n = ML_IN + i
            at = slice(half * P, half * P + P)
            dst = parts[:, i % 2, :].rearrange("p (c n) -> p c n", c=DC)[:, :, at]
            return dst, ring[:, n % RING, :].rearrange("p (c n) -> p c n", c=DC)[:, :, at]

        block = ctx.enter_context(nc.Block())

        AB_U, AB_Q, AB_K, AB_V, AB_R, AB_GLU, AB_OUT = 0, 2, 3, 4, 6, 8, 9
        MOE0 = AB_OUT + 4
        ML_IN = MOE0 + 3 * NE
        ML_OUT = ML_IN + 16
        MOE1 = ML_OUT + 4
        MOE_AT = (MOE0, MOE1)

        def used_at(n):
            return n if n < ML_IN else n - 3 * NE

        YS_BANK = (6, 7, 6, 0)

        def row_bank(n):
            return 4 if n < MOD_A else 1 if n < MOD_A + MOD_S5 else 6

        def mod_own(n):
            first = MOD_A + MOD_S5
            return n if n < first else first + MRING * (n - first)

        def mod_used_at(n):
            first = MOD_A + MOD_S5
            if n < first:
                return mod_pe_used, n + 1
            i, m = divmod(n - first, MRING)
            return (mod_pe_used, mod_dve_used, mod_pool_used)[m], (first if m == 0 else 0) + i + 1

        @block.sync
        def _(sp):
            def refill(n):
                old = n - RING
                if 0 <= old < MOE0:
                    sp.wait_ge(used, old + 1)
                elif MOE0 <= old < ML_IN:
                    e, k = divmod(old - MOE0, 3)
                    sp.wait_ge(d_used if k == 2 else gu_used, e + 1)
                elif ML_IN <= old < MOE1:
                    sp.wait_ge(used, MOE0 + old - ML_IN + 1)

            def load(n, src, split=DC):
                refill(n)
                dst = ring[:, n % RING, :].rearrange("p (c n) -> p c n", c=split)
                sp.dma_start(dst, src).then_inc(landed[n % RING], 16)

            def load_cols(n, w, j):
                load(n, w[:, j * SC:(j + 1) * SC].rearrange("(c p) n -> p c n", p=P))

            def load_mod(n, layer, j):
                if n >= MRING:
                    sp.wait_ge(*mod_used_at(n - MRING))
                sp.dma_start(mring[:, n % MRING, :].rearrange("p (c n) -> p c n", c=DC),
                             ada_w[layer, :, j * SC:(j + 1) * SC].rearrange("(p c) n -> p c n", c=DC)
                             ).then_inc(mlanded[n % MRING], 16)

            sp.dma_start(c_col[:, 0, :], c.rearrange("b (p c) -> (b p) c", c=DC)).then_inc(S["c_loaded"], 16)
            lam = lambda a: a[0].rearrange("(j g) p -> j g p", g=2)
            for i, a in enumerate((s5_lam_re, s5_lam_im)):
                sp.dma_start(s5p[:, i, :].rearrange("j (g p) -> j g p", g=2), lam(a)).then_inc(S["s5_loaded"], 16)
            sp.dma_start(s5dt[:, 0, :], s5_log_dt[0].rearrange("(j g) -> j g", g=2)).then_inc(S["s5_loaded"], 16)
            for j in range(MOD_A):
                if j == MRING:
                    for l in range(DEPTH):
                        sp.dma_start(rows[48 * l:48 * l + 48, 0, :], ada_b[l].rearrange("(r n) -> r n", n=P)
                                      ).then_inc(S["rows_loaded"], 16)
                    for a, at in ((ln1_g, LN_G1), (ln1_b, LN_B1), (ln2_g, LN_G2), (ln2_b, LN_B2)):
                        sp.dma_start(rows[at:at + 16, 1, :], a.rearrange("l (r n) -> (l r) n", n=P)
                                      ).then_inc(S["rows_loaded"], 16)
                    for a, at, n in ((s5_d, V_D, 4), (s5_glu_b, V_GLUB, 4), (gla_gate_b, V_GATEB, 2),
                                     (gla_norm_g, V_GNORM, 4), (ml_conv_b, V_CONVB, 16), (ml_norm_g, V_MNORM, 8)):
                        sp.dma_start(rows[at:at + n, 1, :], a[0].rearrange("(r n) -> r n", n=P)
                                      ).then_inc(S["rows_loaded"], 16)
                    sp.dma_start(rows[0:64, 2, :], ml_conv_w[0].rearrange("j (r n) -> (j r) n", n=P)
                                  ).then_inc(S["rows_loaded"], 16)
                load_mod(j, 0, j)
                if j == 1:
                    sp.dma_start(sqT[:, :, :].rearrange("p (a b) t -> p a (b t)", a=TT),
                                 x[0].rearrange("(a p) d -> p a d", p=P)).then_inc(S["x_loaded"], 16)
            for i, a in enumerate((s5_b_re, s5_b_im)):
                sp.dma_start(b_raw[:, i, :, :], a[0].rearrange("(j g) p c -> (g p) j c", g=2)
                              ).then_inc(S["bc_loaded"], 16)
            for i, a in enumerate((s5_c_re, s5_c_im)):
                for h in range(2):
                    sp.dma_start(c_raw[:, i, :, h * 64:h * 64 + 64],
                                  a[0].rearrange("(k g) c p -> (g c) k p", g=8)).then_inc(S["bc_loaded"], 16)
            for j in range(6):
                load_cols(AB_U + j, ab_w_in[0], j)
            for j in range(MOD_A, MOD_A + 3):
                load_mod(j, 0, j)
            for j in range(6, 8):
                load_cols(AB_U + j, ab_w_in[0], j)
            load(AB_GLU, s5_glu_w[0].rearrange("(c p) n -> p c n", p=P), UC)
            for j in range(MOD_A + 3, MOD_A + MOD_S5 + 2):
                load_mod(j, 0, j)
            for j in range(4):
                load_cols(AB_OUT + j, ab_w_out[0], j)
            for j in range(MOD_A + MOD_S5 + 2, MOD_0):
                load_mod(j, 0, j)

            def next_mod(it, m):
                if isinstance(it, int) and it == 0:
                    sp.wait_ge(*mod_used_at(MOD_0 + m - MRING))
                elif m < 2:
                    sp.wait_ge(mod_dve_used, it * 2 + (MOD_GLA + m - 1))
                else:
                    sp.wait_ge(mod_pool_used, it + MOD_GLA)
                sp.dma_start(mring[:, m, :].rearrange("p (c n) -> p c n", c=DC),
                             ada_w[1, :, bass.ds(it * (MRING * SC) + m * SC, SC)].rearrange(
                                 "(p c) n -> p c n", c=DC)).then_inc(mlanded[m], 16)

            def experts(layer):
                first = MOE_AT[layer]

                def two(it):
                    for e2 in range(2):
                        for k in range(3):
                            j = 3 * e2 + k
                            n = first + j
                            slot = n % RING
                            w = (moe_w_gate, moe_w_up, moe_w_down)[k][layer]
                            src = w[bass.ds(it * 2 + e2, 1), :, :]
                            if isinstance(it, int):
                                refill(n)
                            else:
                                sp.wait_ge(d_used if k == 2 else gu_used, it * 2 + (NE * layer + e2 - 1))
                            if k < 2:
                                src = src.rearrange("e (c p) n -> p (e c) n", p=P)
                                dst = ring[:, slot, :].rearrange("p (c n) -> p c n", c=DC)
                            else:
                                src = src.rearrange("e (c p) n -> p (e c) n", p=P)
                                dst = ring[:, slot, :].rearrange("p (c n) -> p c n", c=2)
                            sp.dma_start(dst, src).then_inc(landed[slot], 16)
                            if layer == 0:
                                if j == 5:
                                    next_mod(it, 0)
                                    next_mod(it, 2)
                                elif j == 2 and not isinstance(it, int):
                                    next_mod(it - 1, 1)

                two(0)
                if layer == 0:
                    sp.wait_ge(*mod_used_at(MOD_0 + 1 - MRING))
                with sp.Fori(1, NE // 2) as it:
                    two(it)
                if layer == 0:
                    next_mod(NE // 2 - 1, 1)

            experts(0)
            for j in range(16):
                load_cols(ML_IN + j, ml_w_in[0], j)
            for j in range(4):
                load_cols(ML_OUT + j, ml_w_out[0], j)
            experts(1)
            for b in range(4):
                sp.wait_ge(S["final_out"], b + 1)
                sp.dma_start(out[0].rearrange("(a p) d -> p a d", p=P)[:, b // 2, (b % 2) * 512:(b % 2) * 512 + 512],
                             sqT[:, :, :].rearrange("p (b c) t -> p b (c t)", b=4)[:, b, :]).then_inc(S["stored"], 16)
            sp.wait_ge(S["stored"], 64)

        @block.gpsimd
        def _(pool):
            step = [0]

            def link(ins):
                step[0] += 1
                ins.then_inc(S["pool_step"], 1)
                pool.wait_ge(S["pool_step"], step[0])

            pool.memset(ones[:, :], 1.0)
            link(pool.memset(ident[:, :], 0.0))
            link(pool.affine_select(out=ident[:, :], in_=ident[:, :], compare_op=ALU.not_equal, fill=1.0,
                                    base=0, pattern=[[-1, P]], channel_multiplier=1))
            pool.nop().then_inc(S["ident_ready"], 1)
            pool.memset(mean_w[:, :], 1.0 / D)
            pool.memset(head_w[:, :], 1.0 / P)
            link(pool.memset(to_row[:, :, :], 0.0))
            for h in range(MH):
                pool.memset(to_row[:, h, h:h + 1], 1.0)
            pool.memset(zero16[:, :], 0.0)
            link(pool.tensor_copy(ident16[:, :], ident[:, :]))
            link(pool.memset(future16[:, :], 0.0))
            pool.affine_select(out=future16[:, :], in_=future16[:, :], compare_op=ALU.is_ge, fill=BIG,
                               base=0, pattern=[[1, P]], channel_multiplier=-1)
            link(pool.memset(level_mask[:, :, :], 0))
            for lv in range(LEVELS - 1):
                h = 1 << lv
                m = level_mask[:, lv, :].rearrange("p (n two h) -> p n two h", two=2, h=h)[:, :, 1, :]
                link(pool.memset(m, 1))
                link(pool.affine_select(out=m, in_=m, compare_op=ALU.is_ge, fill=0.0, base=0,
                                        pattern=[[-2 * h, P // (2 * h)], [0, h]], channel_multiplier=1))
                link(pool.affine_select(out=m, in_=m, compare_op=ALU.is_ge, fill=0.0, base=h - 1,
                                        pattern=[[2 * h, P // (2 * h)], [0, h]], channel_multiplier=-1))
            pool.tensor_copy(level_mask[:, LEVELS - 1, :], ident[:, :]).then_inc(S["pool_const"], 1)

            pool.wait_ge(S["xT_ready"], 4)
            for ch in range(DC):
                pool.tensor_scalar(axT[:, ch, :], rT[:, ch, :], ALPHA, None, ALU.mult).then_inc(S["ax_ready"], 1)

            pool.wait_ge(S["s5c_ready"], 1)
            doubling(pool, link, TABLE_DVE, ST, en2, tmp_pool)
            pool.nop().then_inc(S["tables_done"], 1)

            def rotate_in(j):
                pool.wait_ge(S["rot1_done"], 2 * j + 2)
                if j >= 2:
                    pool.wait_ge(S["scan_done"], 2 * (j - 1))
                q = j % 2
                pool.tensor_tensor(vin[:, q, 0, :], rot[:, q, 0, 0, :], rot[:, q, 1, 1, :], ALU.add)
                pool.tensor_tensor(vin[:, q, 1, :], rot[:, q, 0, 1, :], rot[:, q, 1, 0, :],
                                   ALU.subtract).then_inc(S["vin_done"], 1)

            def rotate_out(j):
                pool.wait_ge(S["rot2_done"], 2 * j + 2)
                if j >= 2:
                    pool.wait_ge(S["ys_done"], j - 1)
                q = j % 2
                pool.tensor_tensor(sst[:, q, 0, :], rotp[:, 0, 0, :], rotp[:, 1, 1, :], ALU.subtract)
                pool.tensor_tensor(sst[:, q, 1, :], rotp[:, 0, 1, :], rotp[:, 1, 0, :],
                                   ALU.add).then_inc(S["sst_done"], 1)

            for j in range(ST + 1):
                if j < ST:
                    rotate_in(j)
                if j >= 1:
                    rotate_out(j - 1)

            def mod_multiply(before):
                slot = mring[:, 2, :].rearrange("p (c n) -> p c n", c=DC)
                c_b = bc(c_col[:, 1, :].rearrange("p (c a) -> p c a", a=1), P, DC, SC)
                pool.tensor_tensor(slot, slot, c_b, ALU.mult).then_inc(S["mpool_step"], 1)
                pool.wait_ge(S["mpool_step"], before + 1)

            def mod_add(before):
                slot = mring[:, 2, :].rearrange("p (c n) -> p c n", c=DC)
                pool.tensor_tensor(slot[:, 0:4, :], slot[:, 0:4, :], slot[:, 4:8, :], ALU.add
                                   ).then_inc(S["mpool_step"], 1)
                pool.wait_ge(S["mpool_step"], before + 2)
                pool.tensor_tensor(slot[:, 0:2, :], slot[:, 0:2, :], slot[:, 2:4, :], ALU.add
                                   ).then_inc(S["mpool_step"], 1)
                pool.wait_ge(S["mpool_step"], before + 3)
                pool.tensor_tensor(macc[:, 2, :], slot[:, 0, :], slot[:, 1, :], ALU.add).then_inc(mod_pool_used, 1)

            def mod_first(i):
                n = MOD_A + MOD_S5 + MRING * i + 2
                pool.wait_ge(mlanded[2], 16 * (n // MRING + 1))
                mod_multiply(3 * i)

            def mod_second(i):
                if i:
                    pool.wait_ge(S["mcol_out"], MOD_A + MOD_S5 + MRING * i)
                mod_add(3 * i)

            pool.memset(kd[:, :, :, :], 0.0)
            link(pool.memset(qd[:, :, :, :], 0.0))
            pool.wait_ge(S["proj_out"], 4)
            for lv in range(LEVELS):
                h = 1 << lv
                q = lv % 2
                pool.wait_ge(S["dec_done"], 2 * lv + 2)
                if lv >= 2:
                    pool.wait_ge(S["att_done"], 2 * (lv - 1))
                k5 = kT.rearrange("p c (n two h) -> p (c n) two h", two=2, h=h)[:, :, 0, :]
                q5 = qT.rearrange("p c (n two h) -> p (c n) two h", two=2, h=h)[:, :, 1, :]
                d5 = dec[:, q, :, :].rearrange("p c (n two h) -> p (c n) two h", two=2, h=h)
                ko = kd[:, q, :, :].rearrange("p c (n two h) -> p (c n) two h", two=2, h=h)[:, :, 0, :]
                qo = qd[:, q, :, :].rearrange("p c (n two h) -> p (c n) two h", two=2, h=h)[:, :, 1, :]
                pool.tensor_tensor(ko, k5, d5[:, :, 0, :], ALU.mult)
                pool.tensor_tensor(qo, q5, d5[:, :, 1, :], ALU.mult).then_inc(S["kq_done"], 1)
                if lv in ROUND_AT:
                    mod_first(ROUND_AT[lv])
                elif lv - 1 in ROUND_AT:
                    mod_second(ROUND_AT[lv - 1])
            for i in (2, 3):
                mod_first(i)
                mod_second(i)

            def axes(i):
                for b in range(4):
                    pool.wait_ge(S["norm_done"], 4 * i + b + 1)
                    if b == 0:
                        pool.wait_ge(S["coef_ready"], i + 1)
                    for ch in (2 * b, 2 * b + 1):
                        pool.tensor_scalar(axT[:, ch, :], rT[:, ch, :], coef[:, i, 2, ch:ch + 1],
                                           coef[:, i, 3, ch:ch + 1], ALU.mult, ALU.add).then_inc(S["ax_ready"], 1)

            def mod_slot(it):
                pool.wait_ge(mlanded[2], it * 16 + 16 * (MOD_0 // MRING + 1))
                pool.wait_ge(S["mcol_out"], it * MRING + MOD_0)
                mod_multiply(it * 3 + 3 * MOD_GLA)
                mod_add(it * 3 + 3 * MOD_GLA)

            def moe(layer):
                def down_low(it, e2):
                    n = MOE_AT[layer] + 3 * e2 + 2
                    for half in range(2):
                        at = slice(half * D, half * D + D)
                        pool.wait_ge(S["whi_done"], it * 12 + (6 * (NE * layer + e2) + 5 + half))
                        pool.tensor_tensor(wlo[:, 2, at], ring[:, n % RING, at], whi[:, 2, at].bitcast(F32),
                                           ALU.subtract).then_inc(S["wlod_done"], 1)
                    pool.wait_ge(S["wlod_done"], it * 4 + (2 * (NE * layer + e2) + 2))
                    pool.nop().then_inc(d_used, 1)

                def two(it, last=False):
                    if layer == 0:
                        mod_slot(it)
                    down_low(it, 1)
                    if not last:
                        down_low(it + 1, 0)

                down_low(0, 0)
                pool.wait_ge(S["gt_copied"], layer + 1)
                pool.wait_ge(S["ax_ready"], 8 * (2 * layer + 2))
                pool.wait_ge(S["h_ready"], 8 * (2 * layer + 2))
                own_gates(pool, 2, NE).then_inc(S["gsel_rest"], 1)
                with pool.Fori(0, NE // 2 - 1) as it:
                    two(it)
                two(NE // 2 - 1, last=True)

            def mix_low(i):
                pool.wait_ge(S["mix_hi"], 2 * i + 2)
                dst, src = mix_part(wlo, i, 1)
                pool.tensor_tensor(dst, src, mix_part(whi, i, 1)[0].bitcast(F32), ALU.subtract
                                   ).then_inc(S["mix_lo_pool"], 1)

            axes(0)
            moe(0)
            mix_low(0)
            mix_low(1)
            axes(1)
            for i in range(2, 20):
                mix_low(i)
            axes(2)
            moe(1)

        @block.scalar
        def _(act):
            step = [0]

            def link(ins):
                step[0] += 1
                ins.then_inc(S["act_step"], 1)
                act.wait_ge(S["act_step"], step[0])

            act.wait_ge(S["c_loaded"], 16)
            act.activation(c_col[:, 1, :], c_col[:, 0, :], ACT.Silu).then_inc(S["c_ready"], 1)
            act.wait_ge(S["s5_loaded"], 48)
            act.activation(s5dt[:, 1, :], s5dt[:, 0, :], ACT.Exp).then_inc(S["tables_ready"], 1)
            act.wait_ge(S["tables_ready"], 2)
            act.activation(s5p[:, 4, :], s5p[:, 2, :], ACT.Exp).then_inc(S["tables_ready"], 1)
            act.wait_ge(S["tables_ready"], 4)
            act.activation(s5p[:, 6, :], s5p[:, 3, :], ACT.Sin).then_inc(S["tables_ready"], 1)
            act.activation(s5p[:, 9, :], s5p[:, 3, :], ACT.Sin, scale=0.5).then_inc(S["tables_ready"], 1)
            def mod_row(n):
                ps = slice(32 * (n % 2), 32 * (n % 2) + 1)
                act.wait_ge(mod_pe_used, n + 1)
                if n >= 2:
                    act.wait_ge(S["mod_row_used"], n - 1)
                act.activation(mrows[ps, :], bank[ps, row_bank(n), TOK:TOK + SC], ACT.Copy
                               ).then_inc(S["mod_row_out"], 1)

            mod_row(0)
            for b in range(4):
                act.wait_ge(S["x_turned"], b + 1)
                act.activation(rT[:, 2 * b:2 * b + 2, :], b2(b), ACT.Copy).then_inc(S["xT_ready"], 1)
            for n in range(1, 4):
                mod_row(n)
            act.dma_start(lr_w[:, :, :], ab_w_in[0, :, AB_LR:AB_LR + RANK].rearrange("(c p) n -> p c n", p=P)
                          ).then_inc(S["small_loaded"], 16)
            act.dma_start(gate_w[:, :], gla_gate_w[0]).then_inc(S["small_loaded"], 16)
            act.dma_start(router_sb[:, :, :], router_w.rearrange("(c p) n -> p c n", p=P)
                          ).then_inc(S["small_loaded"], 16)
            act.dma_start(rbias[:, :], router_bias.rearrange("(a n) -> a n", a=1).to_broadcast([P, NE])
                          ).then_inc(S["small_loaded"], 16)
            act.dma_start(mg_w[:, :, :], ml_w_in[0, :, 4 * D:4 * D + 2 * MH].rearrange("(c p) n -> p c n", p=P)
                          ).then_inc(S["small_loaded"], 16)
            act.dma_start(mg_b[:, 0:1], ml_igate_b[0].rearrange("(h a) -> h a", a=1)).then_inc(S["small_loaded"], 16)
            act.dma_start(mg_b[:, 1:2], ml_fgate_b[0].rearrange("(h a) -> h a", a=1)).then_inc(S["small_loaded"], 16)
            for n in range(4, MOD_A):
                mod_row(n)
            act.wait_ge(S["mod_ready"], 1)
            act.wait_ge(S["xT_ready"], 4)
            for ch in range(DC):
                act.activation(hT[:, ch, :], rT[:, ch, :], ACT.Identity, scale=mcol(0, SC1, ch),
                               bias=mcol(0, SH1, ch)).then_inc(S["h_ready"], 1)

            act.wait_ge(S["lr_done"], 1)
            act.activation(s5p[0:RANK, 0:2, :], bank[0:RANK, 6, 0:TOK].rearrange("p (a t) -> p a t", a=2),
                           ACT.Copy).then_inc(S["lr_copied"], 1)

            def leave(j):
                act.wait_ge(used, j + 1)
                bk = b2(j % 4)
                if j < 2:
                    ins = act.activation(uT[:, 2 * j:2 * j + 2, :], bk, ACT.Copy)
                elif j == 2:
                    ins = act.activation(qT[:, :, :], bk, ACT.Copy, scale=GDK ** -0.5)
                elif j == 3:
                    ins = act.activation(kT[:, :, :], bk, ACT.Copy)
                elif j < 6:
                    ins = act.activation(vS[:, :, (j - 4) * SC:(j - 3) * SC], bk, ACT.Copy)
                else:
                    ins = act.activation(rS[:, 2 * (j - 6):2 * (j - 6) + 2, :], bk, ACT.Silu)
                ins.then_inc(S["proj_out"], 1)

            leave(0)
            leave(1)
            act.wait_ge(S["gate_done"], 1)
            for ch in range(QC):
                act.activation(cum[:, ch, :], b2(5)[:, ch, :], ACT.Identity, bias=vcol(V_GATEB + ch)
                               ).then_inc(S["gate_x"], 1)
            act.wait_ge(S["gate_x"], 2)
            link(act.activation(kd[:, 0, :, :], cum[:, :, :], ACT.Abs))
            link(act.activation(kd[:, 1, :, :], kd[:, 0, :, :], ACT.Exp, scale=-1.0))
            act.activation(kd[:, 0, :, :], kd[:, 1, :, :], ACT.Ln, bias=1.0).then_inc(S["gate_ln"], 1)

            for j in range(2, 6):
                leave(j)

            def gelu(k):
                act.wait_ge(S["yy_done"], k + 1)
                act.activation(zT[:, k, :], yy[:, k, :], ACT.Gelu_apprx_tanh).then_inc(S["z_done"], 1)

            gelu(0)
            mod_row(MOD_A)
            mod_row(MOD_A + 1)
            gelu(1)
            leave(6)
            mod_row(MOD_A + 2)
            mod_row(MOD_A + 3)
            gelu(2)
            leave(7)
            gelu(3)

            def glu_sigmoid():
                for k in range(UC):
                    if k == 0:
                        act.wait_ge(S["glu_done"], 1)
                    elif k == 2:
                        act.wait_ge(used, AB_GLU + 1)
                    act.activation(sgT[:, k, :], b2(4 + k // 2)[:, k % 2, :], ACT.Sigmoid,
                                   bias=vcol(V_GLUB + k)).then_inc(S["glu_sig"], 1)

            for lv in range(LEVELS):
                h = 1 << lv
                q = lv % 2
                act.wait_ge(S["dif_done"], lv + 1)
                if lv >= 2:
                    act.wait_ge(S["kq_done"], lv - 1)
                a5 = dif[:, q, :, :].rearrange("p c (n two h) -> p (c n) two h", two=2, h=h)
                d5 = dec[:, q, :, :].rearrange("p c (n two h) -> p (c n) two h", two=2, h=h)
                for half, sign in ((0, -1.0), (1, 1.0)):
                    act.activation(d5[:, :, half, :], a5[:, :, half, :], ACT.Exp,
                                   scale=sign / GATE_NORM).then_inc(S["dec_done"], 1)
                if lv == 2:
                    glu_sigmoid()
                if lv in ROUND_AT or lv == 6:
                    mod_row(MOD_A + MOD_S5 + ROUND_AT.get(lv, 2))
            for b in range(2):
                act.wait_ge(S["av_done"], b + 1)
                act.activation(oT[:, 2 * b:2 * b + 2, :], b2(b), ACT.Copy).then_inc(S["av_out"], 1)
            for b in range(2):
                act.wait_ge(S["av_out"], b + 1)
                act.activation(yy[:, 2 * b:2 * b + 2, :], oT[:, 2 * b:2 * b + 2, :], ACT.Square
                               ).then_inc(S["hsq_done"], 1)
            for b in range(2):
                act.wait_ge(S["hms_done"], b + 1)
                act.activation(sgT[:, 2 * b:2 * b + 2, :], b2(4 + b), ACT.Sqrt, bias=EPS_H
                               ).then_inc(S["hstd_done"], 1)
            mod_row(MOD_A + MOD_S5 + 3)

            def norm(i):
                for b in range(4):
                    act.wait_ge(S["cen_done"], 4 * i + b + 1)
                    act.activation(sqT[:, 2 * b:2 * b + 2, :], rT[:, 2 * b:2 * b + 2, :], ACT.Square
                                   ).then_inc(S["sq_done"], 1)
                act.wait_ge(S["var_done"], i + 1)
                act.activation(std[:, 0, :], bank[:, 5, 0:TOK], ACT.Sqrt, bias=EPS_LN).then_inc(S["std_done"], 1)
                for b in range(4):
                    act.wait_ge(S["norm_done"], 4 * i + b + 1)
                    for ch in (2 * b, 2 * b + 1):
                        act.activation(hT[:, ch, :], rT[:, ch, :], ACT.Identity, scale=coef[:, i, 0, ch:ch + 1],
                                       bias=coef[:, i, 1, ch:ch + 1]).then_inc(S["h_ready"], 1)

            def high(layer, it, e2, i):
                if i == 0:
                    for k in range(2):
                        n = MOE_AT[layer] + 3 * e2 + k
                        act.wait_ge(landed[n % RING], it * 16 + 16 * (n // RING + 1))
                elif i == 2:
                    n = MOE_AT[layer] + 3 * e2 + 2
                    act.wait_ge(landed[n % RING], it * 16 + 16 * (n // RING + 1))
                act.wait_ge(S["block_done"], it * 6 + (3 * (NE * layer + e2) + i + 1))
                for g in range(2):
                    dst, src = block_part(whi, MOE_AT[layer] + 3 * e2, i, g)
                    act.activation(dst, src, ACT.Copy).then_inc(S["whi_done"], 1)

            def first_weights(layer):
                act.wait_ge(S["yb_done"], 4 * layer + 4)
                for i in range(2):
                    if layer:
                        act.wait_ge(used, used_at(ML_OUT) + 2 + i + 1)
                    high(layer, 0, 0, i)

            def mix_high(i):
                n = ML_IN + i
                act.wait_ge(landed[n % RING], 16 * (n // RING + 1))
                if i < 2:
                    act.wait_ge(S["block_done"], 3 + 3 * (NE - 1) + i + 1)
                else:
                    act.wait_ge(used, used_at(ML_IN) + i - 1)
                for half in range(2):
                    dst, src = mix_part(whi, i, half)
                    act.activation(dst, src, ACT.Copy).then_inc(S["mix_hi"], 1)

            def moe(layer):
                act.wait_ge(S["logit_done"], layer + 1)
                act.activation(affT[:, :], bank[0:NE, 6, 0:TOK], ACT.Sigmoid).then_inc(S["aff_done"], 1)

                def halves(it, e2, half):
                    u = 2 * e2 + half
                    n = 32 * layer + u
                    act.wait_ge(S["block_done"], it * 6 + (3 * (NE * layer + e2) + half + 4))
                    act.wait_ge(S["prod_done"], it * 4 + (n + 1))
                    act.activation(sil[:, u % 2, :], bank[:, 4 + u % 2, 0:TOK], ACT.Silu
                                   ).then_inc(S["sil_done"], 1)

                def part(it, e2, half):
                    n = 32 * layer + 2 * e2 + half
                    act.wait_ge(S["ef_done"], it * 4 + (n + 3))
                    act.wait_ge(S["block_done"], it * 6 + (3 * (NE * layer + e2) + 2))
                    act.activation(ehi[:, e2, half, :], ef[:, half, :], ACT.Copy).then_inc(S["ehi_done"], 1)

                def two(it, last=False):
                    for e2 in range(2):
                        halves(it, e2, 0)
                        part(it, e2, 0)
                        if e2 == 0:
                            high(layer, it, 1, 0)
                        elif not last:
                            high(layer, it + 1, 0, 0)
                        halves(it, e2, 1)
                        part(it, e2, 1)
                        if e2 == 0:
                            high(layer, it, 1, 1)
                            high(layer, it, 1, 2)
                        elif not last:
                            high(layer, it + 1, 0, 1)
                            high(layer, it + 1, 0, 2)

                high(layer, 0, 0, 2)
                act.wait_ge(S["gt_turned"], layer + 1)
                act.activation(gT[:, :], bank[0:NE, 6, 0:TOK], ACT.Copy).then_inc(S["gt_copied"], 1)
                with act.Fori(0, NE // 2 - 1) as it:
                    two(it)
                two(NE // 2 - 1, last=True)

            first_weights(0)
            norm(0)
            moe(0)
            mix_high(0)
            mix_high(1)
            norm(1)

            act.wait_ge(S["mgate_done"], 1)
            for g in range(2):
                act.activation(mrow[0:MH, g, :], bank[0:MH, 6, g * TOK:(g + 1) * TOK], ACT.Identity,
                               bias=mg_b[:, g:g + 1]).then_inc(S["mgate_x"], 1)
            act.wait_ge(S["mgate_x"], 2)
            link(act.activation(mrow[0:MH, 2, :], mrow[0:MH, 1, :], ACT.Abs))
            link(act.activation(mrow[0:MH, 3, :], mrow[0:MH, 2, :], ACT.Exp, scale=-1.0))
            act.activation(mrow[0:MH, 4, :], mrow[0:MH, 3, :], ACT.Ln, bias=1.0).then_inc(S["mgate_ln"], 1)
            for j in range(16):
                act.wait_ge(used, used_at(ML_IN) + j + 1)
                mix_high(j + 2)
                bk = b2(j % 4)
                if j < 8:
                    if j >= 2:
                        act.wait_ge(S["qk_done"], 2 * (j - 1))
                    for a in range(2):
                        m = 2 * j + a
                        act.activation(cv[:, j % 2, a, :], bk[:, a, :], ACT.Identity,
                                       scale=cols[:, 2, 48 + m:49 + m], bias=vcol(V_CONVB + m)
                                       ).then_inc(S["conv_a"], 1)
                    if j >= 1:
                        for a in range(2):
                            m = 2 * (j - 1) + a
                            act.wait_ge(S["conv_done"], m + 1)
                            act.activation(qk_at(m), cv[:, (j - 1) % 2, a, :], ACT.Silu
                                           ).then_inc(S["qk_done"], 1)
                elif j < 12:
                    if j == 8:
                        for a in range(2):
                            m = 14 + a
                            act.wait_ge(S["conv_done"], m + 1)
                            act.activation(qk_at(m), cv[:, 1, a, :], ACT.Silu).then_inc(S["qk_done"], 1)
                    act.activation(vM[:, :, (j - 8) * SC:(j - 7) * SC], bk, ACT.Copy).then_inc(S["proj_out"], 1)
                else:
                    act.activation(oG[:, 2 * (j - 12):2 * (j - 12) + 2, :], bk, ACT.Sigmoid
                                   ).then_inc(S["proj_out"], 1)
            act.wait_ge(S["mrow_done"], 1)
            act.activation(mrow[0:MH, 2, :], mrow[0:MH, 9, :], ACT.Exp, scale=-1.0).then_inc(S["mfloor_done"], 1)

            def square(hd):
                act.wait_ge(S["mnum_done"], hd + 1)
                if hd >= 2:
                    act.wait_ge(S["mmean_done"], hd - 1)
                act.activation(numsq[:, hd % 2, :], bank[:, 4 + hd % 2, 0:TOK], ACT.Square
                               ).then_inc(S["mnumsq_done"], 1)

            for hd in range(MH):
                q = hd % 2
                act.wait_ge(S["md_done"], 2 * hd + 2)
                if hd >= 2:
                    act.wait_ge(S["ms_done"], hd - 1)
                act.activation(eM[:, q, :], dM[:, q, :], ACT.Exp, scale=-1.0).then_inc(S["me_done"], 1)
                if hd >= 2:
                    square(hd - 2)
            square(MH - 2)
            square(MH - 1)
            act.wait_ge(S["mvar_done"], 1)
            act.activation(mrow[0:MH, 11, :], mrow[0:MH, 10, :], ACT.Sqrt).then_inc(S["msqrt_done"], 1)
            for b in range(4):
                act.wait_ge(S["yb_done"], 4 + b + 1)
                act.activation(yhi[:, 2 * b:2 * b + 2, :], yT[:, 2 * b:2 * b + 2, :], ACT.Copy
                               ).then_inc(S["yhi_done"], 1)
            mix_high(18)
            mix_high(19)
            first_weights(1)
            norm(2)
            moe(1)
            norm(3)
            for b in range(4):
                act.wait_ge(S["final_turned"], b + 1)
                act.activation(sqT[:, 2 * b:2 * b + 2, :], b2(b), ACT.Copy).then_inc(S["final_out"], 1)

        @block.vector
        def _(dve):
            step = [0]

            def link(ins):
                step[0] += 1
                ins.then_inc(S["dve_step"], 1)
                dve.wait_ge(S["dve_step"], step[0])

            tt, ts, stt = dve.tensor_tensor, dve.tensor_scalar, dve.scalar_tensor_tensor
            lre, lim, lrd, ang, mag, are, sn, cs, nre, sh, kk, t0, t1, cre, cim, rdn = (
                s5p[:, i, :] for i in range(16))
            dtb = bc(s5dt[:, 1, :].rearrange("j (g a) -> j g a", a=1), 16, 2, 64)
            g2 = lambda a: a.rearrange("j (g p) -> j g p", g=2)

            dve.nop().then_inc(S["prod_done"], 2)
            dve.nop().then_inc(S["he_done"], 2)
            dve.nop().then_inc(S["ef_done"], 2)
            dve.wait_ge(S["tables_ready"], 1)
            tt(g2(lrd), g2(lre), dtb, ALU.mult).then_inc(S["tables_ready"], 1)
            link(tt(g2(ang), g2(lim), dtb, ALU.mult))
            link(ts(kk, ang, 1.0 / (2.0 * np.pi), ROUND, ALU.mult, ALU.add))
            link(ts(kk, kk, ROUND, None, ALU.subtract))
            for part in TWO_PI:
                link(stt(ang, kk, -part, ang, ALU.mult, ALU.add))
            dve.wait_ge(S["tables_ready"], 3)
            ts(ang, ang, PI_BELOW, -PI_BELOW, ALU.min, ALU.max).then_inc(S["tables_ready"], 1)
            dve.wait_ge(S["tables_ready"], 6)
            link(tt(cs, sh, sh, ALU.mult))
            link(ts(cs, cs, -2.0, 1.0, ALU.mult, ALU.add))
            link(tt(are, mag, cs, ALU.mult))
            link(ts(nre, are, 1.0, None, ALU.subtract))
            link(tt(are, mag, sn, ALU.mult))
            link(tt(t0, lre, lre, ALU.mult))
            link(tt(t1, lim, lim, ALU.mult))
            link(tt(t0, t0, t1, ALU.add))
            link(dve.reciprocal(rdn, t0))
            link(tt(t0, nre, lre, ALU.mult))
            link(tt(t1, are, lim, ALU.mult))
            link(tt(t0, t0, t1, ALU.add))
            link(tt(cre, t0, rdn, ALU.mult))
            link(tt(t0, are, lre, ALU.mult))
            link(tt(t1, nre, lim, ALU.mult))
            link(tt(t0, t0, t1, ALU.subtract))
            tt(cim, t0, rdn, ALU.mult).then_inc(S["bb_done"], 1)

            def mod_products(n, acc_at, done_before, it=0):
                slot = mring[:, n % MRING, :].rearrange("p (c n) -> p c n", c=DC)
                acc = macc[:, acc_at, :]
                for k in range(DC):
                    if k == 0:
                        ins = ts(acc, slot[:, 0, :], c_col[:, 1, 0:1], None, ALU.mult)
                    else:
                        ins = stt(acc, slot[:, k, :], c_col[:, 1, k:k + 1], acc, ALU.mult, ALU.add)
                    if k == DC - 1:
                        ins.then_inc(mod_dve_used, 1)
                    else:
                        ins.then_inc(S["macc_step"], 1)
                        dve.wait_ge(S["macc_step"], it * (2 * (DC - 1)) + ((DC - 1) * done_before + k + 1))

            def mod_slot(i):
                n = MOD_A + MOD_S5 + MRING * i + 1
                dve.wait_ge(mlanded[n % MRING], 16 * (n // MRING + 1))
                if i >= 2:
                    dve.wait_ge(S["mcol_out"], n - 2 * MRING + 1)
                mod_products(n, i % 2, i)

            def mod_slot_moe(it, m):
                dve.wait_ge(mlanded[m], it * 16 + 16 * (MOD_0 // MRING + 1))
                dve.wait_ge(S["mcol_out"], it * MRING + (MOD_0 + m + 1 - MRING))
                mod_products(MOD_0 + m, m, MOD_GLA + m, it)

            def modulation(layer, parts, done):
                dve.wait_ge(S["mcol_out"], done)
                a, b = 8 * parts[0], 8 * parts[-1] + 8
                link(tt(mod[:, layer, a:b], bank[:, 7, 48 * layer + a:48 * layer + b],
                        cols[:, 0, 48 * layer + a:48 * layer + b], ALU.add))
                for q in (SC1, G1, SC2, G2):
                    if q in parts:
                        m = mod[:, layer, 8 * q:8 * q + 8]
                        link(ts(m, m, 1.0, None, ALU.add))

            dve.wait_ge(S["s5_turned"], 1)
            dve.tensor_copy(s5c[:, :, :], bank[:, 5, 0:5 * ST].rearrange("p (a j) -> p a j", a=5)
                            ).then_inc(S["s5c_ready"], 1)
            dve.wait_ge(S["s5c_ready"], 1)

            def matrices():
                dve.wait_ge(S["cols_turned"], 1)
                dve.tensor_copy(cols[:, 0, 0:96], bank[:, 6, 0:96])
                dve.tensor_copy(cols[:, 1, 0:V_END], bank[:, 6, P:P + V_END])
                dve.tensor_copy(cols[:, 2, 0:64], bank[:, 6, 2 * P:2 * P + 64]).then_inc(S["cols_ready"], 1)
                dve.wait_ge(S["cols_ready"], 1)
                modulation(0, (SH1, SC1), MOD_A)
                dve.nop().then_inc(S["mod_ready"], 1)
                link(dve.memset(bb[:, :, :, :], 0.0))
                dve.wait_ge(S["bc_loaded"], 96)
                coef_b = [bc(s5c[:, 3 + i, :].rearrange("p (j a) -> p j a", a=1), P, ST, S5_G) for i in range(2)]
                for i, (a, b) in enumerate(((0, 0), (1, 1), (0, 1), (1, 0))):
                    link(tt(bt[:, i, :, :], b_raw[:, b, :, :], coef_b[a], ALU.mult))
                for i, op in ((0, ALU.subtract), (1, ALU.add)):
                    for g in range(2):
                        ps = slice(64 * g, 64 * g + 64)
                        link(tt(bb[ps, i, :, 16 * g:16 * g + 16], bt[ps, 2 * i, :, :], bt[ps, 2 * i + 1, :, :], op))
                dve.nop().then_inc(S["bb_done"], 1)
                link(dve.memset(ctT[:, :, :, :], 0.0))
                for i, sign in ((0, 1.0), (1, -1.0)):
                    dve.wait_ge(S["ct_turned"], i + 1)
                    for g in range(2):
                        ps = slice(64 * g, 64 * g + 64)
                        src = bank[ps, i, :].rearrange("p (j g c) -> p j g c", g=2, c=16)[:, :, g, :]
                        ins = ts(ctT[ps, i, :, 16 * g:16 * g + 16], src, sign, None, ALU.mult)
                    ins.then_inc(S["ct_ready"], 1)

            doubling(dve, link, 0, TABLE_DVE, en, tmp_dve, matrices)
            for i in range(2):
                dve.wait_ge(S["bb_turned"], i + 1)
                dve.tensor_copy(bbT[:, i, :, :], bank[:, 2 + i, :].rearrange("p (k n) -> p k n", k=UC)
                                ).then_inc(S["bbT_ready"], 1)

            dve.wait_ge(S["h_ready"], 8)
            dve.wait_ge(S["ax_ready"], 8)

            def log_decay():
                dve.wait_ge(S["gate_ln"], 1)
                link(stt(cum[:, :, :], cum[:, :, :], 0.0, kd[:, 0, :, :], ALU.min, ALU.subtract))
                for ch in range(QC):
                    dve.tensor_tensor_scan(qd[:, 0, ch, :], bc(ones[:, 0:1], P, TOK), cum[:, ch, :], 0.0,
                                           ALU.mult, ALU.add).then_inc(S["cum_done"], 1)
                dve.wait_ge(S["cum_done"], 2)
                link(dve.tensor_copy(cum[:, :, :], qd[:, 0, :, :]))

            def rot1(j):
                dve.wait_ge(S["bu_done"], j + 1)
                if j == TABLE_DVE:
                    dve.wait_ge(S["tables_done"], 1)
                if j >= 2:
                    dve.wait_ge(S["vin_done"], j - 1)
                for i, t in enumerate((cosT, sinT)):
                    tb = bc(t[:, j, :].rearrange("p (a t) -> p a t", a=1), P, 2, TOK)
                    tt(rot[:, j % 2, i, :, :], b2(4 + j % 2), tb, ALU.mult).then_inc(S["rot1_done"], 1)

            def scans(j):
                dve.wait_ge(S["vin_done"], j + 1)
                if j:
                    dve.wait_ge(S["rot2_done"], 2 * j)
                for i in range(2):
                    dve.tensor_tensor_scan(zst[:, i, :], bc(s5c[:, 0, j:j + 1], P, TOK), vin[:, j % 2, i, :],
                                           0.0, ALU.mult, ALU.add).then_inc(S["scan_done"], 1)
                dve.wait_ge(S["scan_done"], 2 * j + 2)
                if j >= 1:
                    dve.wait_ge(S["sst_done"], j)
                for i, t in enumerate((cosT, sinT)):
                    tb = bc(t[:, j, :].rearrange("p (a t) -> p a t", a=1), P, 2, TOK)
                    tt(rotp[:, i, :, :], zst[:, :, :], tb, ALU.mult).then_inc(S["rot2_done"], 1)

            def skip(k):
                dve.wait_ge(S["ys_done"], 4 * k + 4)
                stt(yy[:, k, :], uT[:, k, :], vcol(V_D + k), b2(YS_BANK[k])[:, 1, :], ALU.mult, ALU.add
                    ).then_inc(S["yy_done"], 1)

            for j in range(ST + 1):
                if j == 2:
                    log_decay()
                if j < ST:
                    rot1(j)
                if j >= 1:
                    scans(j - 1)
                    if j - 1 >= 4 and (j - 1) % 4 == 1:
                        skip((j - 1) // 4 - 1)
            skip(UC - 1)

            dve.wait_ge(S["rot2_done"], 2 * ST)
            link(dve.memset(attD[:, :, :, :, :], 0.0))

            def level_dif(lv):
                h = 1 << lv
                if lv >= 2:
                    dve.wait_ge(S["dec_done"], 2 * (lv - 1))
                m5 = cum.rearrange("p c (n h) -> p (c n) h", h=2 * h)
                ref = bc(m5[:, :, h - 1:h], P, QC * TOK // (2 * h), 2 * h)
                o5 = dif[:, lv % 2, :, :].rearrange("p c (n h) -> p (c n) h", h=2 * h)
                tt(o5, m5, ref, ALU.subtract).then_inc(S["dif_done"], 1)

            def level_out(n, lv):
                for par in range(2):
                    dve.wait_ge(S["att_done"], 2 * n + par + 1)
                    if n:
                        dve.wait_ge(S["att_out"], 2 * n + par - 1)
                    src = bank[:, 2 * (n % 2) + par, :].rearrange("p (b t) -> p b t", t=P)
                    if lv == LEVELS - 1 and n < LEVELS:
                        dve.tensor_copy(attX[:, par, :, :], src[:, 0:2, :]).then_inc(S["att_out"], 1)
                    else:
                        mask = bc(level_mask[:, lv, :].rearrange("p (a t) -> p a t", a=1), P, 4, P)
                        dve.copy_predicated(attD[:, par, :, :, :].rearrange("p a b t -> p (a b) t"), mask, src
                                            ).then_inc(S["att_out"], 1)

            level_dif(0)
            for lv in range(LEVELS):
                if lv + 1 < LEVELS:
                    level_dif(lv + 1)
                if lv in ROUND_AT:
                    mod_slot(ROUND_AT[lv])
                if lv == 3:
                    for k in range(UC):
                        dve.wait_ge(S["glu_sig"], k + 1)
                        tt(yT[:, k, :], zT[:, k, :], sgT[:, k, :], ALU.mult).then_inc(S["ya_done"], 1)
                level_out(lv, lv)
            level_out(LEVELS, LEVELS - 1)

            modulation(0, (G1,), MOD_A + MOD_S5 + 2 * MRING)

            for b in range(2):
                dve.wait_ge(S["hstd_done"], b + 1)
                link(dve.reciprocal(sgT[:, 2 * b:2 * b + 2, :], sgT[:, 2 * b:2 * b + 2, :]))
                link(tt(oT[:, 2 * b:2 * b + 2, :], oT[:, 2 * b:2 * b + 2, :], sgT[:, 2 * b:2 * b + 2, :], ALU.mult))
                for k in (2 * b, 2 * b + 1):
                    stt(yT[:, UC + k, :], oT[:, k, :], vcol(V_GNORM + k), rS[:, k, :], ALU.mult, ALU.mult
                        ).then_inc(S["yb_done"], 1)

            def norm(i, beside=None):
                layer, second = i // 2, i % 2
                dve.wait_ge(S["ax_ready"], 8 * i + 8)
                dve.wait_ge(S["h_ready"], 8 * i + 8)
                for ch in range(DC):
                    if not second:
                        if ch % 2 == 0:
                            dve.wait_ge(used, used_at(ML_OUT if layer else AB_OUT) + ch // 2 + 1)
                    elif ch == 0:
                        dve.wait_ge(S["block_done"], 3 + 3 * NE * (layer + 1))
                    stt(rT[:, ch, :], b2(ch // 2)[:, ch % 2, :], mcol(layer, G2 if second else G1, ch),
                        axT[:, ch, :], ALU.mult, ALU.add).then_inc(S["r_done"], 1)
                dve.wait_ge(S["mean_done"], i + 1)
                mb = bc(bank[:, 4, 0:TOK].rearrange("p (a t) -> p a t", a=1), P, 2, TOK)
                for b in range(4):
                    v = rT[:, 2 * b:2 * b + 2, :]
                    tt(v, v, mb, ALU.subtract).then_inc(S["cen_done"], 1)
                if beside:
                    beside()
                gain, shift = (LN_G2, LN_B2) if second else (LN_G1, LN_B1)
                gv = cols[:, 1, gain + 8 * layer:gain + 8 * layer + 8]
                bv = cols[:, 1, shift + 8 * layer:shift + 8 * layer + 8]
                if i < 3:
                    nl, sc, sh_ = (layer, SC2, SH2) if not second else (layer + 1, SC1, SH1)
                    scv = mod[:, nl, 8 * sc:8 * sc + 8]
                    link(tt(coef[:, i, 0, :], gv, scv, ALU.mult))
                    link(tt(coef[:, i, 1, :], bv, scv, ALU.mult))
                    link(tt(coef[:, i, 1, :], coef[:, i, 1, :], mod[:, nl, 8 * sh_:8 * sh_ + 8], ALU.add))
                    link(ts(coef[:, i, 2, :], gv, ALPHA, None, ALU.mult))
                    ts(coef[:, i, 3, :], bv, ALPHA, None, ALU.mult).then_inc(S["coef_ready"], 1)
                else:
                    link(dve.tensor_copy(coef[:, i, 0, :], gv))
                    dve.tensor_copy(coef[:, i, 1, :], bv).then_inc(S["coef_ready"], 1)
                dve.wait_ge(S["std_done"], i + 1)
                link(dve.reciprocal(std[:, 1, :], std[:, 0, :]))
                sb_ = bc(std[:, 1, :].rearrange("p (a t) -> p a t", a=1), P, 2, TOK)
                for b in range(4):
                    v = rT[:, 2 * b:2 * b + 2, :]
                    tt(v, v, sb_, ALU.mult).then_inc(S["norm_done"], 1)

            def low(layer, it, e2, i):
                for g in range(2):
                    dve.wait_ge(S["whi_done"], it * 12 + (6 * (NE * layer + e2) + 2 * i + g + 1))
                    dst, src = block_part(wlo, MOE_AT[layer] + 3 * e2, i, g)
                    hi, _ = block_part(whi, MOE_AT[layer] + 3 * e2, i, g)
                    tt(dst, src, hi.bitcast(F32), ALU.subtract).then_inc(S["wlo_done"], 1)
                if i == 1:
                    dve.wait_ge(S["wlo_done"], it * 8 + (4 * (NE * layer + e2) + 4))
                    dve.nop().then_inc(gu_used, 1)

            def input_parts(i):
                for b in range(4):
                    v = slice(2 * b, 2 * b + 2)
                    dve.wait_ge(S["h_ready"], 8 * (i + 1) + 2 * b + 2)
                    dve.tensor_copy(hhi[:, v, :], hT[:, v, :]).then_inc(S["hhi_done"], 1)
                    dve.wait_ge(S["hhi_done"], 4 * i + b + 1)
                    tt(hlo[:, v, :], hT[:, v, :], hhi[:, v, :].bitcast(F32), ALU.subtract).then_inc(S["hlo_done"], 1)

            def mix_low(i):
                dve.wait_ge(S["mix_hi"], 2 * i + 1)
                dst, src = mix_part(wlo, i, 0)
                tt(dst, src, mix_part(whi, i, 0)[0].bitcast(F32), ALU.subtract).then_inc(S["mix_lo_dve"], 1)

            def moe(layer):
                input_parts(2 * layer)
                dve.wait_ge(S["aff_turned"], layer + 1)
                aff = rt[:, 0, 0:TT * NE]
                link(dve.tensor_copy(aff, bank[:, 6, 0:TT * NE]))
                sel, one, two, gates = (rt[:, i, 0:TT * NE] for i in (1, 2, 3, 4))
                psum_ = pair6[:, :, :]
                score, best, key, chosen = (rt[:, i, 0:TT * NG] for i in (6, 7, 8, 9))
                kmax, tot = (rt[:, i, 0:TT] for i in (10, 11))
                order = rt[:, 12, 0:NG]
                v4 = lambda a: a.rearrange("p (q e) -> p q e", e=EG)
                vg = lambda a: a.rearrange("p (a g) -> p a g", g=NG)
                for g in range(NG):
                    link(dve.memset(order[:, g:g + 1], float(NG - g)))
                link(tt(sel.rearrange("p (a e) -> p a e", e=NE), aff.rearrange("p (a e) -> p a e", e=NE),
                        bc(rbias[:, :].rearrange("p (a e) -> p a e", a=1), P, TT, NE), ALU.add))
                s4 = v4(sel)
                at = 0
                for d in range(1, EG):
                    link(tt(psum_[:, :, at:at + EG - d], s4[:, :, 0:EG - d], s4[:, :, d:EG], ALU.add))
                    at += EG - d
                link(dve.tensor_reduce(score, psum_, AX.X, ALU.max))
                link(dve.tensor_reduce(kmax, vg(score), AX.X, ALU.max))
                link(tt(vg(best), vg(score), bc(kmax.rearrange("p (a g) -> p a g", g=1), P, TT, NG), ALU.is_equal))
                link(tt(vg(key), vg(best), bc(order.rearrange("p (a g) -> p a g", a=1), P, TT, NG), ALU.mult))
                link(dve.tensor_reduce(kmax, vg(key), AX.X, ALU.max))
                link(tt(vg(chosen), vg(key), bc(kmax.rearrange("p (a g) -> p a g", g=1), P, TT, NG), ALU.is_equal))
                cmp_ = pairs[:, 0, :, :, :].rearrange("p a q e -> p (a q e)").rearrange(
                    "p (q i j) -> p q i j", i=EG, j=EG)
                eq_ = pairs[:, 1, :, :, :].rearrange("p a q e -> p (a q e)").rearrange(
                    "p (q i j) -> p q i j", i=EG, j=EG)
                Q = TT * NG
                sj = bc(s4.rearrange("p q (i j) -> p q i j", i=1), P, Q, EG, EG)
                si = bc(s4.rearrange("p q (i j) -> p q i j", j=1), P, Q, EG, EG)
                link(tt(cmp_, sj, si, ALU.is_gt))
                for i in range(1, EG):
                    link(tt(eq_[:, :, i, 0:i], sj[:, :, i, 0:i], si[:, :, i, 0:i], ALU.is_equal))
                    link(tt(cmp_[:, :, i, 0:i], cmp_[:, :, i, 0:i], eq_[:, :, i, 0:i], ALU.add))
                link(dve.tensor_reduce(one, cmp_, AX.X, ALU.add))
                link(ts(one, one, 2.0, None, ALU.is_lt))
                link(tt(v4(one), v4(one), bc(chosen.rearrange("p (q e) -> p q e", e=1), P, Q, EG), ALU.mult))
                link(tt(two, one, aff, ALU.mult))
                link(dve.tensor_reduce(tot, two.rearrange("p (a e) -> p a e", e=NE), AX.X, ALU.add))
                link(dve.reciprocal(tot, tot))
                tt(gates.rearrange("p (a e) -> p a e", e=NE), two.rearrange("p (a e) -> p a e", e=NE),
                   bc(tot.rearrange("p (a e) -> p a e", e=1), P, TT, NE), ALU.mult).then_inc(S["gates_done"], 1)

                dve.wait_ge(S["gt_copied"], layer + 1)
                dve.wait_ge(S["ax_ready"], 8 * (2 * layer + 2))
                dve.wait_ge(S["h_ready"], 8 * (2 * layer + 2))
                own_gates(dve, 0, 2).then_inc(S["gsel_done"], 1)

                def gated(it, e2, half):
                    n = 32 * layer + 2 * e2 + half
                    dve.wait_ge(S["sil_done"], it * 4 + (n + 1))
                    dve.wait_ge(S["ef_done"], it * 4 + (n + 1))
                    tt(pr[:, half, :], bank[:, 4 + half, TOK:2 * TOK], sil[:, half, :], ALU.mult
                       ).then_inc(S["prod_done"], 1)
                    dve.wait_ge(S["prod_done"], it * 4 + (n + 3))
                    dve.wait_ge(S["gb_done"], it + (8 * layer + 1))
                    dve.wait_ge(S["he_done"], it * 4 + (n + 1))
                    tt(ef[:, half, :], pr[:, half, :], b2(6)[:, e2, :], ALU.mult).then_inc(S["ef_done"], 1)

                def gated_low(it, e2, half):
                    n = 32 * layer + 2 * e2 + half
                    dve.wait_ge(S["ehi_done"], it * 4 + (n + 1))
                    tt(elo[:, e2, half, :], ef[:, half, :], ehi[:, e2, half, :].bitcast(F32), ALU.subtract
                       ).then_inc(S["he_done"], 1)

                def two(it, last=False):
                    for e2 in range(2):
                        gated(it, e2, 0)
                        gated_low(it, e2, 0)
                        if e2 == 0:
                            low(layer, it, 1, 0)
                        elif not last:
                            low(layer, it + 1, 0, 0)
                        elif layer == 0:
                            mod_slot_moe(it, 1)
                        gated(it, e2, 1)
                        gated_low(it, e2, 1)
                        if e2 == 0:
                            low(layer, it, 1, 1)
                        elif not last:
                            low(layer, it + 1, 0, 1)
                        if layer == 0 and not (last and e2):
                            mod_slot_moe(it, e2)

                with dve.Fori(0, NE // 2 - 1) as it:
                    two(it)
                two(NE // 2 - 1, last=True)

            mod_slot(2)
            mod_slot(3)
            low(0, 0, 0, 0)
            low(0, 0, 0, 1)

            def rest_of_modulation():
                modulation(0, (SH2, SC2, G2), MOD_0)

            norm(0, rest_of_modulation)
            moe(0)

            def before_mixer():
                modulation(1, (SH1, SC1, G1, SH2, SC2, G2), 48)
                mix_low(0)
                mix_low(1)

            norm(1, before_mixer)
            input_parts(1)

            R = [mrow[0:MH, i, :] for i in range(12)]
            dve.wait_ge(S["mgate_ln"], 1)
            link(stt(R[5], R[1], 0.0, R[4], ALU.min, ALU.subtract))
            link(dve.tensor_tensor_scan(R[6], bc(ones[0:MH, 0:1], MH, TOK), R[5], 0.0, ALU.mult, ALU.add))
            link(tt(R[7], R[0], R[6], ALU.subtract))
            link(dve.tensor_tensor_scan(R[8], R[7], R[7], 0.0, ALU.max, ALU.max))
            tt(R[9], R[8], R[6], ALU.add).then_inc(S["mrow_done"], 1)
            mix_low(2)
            dve.wait_ge(S["mcol_turned"], 1)
            dve.tensor_copy(ccol[:, :, :], bank[:, 6, 0:TT * MH].rearrange("p (a h) -> p a h", a=TT)
                            ).then_inc(S["mcol_done"], 1)
            for j in range(8):
                if j:
                    mix_low(j + 2)
                for a in range(2):
                    m = 2 * j + a
                    dve.wait_ge(S["conv_a"], 2 * j + 2)
                    o = cv[:, j % 2, a, :]
                    src = b2(j % 4)[:, a, :]
                    for tap in range(CW - 2, -1, -1):
                        d = CW - 1 - tap
                        ins = stt(o[:, d:TOK], src[:, 0:TOK - d], cols[:, 2, 16 * tap + m:16 * tap + m + 1],
                                  o[:, d:TOK], ALU.mult, ALU.add)
                        if tap:
                            link(ins)
                    ins.then_inc(S["conv_done"], 1)
            for i in range(10, 18):
                mix_low(i)

            def log_weights(hd):
                q = hd % 2
                dve.wait_ge(S["mb_done"], hd + 1)
                if hd >= 2:
                    dve.wait_ge(S["me_done"], hd - 1)
                src = bank[:, q, 0:384]
                ts(dM[:, q, 0:TOK], src[:, 0:TOK], ccol[:, 0, hd:hd + 1], 0.0, ALU.subtract, ALU.max
                   ).then_inc(S["md_done"], 1)
                ts(dM[:, q, TOK:384], src[:, TOK:384], ccol[:, 1, hd:hd + 1], 0.0, ALU.subtract, ALU.max
                   ).then_inc(S["md_done"], 1)

            def weighted(hd):
                q = hd % 2
                dve.wait_ge(S["me_done"], hd + 1)
                dve.wait_ge(S["mqk_done"], hd + 1)
                if hd >= 2:
                    dve.wait_ge(S["mnum_done"], hd - 1)
                stt(sM[:, q, :], bank[:, 2 + q, 0:384], float(P) ** -0.5, eM[:, q, :], ALU.mult, ALU.mult
                    ).then_inc(S["ms_done"], 1)

            def gained(hd):
                dve.wait_ge(S["mnumsq_done"], hd + 1)
                stt(hh[:, hd, :], bank[:, 4 + hd % 2, 0:TOK], vcol(V_MNORM + hd), oG[:, hd, :], ALU.mult, ALU.mult
                    ).then_inc(S["mh_done"], 1)

            for i in range(MH + 3):
                if i < MH:
                    log_weights(i)
                if 1 <= i <= MH:
                    weighted(i - 1)
                if i >= 3:
                    gained(i - 3)
            dve.wait_ge(S["mfloor_done"], 1)
            link(stt(R[10], bank[0:MH, 6, 0:TOK], -1.0, R[2], ALU.mult, ALU.max))
            link(tt(R[10], bank[0:MH, 6, 0:TOK], R[10], ALU.max))
            link(stt(R[11], R[10], EPS_H, R[10], ALU.mult, ALU.mult))
            dve.wait_ge(S["mmean_done"], MH)
            link(stt(R[10], bank[0:MH, 7, 0:TOK], 1.0 / P, R[11], ALU.mult, ALU.add))
            ts(R[10], R[10], TINY, None, ALU.max).then_inc(S["mvar_done"], 1)
            dve.wait_ge(S["msqrt_done"], 1)
            dve.reciprocal(R[3], R[11]).then_inc(S["mscale_done"], 1)
            dve.wait_ge(S["mh_done"], MH)
            for b in range(5):
                if b < 4:
                    v = slice(2 * b, 2 * b + 2)
                    dve.wait_ge(S["mscaleb_done"], b + 1)
                    tt(yT[:, v, :], hh[:, v, :], b2(b), ALU.mult).then_inc(S["yb_done"], 1)
                if b:
                    v = slice(2 * b - 2, 2 * b)
                    dve.wait_ge(S["yhi_done"], b)
                    tt(ylo[:, v, :], yT[:, v, :], yhi[:, v, :].bitcast(F32), ALU.subtract).then_inc(S["ylo_done"], 1)
            mix_low(18)
            mix_low(19)
            low(1, 0, 0, 0)
            low(1, 0, 0, 1)
            norm(2)
            moe(1)
            norm(3)

        @block.tensor
        def _(pe):
            mm = pe.matmul

            def mod_rows(n, halves=(0, 1)):
                slot_n = mod_own(n)
                slot = mring[:, slot_n % MRING, :].rearrange("p (c n) -> p c n", c=DC)
                pe.wait_ge(mlanded[slot_n % MRING], 16 * (slot_n // MRING + 1))
                if n >= 2:
                    pe.wait_ge(S["mod_row_out"], n - 1)
                ps = slice(32 * (n % 2), 32 * (n % 2) + 1)
                for half in halves:
                    for k in range(4 * half, 4 * half + 4):
                        ins = mm(bank[ps, row_bank(n), TOK:TOK + SC], c_col[:, 1, k:k + 1], slot[:, k, :],
                                 start=(k == 0), stop=(k == DC - 1))
                if halves[-1]:
                    ins.then_inc(mod_pe_used, 1)

            def mod_turn(n):
                slot_n = mod_own(n)
                ps = slice(32 * (n % 2), 32 * (n % 2) + 1)
                pe.wait_ge(S["mod_row_out"], n + 1)
                for a in range(2):
                    ins = mm(bank[:, 7, 2 * slot_n + a:2 * slot_n + a + 1], mrows[ps, a * P:(a + 1) * P],
                             ones[ps, 0:1], start=True, stop=True)
                ins.then_inc(S["mcol_out"], 1)
                pe.wait_ge(S["mcol_out"], slot_n + 1)
                pe.nop().then_inc(S["mod_row_used"], 1)

            def mod_sum(i, m):
                n = MOD_A + MOD_S5 + MRING * i + m
                pe.wait_ge(mod_dve_used if m == 1 else mod_pool_used, i + 1)
                for a in range(2):
                    ins = mm(bank[:, 7, 2 * n + a:2 * n + a + 1],
                             macc[:, i % 2 if m == 1 else 2, a * P:(a + 1) * P], ones[:, 0:1], start=True, stop=True)
                ins.then_inc(S["mcol_out"], 1)

            def mod_columns(i):
                mod_turn(MOD_A + MOD_S5 + i)
                mod_sum(i, 1)
                mod_sum(i, 2)

            def mod_sum_moe(it, m):
                if m < 2:
                    pe.wait_ge(mod_dve_used, it * 2 + (MOD_GLA + m + 1))
                else:
                    pe.wait_ge(mod_pool_used, it + (MOD_GLA + 1))
                for a in range(2):
                    ins = mm(bank[:, 7, bass.ds(it * (2 * MRING) + (2 * (MOD_0 + m) + a), 1)],
                             macc[:, m, a * P:(a + 1) * P], ones[:, 0:1], start=True, stop=True)
                ins.then_inc(S["mcol_out"], 1)

            def x_turns():
                pe.wait_ge(S["ident_ready"], 1)
                pe.wait_ge(S["x_loaded"], 16)
                xin = sqT[:, :, :].rearrange("p (a b) t -> p a (b t)", a=TT)
                for b in range(4):
                    for ch in (2 * b, 2 * b + 1):
                        for t in range(TT):
                            ins = pe.transpose(b2(b)[:, ch % 2, t * P:(t + 1) * P], xin[:, t, ch * P:(ch + 1) * P],
                                               ident[:, :])
                    ins.then_inc(S["x_turned"], 1)

            def cols_turns():
                pe.wait_ge(S["rows_loaded"], 16 * 13)
                for i, n in enumerate((96, V_END, 64)):
                    ins = pe.transpose(bank[:, 6, i * P:i * P + n], rows[0:n, i, :], ident[0:n, 0:n])
                ins.then_inc(S["cols_turned"], 1)

            def s5_turns():
                pe.wait_ge(S["bb_done"], 1)
                for i, row in enumerate((4, 7, 6, 13, 14)):
                    ins = pe.transpose(bank[:, 5, i * ST:(i + 1) * ST], s5p[:, row, :], ident[0:ST, 0:ST])
                ins.then_inc(S["s5_turned"], 1)

            def ct_turns():
                pe.wait_ge(S["bc_loaded"], 96)
                pe.wait_ge(S["xT_ready"], 4)
                for i in range(2):
                    for k in range(UC):
                        ins = pe.transpose(bank[:, i, k * P:(k + 1) * P], c_raw[:, i, k, :], ident[:, :])
                    ins.then_inc(S["ct_turned"], 1)

            pe.nop().then_inc(S["block_done"], 3)
            pe.wait_ge(S["c_ready"], 1)
            for n in range(MOD_A):
                mod_rows(n)
                if n:
                    pe.wait_ge(S["ident_ready"], 1)
                    mod_turn(n - 1)
                if n == 1:
                    s5_turns()
                    x_turns()
                elif n == 2:
                    cols_turns()
            mod_turn(MOD_A - 1)
            ct_turns()
            pe.wait_ge(S["pool_const"], 1)
            pe.wait_ge(S["cols_ready"], 1)
            pe.wait_ge(S["small_loaded"], 112)
            pe.wait_ge(S["h_ready"], 8)
            for k in range(DC):
                ins = mm(bank[0:RANK, 6, 0:TOK], lr_w[:, k, :], hT[:, k, :], start=(k == 0), stop=(k == DC - 1))
            ins.then_inc(S["lr_done"], 1)

            def by_feature(n, bk, src, halves=(0, 1)):
                s = ring[:, n % RING, :].rearrange("p (c n) -> p c n", c=DC)
                pe.wait_ge(landed[n % RING], 16 * (n // RING + 1))
                for a in halves:
                    for k in range(DC):
                        ins = mm(b2(bk)[:, a, :], s[:, k, a * P:(a + 1) * P], src[:, k, :],
                                 start=(k == 0), stop=(k == DC - 1))
                if halves[-1]:
                    ins.then_inc(used, 1)

            def by_token(n, bk, halves=(0, 1)):
                s = ring[:, n % RING, :].rearrange("p (c n) -> p c n", c=DC)
                pe.wait_ge(landed[n % RING], 16 * (n // RING + 1))
                for t in halves:
                    for k in range(DC):
                        ins = mm(b2(bk)[:, t, :], hT[:, k, t * P:(t + 1) * P], s[:, k, :],
                                 start=(k == 0), stop=(k == DC - 1))
                if halves[-1]:
                    ins.then_inc(used, 1)

            def bu(j):
                if j >= 2:
                    pe.wait_ge(S["rot1_done"], 2 * (j - 1))
                ps = slice(32 * (j % 4), 32 * (j % 4) + 32)
                for i in range(2):
                    ins = mm(b2(4 + j % 2)[:, i, :], bbT[ps, i, j // 4, :], uT[ps, j // 4, :],
                             start=True, stop=True)
                ins.then_inc(S["bu_done"], 1)

            def ys(j):
                pe.wait_ge(S["sst_done"], j + 1)
                if j % 4 == 0 and j >= 8:
                    pe.wait_ge(S["yy_done"], j // 4 - 1)
                r = j % 4
                for i in range(2):
                    ins = mm(b2(YS_BANK[j // 4])[32 * r:32 * r + 32, 1, :], ctT[:, i, j, :], sst[:, j % 2, i, :],
                             start=(i == 0), stop=(i == 1))
                ins.then_inc(S["ys_done"], 1)

            pe.wait_ge(S["ct_ready"], 2)
            by_feature(AB_U, 0, hT)
            by_feature(AB_U + 1, 1, hT)
            pe.wait_ge(S["lr_copied"], 1)
            for m in range(QC):
                ins = mm(b2(5)[:, m, :], gate_w[:, m * P:(m + 1) * P],
                         s5p[0:RANK, 0:2, :].rearrange("p a t -> p (a t)"), start=True, stop=True)
            ins.then_inc(S["gate_done"], 1)
            pe.wait_ge(S["bb_done"], 2)
            for i in range(2):
                for k in range(UC):
                    ins = pe.transpose(bank[:, 2 + i, k * P:(k + 1) * P],
                                       bb[:, i, 4 * k:4 * k + 4, :].rearrange("p j c -> p (j c)"), ident[:, :])
                ins.then_inc(S["bb_turned"], 1)
            pe.wait_ge(S["bbT_ready"], 2)
            pe.wait_ge(S["proj_out"], 2)
            pe.wait_ge(S["gate_x"], 2)
            halves_at = {j: (AB_Q + j // 2, j % 2) for j in range(8)}
            halves_at.update({10: (AB_R, 0), 11: (AB_R, 1), 14: (AB_R + 1, 0), 15: (AB_R + 1, 1)})
            mod_at = {8: MOD_A, 9: MOD_A + 1, 12: MOD_A + 2, 13: MOD_A + 3}
            for j in range(ST):
                bu(j)
                if j >= 2:
                    ys(j - 2)
                if j in halves_at:
                    n, half = halves_at[j]
                    if half == 0 and n >= AB_V:
                        pe.wait_ge(S["proj_out"], n - 3)
                    if AB_V <= n < AB_R:
                        by_token(n, n % 4, (half,))
                    else:
                        by_feature(n, n % 4, hT, (half,))
                else:
                    n = mod_at[j]
                    pe.wait_ge(S["proj_out"], 6)
                    if j >= 12:
                        pe.wait_ge(S["yy_done"], 2)
                        mod_turn(n - 2)
                    mod_rows(n)
            ys(ST - 2)
            ys(ST - 1)
            mod_turn(MOD_A + MOD_S5 - 2)
            mod_turn(MOD_A + MOD_S5 - 1)

            pe.wait_ge(S["rot1_done"], 2 * ST)
            pe.wait_ge(S["z_done"], UC)

            def glu():
                pe.wait_ge(landed[AB_GLU % RING], 16 * (AB_GLU // RING + 1))
                s = ring[:, AB_GLU % RING, :].rearrange("p (c n) -> p c n", c=UC)
                pe.wait_ge(S["z_done"], UC)
                for b in range(2):
                    for a in range(2):
                        m = 2 * b + a
                        for k in range(UC):
                            ins = mm(b2(4 + b)[:, a, :], s[:, k, m * P:(m + 1) * P], zT[:, k, :],
                                     start=(k == 0), stop=(k == UC - 1))
                    ins.then_inc(used if b else S["glu_done"], 1)

            pe.wait_ge(S["proj_out"], 8)
            for n in range(LEVELS + 1):
                diag = n == LEVELS
                if n in ROUND_AT or n == 6:
                    i = ROUND_AT.get(n, 2)
                    mod_rows(MOD_A + MOD_S5 + i)
                    if i:
                        mod_columns(i - 1)
                if diag:
                    ks, qs = kT, qT
                else:
                    pe.wait_ge(S["kq_done"], n + 1)
                    ks, qs = kd[:, n % 2, :, :], qd[:, n % 2, :, :]
                if n >= 2:
                    pe.wait_ge(S["att_out"], 2 * (n - 1))
                for par in range(2):
                    ps = slice(64 * par, 64 * par + 64)
                    o = bank[:, 2 * (n % 2) + par, :].rearrange("p (b t) -> p b t", t=P)
                    for pair in range(2):
                        if n == LEVELS - 1:
                            ins = mm(o[:, pair, :], ks[ps, pair, 0:P], qs[ps, pair, P:TOK], start=True, stop=True)
                        else:
                            for t in range(TT):
                                ins = mm(o[:, 2 * pair + t, :], ks[ps, pair, t * P:(t + 1) * P],
                                         qs[ps, pair, t * P:(t + 1) * P], start=True, stop=True)
                    ins.then_inc(S["att_done"], 1)
                if n == 1:
                    glu()
            pe.wait_ge(S["att_out"], 2 * (LEVELS + 1))
            for b in range(2):
                for a in range(2):
                    hd = 2 * b + a
                    o = b2(b)[:, a, :]
                    vh = lambda t: vS[:, t, hd * GDV:(hd + 1) * GDV]
                    mm(o[:, 0:P], vh(0), attD[:, hd % 2, hd // 2, 0, :], start=True, stop=True)
                    mm(o[:, P:TOK], vh(0), attX[:, hd % 2, hd // 2, :], start=True, stop=False)
                    ins = mm(o[:, P:TOK], vh(1), attD[:, hd % 2, hd // 2, 1, :], start=False, stop=True)
                ins.then_inc(S["av_done"], 1)
            pe.wait_ge(S["glu_sig"], 4)
            for b in range(2):
                pe.wait_ge(S["hsq_done"], b + 1)
                mm(bank[:, 4 + b, :], head_w[:, :], yy[:, 2 * b:2 * b + 2, :].rearrange("p a t -> p (a t)"),
                   start=True, stop=True).then_inc(S["hms_done"], 1)
            mod_rows(MOD_A + MOD_S5 + 3)
            pe.wait_ge(S["av_out"], 2)
            pe.wait_ge(S["ya_done"], 4)
            for b in range(4):
                mm(bank[:, b, :], zero16[:, 0:P], zero16[:, :], start=True, stop=True, skip_group_check=True)
            for chunks in (range(UC), range(UC, DC)):
                if chunks[0]:
                    pe.wait_ge(S["yb_done"], 4)
                for j in range(4):
                    n = AB_OUT + j
                    s = ring[:, n % RING, :].rearrange("p (c n) -> p c n", c=DC)
                    pe.wait_ge(landed[n % RING], 16 * (n // RING + 1))
                    for a in range(2):
                        for k in chunks:
                            ins = mm(b2(j)[:, a, :], s[:, k, a * P:(a + 1) * P], yT[:, k, :],
                                     start=False, stop=True, skip_group_check=True)
                    if chunks[0]:
                        ins.then_inc(used, 1)
                        if j in (0, 3):
                            mod_columns(2 + j // 3)

            def norm(i):
                for ch in range(DC):
                    pe.wait_ge(S["r_done"], 8 * i + ch + 1)
                    ins = mm(bank[:, 4, 0:TOK], mean_w[:, :], rT[:, ch, :], start=(ch == 0), stop=(ch == DC - 1))
                ins.then_inc(S["mean_done"], 1)
                for ch in range(DC):
                    if ch % 2 == 0:
                        pe.wait_ge(S["sq_done"], 4 * i + ch // 2 + 1)
                    ins = mm(bank[:, 5, 0:TOK], mean_w[:, :], sqT[:, ch, :], start=(ch == 0), stop=(ch == DC - 1))
                ins.then_inc(S["var_done"], 1)

            def moe(layer):
                for k in range(DC):
                    pe.wait_ge(S["h_ready"], 8 * (2 * layer + 1) + k + 1)
                    ins = mm(bank[0:NE, 6, 0:TOK], router_sb[:, k, :], hT[:, k, :], start=(k == 0), stop=(k == DC - 1))
                ins.then_inc(S["logit_done"], 1)
                pe.wait_ge(S["aff_done"], layer + 1)
                for t in range(TT):
                    ins = pe.transpose(bank[:, 6, t * NE:(t + 1) * NE], affT[:, t * P:(t + 1) * P],
                                       ident[0:NE, 0:NE])
                ins.then_inc(S["aff_turned"], 1)
                pe.wait_ge(S["r_done"], 8 * (2 * layer + 1))
                for b in range(4):
                    mm(bank[:, b, :], zero16[:, 0:P], zero16[:, :], start=True, stop=True, skip_group_check=True)
                first = MOE_AT[layer]
                pe.wait_ge(S["hlo_done"], 8 * layer + 4)

                def gates_turned():
                    pe.wait_ge(S["gates_done"], layer + 1)
                    for t in range(TT):
                        ins = pe.transpose(bank[0:NE, 6, t * P:(t + 1) * P],
                                           rt[:, 4, t * NE:(t + 1) * NE], ident[:, :])
                    ins.then_inc(S["gt_turned"], 1)

                def unit(it, e2, half, between=None):
                    u = 2 * e2 + half
                    n = 32 * layer + u
                    pe.wait_ge(S["prod_done"], it * 4 + (n + 1))
                    for g in range(2):
                        pe.wait_ge(S["wlo_done"], it * 8 + (4 * (NE * layer + e2) + 2 * half + g + 1))
                        hi, lo = (block_part(w, first, half, g)[0] for w in (whi, wlo))
                        o = b2(4 + half)[:, g, :]
                        for k in range(DC):
                            mm(o, hi[:, k, :], hhi[:, k, :], start=(k == 0), stop=False)
                            mm(o, hi[:, k, :], hlo[:, k, :], start=False, stop=False)
                            ins = mm(o, lo[:, k, :], hhi[:, k, :], start=False, stop=(k == DC - 1))
                        if between and g == 0:
                            between(it)
                    ins.then_inc(S["block_done"], 1)

                def down(it, e2):
                    for half in range(2):
                        pe.wait_ge(S["wlod_done"], it * 4 + (2 * (NE * layer + e2) + half + 1))
                        pe.wait_ge(S["he_done"], it * 4 + (32 * layer + 2 * e2 + half + 3))
                        hi, lo = (w[:, 2, half * D:(half + 1) * D] for w in (whi, wlo))
                        for m in range(DC):
                            o = b2(m // 2)[:, m % 2, :]
                            cols_m = slice(m * P, (m + 1) * P)
                            for w, e in ((hi, ehi), (hi, elo), (lo, ehi)):
                                ins = mm(o, w[:, cols_m], e[:, e2, half, :], start=False, stop=True,
                                         skip_group_check=True)
                    ins.then_inc(S["block_done"], 1)

                def gates_out(it):
                    if isinstance(it, int):
                        pe.wait_ge(S["gsel_done"], layer + 1)
                    pe.wait_ge(S["ef_done"], it * 4 + (32 * layer + 2))
                    mm(b2(6), ones[0:NE, :], gsel[:, bass.ds(it * 2, 2), :], start=True, stop=True
                       ).then_inc(S["gb_done"], 1)

                def two(it):
                    at_start = isinstance(it, int) and it == 0
                    for e2 in range(2):
                        unit(it, e2, 0)
                        if e2 == 0 and at_start:
                            gates_turned()
                            unit(it, e2, 1, gates_out)
                        else:
                            if e2 == 0:
                                gates_out(it)
                            unit(it, e2, 1)
                        if layer == 0:
                            if e2:
                                mod_sum_moe(it, 0)
                            elif not (isinstance(it, int) and it == 0):
                                mod_sum_moe(it - 1, 1)
                                mod_sum_moe(it - 1, 2)
                        down(it, e2)

                two(0)
                pe.wait_ge(S["gsel_rest"], layer + 1)
                with pe.Fori(1, NE // 2) as it:
                    two(it)
                if layer == 0:
                    mod_sum_moe(NE // 2 - 1, 1)
                    mod_sum_moe(NE // 2 - 1, 2)

            norm(0)
            moe(0)
            norm(1)

            def mix_feature(i, xhi, xlo):
                whole = [w[:, i % 2, :].rearrange("p (c n) -> p c n", c=DC) for w in (whi, wlo)]
                for a in range(2):
                    pe.wait_ge(S["mix_lo_pool" if a else "mix_lo_dve"], i + 1)
                    hi, lo = (w[:, :, a * P:(a + 1) * P] for w in whole)
                    o = b2(i % 4)[:, a, :]
                    for k in range(DC):
                        if i == 16 and a == 0 and k % 2 == 0:
                            pe.wait_ge(S["ylo_done"], k // 2 + 1)
                        mm(o, hi[:, k, :], xhi[:, k, :], start=(k == 0), stop=False)
                        mm(o, hi[:, k, :], xlo[:, k, :], start=False, stop=False)
                        ins = mm(o, lo[:, k, :], xhi[:, k, :], start=False, stop=(k == DC - 1))
                ins.then_inc(used, 1)

            def mix_token(i):
                hi, lo = (w[:, i % 2, :].rearrange("p (c n) -> p c n", c=DC) for w in (whi, wlo))
                pe.wait_ge(S["mix_lo_dve"], i + 1)
                pe.wait_ge(S["mix_lo_pool"], i + 1)
                for t in range(TT):
                    o = b2(i % 4)[:, t, :]
                    ts_ = slice(t * P, (t + 1) * P)
                    for k in range(DC):
                        mm(o, hhi[:, k, ts_], hi[:, k, :], start=(k == 0), stop=False)
                        mm(o, hhi[:, k, ts_], lo[:, k, :], start=False, stop=False)
                        ins = mm(o, hlo[:, k, ts_], hi[:, k, :], start=False, stop=(k == DC - 1))
                ins.then_inc(used, 1)

            pe.wait_ge(S["h_ready"], 24)
            for g in range(2):
                for k in range(DC):
                    ins = mm(bank[0:MH, 6, g * TOK:(g + 1) * TOK], mg_w[:, k, g * MH:(g + 1) * MH], hT[:, k, :],
                             start=(k == 0), stop=(k == DC - 1))
            ins.then_inc(S["mgate_done"], 1)
            pe.wait_ge(S["r_done"], 16)
            for j in range(16):
                if j == 2:
                    pe.wait_ge(S["mrow_done"], 1)
                    for t in range(TT):
                        ins = pe.transpose(bank[:, 6, t * MH:(t + 1) * MH], mrow[0:MH, 7, t * P:(t + 1) * P],
                                           ident[0:MH, 0:MH])
                    ins.then_inc(S["mcol_turned"], 1)
                if 4 <= j < 12:
                    pe.wait_ge(S["conv_done"], 2 * (j - 4) + 2)
                elif j >= 12:
                    pe.wait_ge(S["proj_out"], 8 + j - 12 + 1)
                if j == 0:
                    pe.wait_ge(S["hlo_done"], 8)
                if 8 <= j < 12:
                    mix_token(j)
                else:
                    mix_feature(j, hhi, hlo)
            pe.wait_ge(S["proj_out"], 16)
            pe.wait_ge(S["qk_done"], 16)
            pe.wait_ge(S["mcol_done"], 1)
            pe.wait_ge(S["norm_done"], 8)

            def scores(hd):
                q = hd % 2
                if hd >= 2:
                    pe.wait_ge(S["md_done"], 2 * (hd - 1))
                pick = bc(ident[0:MH, hd:hd + 1], MH, P)
                o = bank[:, q, :]
                mm(o[:, 0:TOK], pick, mrow[0:MH, 8, :], start=True, stop=True, skip_group_check=True)
                mm(o[:, 0:P], ident16[:, :], future16[:, :], start=False, stop=True, skip_group_check=True)
                mm(o[:, TOK:384], pick, mrow[0:MH, 8, P:TOK], start=False, stop=True, skip_group_check=True)
                mm(o[:, TOK:384], ident16[:, :], future16[:, :], start=False, stop=True, skip_group_check=True
                   ).then_inc(S["mb_done"], 1)
                if hd >= 2:
                    pe.wait_ge(S["ms_done"], hd - 1)
                o = bank[:, 2 + q, :]
                mm(o[:, 0:TOK], kT1[:, hd, 0:P], qT1[:, hd, :], start=True, stop=True)
                mm(o[:, TOK:384], kT1[:, hd, P:TOK], qT1[:, hd, P:TOK], start=True, stop=True
                   ).then_inc(S["mqk_done"], 1)

            def values(hd):
                q = hd % 2
                if hd >= 2:
                    pe.wait_ge(S["mh_done"], hd - 1)
                pe.wait_ge(S["ms_done"], hd + 1)
                o, d = bank[:, 4 + q, :], bank[0:MH, 6, :]
                for t in range(TT):
                    s = sM[:, q, 0:TOK] if t == 0 else sM[:, q, TOK:384]
                    mm(o[:, t * P:TOK], vM[:, t, hd * P:(hd + 1) * P], s, start=(t == 0), stop=(t == 1),
                       skip_group_check=True)
                    ins = mm(d[:, t * P:TOK], to_row[:, hd, :], s, start=(hd == 0 and t == 0), stop=True,
                             skip_group_check=True)
                ins.then_inc(S["mnum_done"], 1)

            def mean_square(hd):
                pe.wait_ge(S["mnumsq_done"], hd + 1)
                mm(bank[0:MH, 7, 0:TOK], to_row[:, hd, :], numsq[:, hd % 2, :], start=(hd == 0), stop=True,
                   skip_group_check=True).then_inc(S["mmean_done"], 1)

            for i in range(MH + 3):
                if i < MH:
                    scores(i)
                if 2 <= i < MH + 2:
                    values(i - 2)
                if i >= 3:
                    mean_square(i - 3)
            pe.wait_ge(S["mscale_done"], 1)
            for b in range(4):
                for a in range(2):
                    hd = 2 * b + a
                    ins = mm(b2(b)[:, a, :], bc(ident[0:MH, hd:hd + 1], MH, P), mrow[0:MH, 3, :],
                             start=True, stop=True)
                ins.then_inc(S["mscaleb_done"], 1)
            for j in range(4):
                mix_feature(16 + j, yhi, ylo)
            norm(2)
            moe(1)
            norm(3)
            pe.wait_ge(S["h_ready"], 40)
            for b in range(4):
                t = b // 2
                for k in range(4):
                    ch = 4 * (b % 2) + k
                    ins = pe.transpose(bank[:, b, k * P:(k + 1) * P], hT[:, ch, t * P:(t + 1) * P], ident[:, :])
                ins.then_inc(S["final_turned"], 1)


EPS_H = 1e-6
EPS_LN = 1e-5

_INS = ["x", "c", "router_w", "router_bias", "ada_w", "ada_b", "ln1_g", "ln1_b", "ln2_g", "ln2_b",
        "moe_w_gate", "moe_w_up", "moe_w_down", "ab_w_in", "s5_lam_re", "s5_lam_im", "s5_log_dt",
        "s5_b_re", "s5_b_im", "s5_c_re", "s5_c_im", "s5_d", "s5_glu_w", "s5_glu_b",
        "gla_gate_w", "gla_gate_b", "gla_norm_g", "ab_w_out", "ml_w_in", "ml_conv_w", "ml_conv_b",
        "ml_igate_b", "ml_fgate_b", "ml_norm_g", "ml_w_out"]


def kernel(**inputs):
    import concourse.bacc as _bacc
    from concourse.bass_utils import run_bass_kernel_spmd as _run

    nc = _bacc.Bacc("TRN2", target_bir_lowering=False, num_devices=1)
    arrays, args = {}, []
    for name in _INS:
        a = np.ascontiguousarray(inputs[name])
        arrays[f"in_{name}_dram"] = a
        args.append(nc.dram_tensor(f"in_{name}_dram", a.shape, mybir.dt.from_np(a.dtype),
                                   kind="ExternalInput").ap())
    args.append(nc.dram_tensor("out_dram", (1, TOK, D), F32, kind="ExternalOutput").ap())
    trunk(nc, *args)
    r = _run(nc, [arrays], core_ids=[0])
    return r.results[0]["out_dram"]
```
